# Optimizing a Trainium2 kernel written in Bass

```python
import jax, jax.numpy as jnp
from jax import lax
import numpy as np

D_MODEL = 1024
BATCH = 1
SEQ = 1024
DEPTH = 1
DEC_BATCH = 1
DEC_SEQ = 1024
PAST_LEN = 128

MIX_WIDTH = D_MODEL
ATTN_WIDTH = MIX_WIDTH // 2
POOL_WIDTH = MIX_WIDTH - ATTN_WIDTH
HEAD_DIM = 64
N_HEADS = ATTN_WIDTH // HEAD_DIM
N_KV_HEADS = 2
GQA_GROUP = N_HEADS // N_KV_HEADS
KV_WIDTH = N_KV_HEADS * HEAD_DIM
ROT_PAIRS = HEAD_DIM // 4
ROPE_THETA = 10000.0
GRID_W = 64
Q_BLOCK = 128
POOL_WINDOWS = (2, 4, 8, 16)
N_POOL_GROUPS = len(POOL_WINDOWS)
POOL_GROUP_W = POOL_WIDTH // N_POOL_GROUPS
IN_WIDTH = ATTN_WIDTH + 2 * KV_WIDTH + POOL_WIDTH
N_EXPERTS = 16
CAPACITY_FACTOR = 2
D_FF = 2048
LN_EPS = 1e-5
RMS_EPS = 1e-6
ALPHA = (2.0 * DEPTH) ** 0.25
BETA = (8.0 * DEPTH) ** -0.25

kernel_name = "hybrid_attn_pool_ec_moe_encoder"

def layer_norm(x, g, b):
    xf = x.astype(jnp.float32)
    mu = jnp.mean(xf, axis=-1, keepdims=True)
    var = jnp.mean(jnp.square(xf - mu), axis=-1, keepdims=True)
    return ((xf - mu) * lax.rsqrt(var + LN_EPS) * g.astype(jnp.float32) + b.astype(jnp.float32)).astype(x.dtype)

def rms_norm(x, g):
    xf = x.astype(jnp.float32)
    return (xf * lax.rsqrt(jnp.mean(xf * xf, axis=-1, keepdims=True) + RMS_EPS) * g.astype(jnp.float32)).astype(x.dtype)

def rope_half(u, cos, sin):
    u1, u2 = jnp.split(u, 2, axis=-1)
    return jnp.concatenate([u1 * cos - u2 * sin, u2 * cos + u1 * sin], axis=-1)

def axial_tables(seq_len, dtype):
    rows = seq_len // GRID_W
    row = jnp.repeat(jnp.arange(rows), GRID_W).astype(jnp.float32)
    col = jnp.tile(jnp.arange(GRID_W), rows).astype(jnp.float32)
    inv_freq = ROPE_THETA ** (-jnp.arange(ROT_PAIRS, dtype=jnp.float32) / ROT_PAIRS)
    ang_r = row[:, None] * inv_freq[None, :]
    ang_c = col[:, None] * inv_freq[None, :]
    tabs = [jnp.cos(ang_r), jnp.sin(ang_r), jnp.cos(ang_c), jnp.sin(ang_c)]
    return [t[:, None, :].astype(dtype) for t in tabs]

def axial_rope(x, tabs):
    cos_r, sin_r, cos_c, sin_c = tabs
    xr, xc = jnp.split(x, 2, axis=-1)
    return jnp.concatenate([rope_half(xr, cos_r, sin_r), rope_half(xc, cos_c, sin_c)], axis=-1)

def block_attention(q, k, v):
    B, S = q.shape[0], q.shape[1]
    nblk = S // Q_BLOCK
    scale = HEAD_DIM ** -0.5
    qb = q.reshape(B, nblk, Q_BLOCK, N_KV_HEADS, GQA_GROUP, HEAD_DIM).transpose(1, 0, 2, 3, 4, 5)

    def one_block(qblk):
        s = jnp.einsum('bqhgd,bkhd->bhgqk', qblk, k).astype(jnp.float32) * scale
        p = jax.nn.softmax(s, axis=-1)
        return jnp.einsum('bhgqk,bkhd->bqhgd', p.astype(v.dtype), v)

    ob = lax.map(one_block, qb)
    return ob.transpose(1, 0, 2, 3, 4, 5).reshape(B, S, N_HEADS * HEAD_DIM)

def pool_mixer(u, w_pool, pool_scale):
    B, S, _ = u.shape
    ug = u.reshape(B, S, N_POOL_GROUPS, POOL_GROUP_W)
    cs = jnp.cumsum(ug.astype(jnp.float32), axis=1)
    cs = jnp.concatenate([jnp.zeros((B, 1, N_POOL_GROUPS, POOL_GROUP_W), jnp.float32), cs], axis=1)
    t = jnp.arange(S)
    outs = []
    for g, w in enumerate(POOL_WINDOWS):
        lo = jnp.clip(t - w // 2, 0, S)
        hi = jnp.clip(t - w // 2 + w, 0, S)
        csg = cs[:, :, g, :]
        win_sum = jnp.take(csg, hi, axis=1) - jnp.take(csg, lo, axis=1)
        cnt = (hi - lo).astype(jnp.float32)[None, :, None]
        outs.append(win_sum / cnt - ug[:, :, g, :].astype(jnp.float32))
    m = jnp.stack(outs, axis=2).astype(u.dtype)
    y = jnp.einsum('bsgc,gcd->bsgd', m, w_pool).reshape(B, S, POOL_WIDTH)
    return y * pool_scale

def token_mixer(x, w_in, q_norm_g, k_norm_g, w_pool, pool_scale, w_out):
    B, S, _ = x.shape
    proj = x @ w_in
    q = proj[..., :ATTN_WIDTH].reshape(B, S, N_HEADS, HEAD_DIM)
    k = proj[..., ATTN_WIDTH:ATTN_WIDTH + KV_WIDTH].reshape(B, S, N_KV_HEADS, HEAD_DIM)
    v = proj[..., ATTN_WIDTH + KV_WIDTH:ATTN_WIDTH + 2 * KV_WIDTH].reshape(B, S, N_KV_HEADS, HEAD_DIM)
    u = proj[..., ATTN_WIDTH + 2 * KV_WIDTH:]
    tabs = axial_tables(S, x.dtype)
    q = axial_rope(rms_norm(q, q_norm_g), tabs)
    k = axial_rope(rms_norm(k, k_norm_g), tabs)
    attn = block_attention(q, k, v)
    pool = pool_mixer(u, w_pool, pool_scale)
    return jnp.concatenate([attn, pool], axis=-1) @ w_out

def expert_choice_ffn(x, w_router, w_gate, w_up, w_down):
    B, S, D = x.shape
    n_tok = B * S
    cap = (CAPACITY_FACTOR * n_tok) // N_EXPERTS
    tok = x.reshape(n_tok, D)
    aff = jax.nn.softmax((tok @ w_router).astype(jnp.float32), axis=-1)
    gate, idx = lax.top_k(aff.T, cap)
    xe = jnp.take(tok, idx, axis=0)
    h = jax.nn.silu(jnp.einsum('ecd,edf->ecf', xe, w_gate)) * jnp.einsum('ecd,edf->ecf', xe, w_up)
    ye = jnp.einsum('ecf,efd->ecd', h, w_down) * gate[..., None].astype(x.dtype)
    out = jnp.zeros_like(tok).at[idx.reshape(-1)].add(ye.reshape(-1, D))
    return out.reshape(B, S, D)

def trunk(x, ln_in_g, ln_in_b, w_in, q_norm_g, k_norm_g, w_pool, pool_scale, w_out,
          ln1_g, ln1_b, w_router, w_gate, w_up, w_down, ln2_g, ln2_b):
    x = layer_norm(x, ln_in_g, ln_in_b)
    for l in range(DEPTH):
        mix = token_mixer(x, w_in[l], q_norm_g[l], k_norm_g[l], w_pool[l], pool_scale[l], w_out[l])
        x = layer_norm(ALPHA * x + mix, ln1_g[l], ln1_b[l])
        ff = expert_choice_ffn(x, w_router[l], w_gate[l], w_up[l], w_down[l])
        x = layer_norm(ALPHA * x + ff, ln2_g[l], ln2_b[l])
    return x

def setup_inputs(seed: int = 0) -> dict:
    key = jax.random.key(seed)
    ks = jax.random.split(key, 20)
    f32 = jnp.float32
    nrm = lambda k, shape, s: jax.random.normal(k, shape, f32) * s
    return {
        "x_prompt": jax.random.normal(ks[0], (BATCH, SEQ, D_MODEL), f32),
        "x_sample": jax.random.normal(ks[1], (DEC_BATCH, DEC_SEQ, D_MODEL), f32),
        "ln_in_g": 1.0 + nrm(ks[2], (D_MODEL,), 0.02),
        "ln_in_b": nrm(ks[3], (D_MODEL,), 0.02),
        "w_in": nrm(ks[4], (DEPTH, D_MODEL, IN_WIDTH), D_MODEL ** -0.5),
        "q_norm_g": 1.0 + nrm(ks[5], (DEPTH, HEAD_DIM), 0.02),
        "k_norm_g": 1.0 + nrm(ks[6], (DEPTH, HEAD_DIM), 0.02),
        "w_pool": nrm(ks[7], (DEPTH, N_POOL_GROUPS, POOL_GROUP_W, POOL_GROUP_W), POOL_GROUP_W ** -0.5),
        "pool_scale": 1.0 + nrm(ks[8], (DEPTH, POOL_WIDTH), 0.02),
        "w_out": nrm(ks[9], (DEPTH, MIX_WIDTH, D_MODEL), BETA * MIX_WIDTH ** -0.5),
        "ln1_g": 1.0 + nrm(ks[10], (DEPTH, D_MODEL), 0.02),
        "ln1_b": nrm(ks[11], (DEPTH, D_MODEL), 0.02),
        "w_router": nrm(ks[12], (DEPTH, D_MODEL, N_EXPERTS), D_MODEL ** -0.5),
        "w_gate": nrm(ks[13], (DEPTH, N_EXPERTS, D_MODEL, D_FF), D_MODEL ** -0.5),
        "w_up": nrm(ks[14], (DEPTH, N_EXPERTS, D_MODEL, D_FF), D_MODEL ** -0.5),
        "w_down": nrm(ks[15], (DEPTH, N_EXPERTS, D_FF, D_MODEL), BETA * D_FF ** -0.5),
        "ln2_g": 1.0 + nrm(ks[16], (DEPTH, D_MODEL), 0.02),
        "ln2_b": nrm(ks[17], (DEPTH, D_MODEL), 0.02),
    }

def reference(x_prompt, x_sample, ln_in_g, ln_in_b, w_in, q_norm_g, k_norm_g, w_pool, pool_scale,
              w_out, ln1_g, ln1_b, w_router, w_gate, w_up, w_down, ln2_g, ln2_b):
    y_prompt = trunk(x_prompt, ln_in_g, ln_in_b, w_in, q_norm_g, k_norm_g, w_pool, pool_scale, w_out,
                     ln1_g, ln1_b, w_router, w_gate, w_up, w_down, ln2_g, ln2_b)
    y_sample = trunk(x_sample, ln_in_g, ln_in_b, w_in, q_norm_g, k_norm_g, w_pool, pool_scale, w_out,
                     ln1_g, ln1_b, w_router, w_gate, w_up, w_down, ln2_g, ln2_b)
    return (y_prompt, y_sample)


_drawn_inputs = setup_inputs


def setup_inputs(seed=0):
    import zlib

    import numpy as np

    out = dict(_drawn_inputs(seed))
    spreads = {}
    factors = {'ln_in_b': 2.867,
     'q_norm_g': 8.0,
     'k_norm_g': 8.0,
     'pool_scale': 7.677,
     'ln1_g': 2.688,
     'ln1_b': 2.755,
     'ln2_g': 2.855,
     'ln2_b': 2.874}
    for name, (base, spread) in spreads.items():
        noise = np.random.default_rng([zlib.crc32(name.encode()), seed]).standard_normal(out[name].shape)
        drawn = base * np.exp(spread * noise) if base else spread * noise
        out[name] = __import__('jax').numpy.asarray(drawn.astype(out[name].dtype))
    for name, factor in factors.items():
        out[name] = (out[name] * factor).astype(out[name].dtype)
    return out
```

```python
import numpy as np
from contextlib import ExitStack
import concourse.bass as bass
from concourse import mybir


def encoder_layer(nc, x, ln_in_g, ln_in_b, w_in, qk_gain, w_pool, pool_scale, w_out, ln1_g, ln1_b, w_router,
                  w_gate, w_up, w_down, ln2_g, ln2_b, rope_cos, rope_sin, pool_edge, eye, out):
    f32, f32r, u32 = mybir.dt.float32, mybir.dt.float32r, mybir.dt.uint32
    ALU, ACT, AX = mybir.AluOpType, mybir.ActivationFunctionType, mybir.AxisListType

    P = 128
    TOK, D = x.shape
    GROUPS = 2
    SEQ = TOK // GROUPS
    KD = D // P
    HD = 64
    HEADS, KVH = 8, 2
    AW, KVW = HEADS * HD, KVH * HD
    QKW = AW + KVW
    QKVW = AW + 2 * KVW
    PW = w_in.shape[1] - QKVW
    WINDOWS = (2, 4, 8, 16)
    PAD = max(WINDOWS) // 2
    NW = len(WINDOWS)
    E, _, F = w_gate.shape
    KF = F // P
    CAP = 2 * SEQ // E
    LN_EPS, RMS_EPS, ALPHA = 1e-5, 1e-6, 2.0 ** 0.25
    TILES = TOK // P
    GT = SEQ // P

    def dram(name, shape, dt=f32):
        return nc.dram_tensor(name, shape, dt, kind="Internal").ap()

    xln_d = dram("xln_d", (TOK, D))
    KVC = AW // KVH + 2 * HD
    q_d = dram("q_d", (KVH * TOK, AW // KVH))
    kv_d = dram("kv_d", (KVH * TOK, 2 * HD))
    ut_d = dram("ut_d", (NW, P, TOK))
    h_d = dram("h_d", (TOK, D))
    acc_d = dram("acc_d", (TOK, D))

    ctx = ExitStack()
    with ctx:
        def sem(name):
            return ctx.enter_context(nc.semaphore(name))

        def alloc(stack):
            return lambda name, shape, dt=f32: stack.enter_context(nc.sbuf_tensor(name, shape, dt))

        def palloc(stack):
            return lambda name, shape, dt=f32: stack.enter_context(nc.psum_tensor(name, shape, dt))

        def some_steps(eng, n, body):
            body(0, True)
            with eng.Fori(1, n) as i:
                body(i, False)

        def at(eng, value):
            return value if isinstance(value, int) else eng.snap(value)

        def steps(eng, n, body):
            body(0, True, False)
            with eng.Fori(1, n - 1) as i:
                body(i, False, False)
            body(n - 1, False, True)

        sb = alloc(ctx)
        ident = sb("ident", [P, P])
        gain_b = sb("gain_b", [P, 2, D])
        eps = sb("eps", [P, 2])
        alpha = sb("alpha", [P, 1])
        logits = sb("logits", [P, TILES, E])
        mv = sb("mv", [P, 2, 2])
        bst = sb("bst", [P, 2, 2, 6])
        sd = sb("sd", [P, 2, 1])
        rs = sb("rs", [P, 2, 1])

        sa = ExitStack()
        sb, pb = alloc(sa), palloc(sa)
        PAIRS = TILES // 2
        win_h = sb("win_h", [P, KD, w_in.shape[1]], f32r)
        win_l = sb("win_l", [P, KD, w_in.shape[1]], f32r)
        RAW = 4
        win_raw = sb("win_raw", [P, RAW, w_in.shape[1]])
        xin = sb("xin", [P, 2, D])
        xln = sb("xln", [P, 2, D])
        xt_h = sb("xt_h", [P, 2, KD, 2 * P], f32r)
        xt_l = sb("xt_l", [P, 2, KD, 2 * P], f32r)
        cos_t = sb("cos_t", [P, TILES, HD])
        sin_t = sb("sin_t", [P, TILES, HD])
        qkg = sb("qkg", [P, QKW])
        sq = sb("sq", [P, QKW])
        qn = sb("qn", [P, 2, QKW])
        rot = sb("rot", [P, QKW])
        qkv = sb("qkv", [P, 2, KVH, KVC])
        ust = sb("ust", [P, 2, NW, 2 * P])
        ss = sb("ss", [P, 2, 16])
        rn = sb("rn", [P, 2, 16])
        ps_xt = [pb(f"ps_xt{i}", [P, KD, P]) for i in range(2)]
        ps_q = pb("ps_q", [P, AW])
        ps_kv = pb("ps_kv", [P, 512])
        ps_u = [pb(f"ps_u{i}", [P, 2, 2 * P]) for i in range(2)]
        sa.close()

        keep = ExitStack()
        sb = alloc(keep)
        SLOTS = KVH * GROUPS
        QH = HEADS // KVH
        QC = QH * HD
        PAIR_H = QH // 2
        mix_at = sb("mix_at", [P, KVH, PAIR_H, TOK])
        mix_pl = sb("mix_pl", [P, NW, TOK])
        sB = ExitStack()
        sb, pb = alloc(sB), palloc(sB)
        QB = 2 * P
        NQB = QH * SEQ // QB
        q_raw = sb("q_raw", [P, GT, QC])
        kv_raw = sb("kv_raw", [P, GT, 2 * HD])
        kd_h = sb("kd_h", [P, GT, P], f32r)
        kd_l = sb("kd_l", [P, GT, P], f32r)
        kt_h = sb("kt_h", [P, SEQ], f32r)
        kt_l = sb("kt_l", [P, SEQ], f32r)
        v_hl = sb("v_hl", [P, GT, P], f32r)
        q_hl = sb("q_hl", [P, 2, GT, P], f32r)
        qt_hl = sb("qt_hl", [P, 2, SEQ], f32r)
        prob = sb("prob", [P, 2, SEQ])
        pt_h = sb("pt_h", [P, 2, GT, QB], f32r)
        pt_l = sb("pt_l", [P, 2, GT, QB], f32r)
        o_hl = sb("o_hl", [P, 2, QB])
        at_tok = sb("at_tok", [P, GT, 2 * HD])
        smax = sb("smax", [P, 2])
        nmax = sb("nmax", [P, 2])
        rsum = sb("rsum", [P, 2 * GT])
        rinv = sb("rinv", [P, 2 * GT])
        ident_r = sb("ident_r", [P, P], f32r)
        ident2 = sb("ident2", [P, HD])
        upad = sb("upad", [P, SEQ + 2 * PAD])
        win_a = sb("win_a", [P, SEQ + 2 * PAD])
        win_b = sb("win_b", [P, SEQ + 2 * PAD])
        edge_t = sb("edge_t", [P, NW, 2, PAD])
        wp_sb = sb("wp_sb", [P, NW, P])
        psc = sb("psc", [P, NW])
        ps_s = [pb(f"ps_s{i}", [P, SEQ]) for i in range(2)]
        ps_t = [pb(f"ps_t{i}", [P, 4, P]) for i in range(2)]
        ps_pv = pb("ps_pv", [P, 512])
        ps_m = pb("ps_m", [P, 4, P])
        sB.close()

        sc = ExitStack()
        sb, pb = alloc(sc), palloc(sc)
        KM = w_out.shape[0] // P
        wo_h = sb("wo_h", [P, KM, D], f32r)
        wo_l = sb("wo_l", [P, KM, D], f32r)
        wo_raw = sb("wo_raw", [P, 2, D])
        wr_sb = sb("wr_sb", [P, KD, E])
        mx_h = sb("mx_h", [P, 2, KM, P], f32r)
        mx_l = sb("mx_l", [P, 2, KM, P], f32r)
        res = sb("res", [P, 2, D])
        hid = sb("hid", [P, 2, D])
        acc = sb("acc", [P, 2, D])
        ht = sb("ht", [P, KD, P])
        ps_o = [pb(f"ps_o{i}", [P, D]) for i in range(2)]
        ps_ht = pb("ps_ht", [P, KD, P])
        ps_l = pb("ps_l", [P, 512])
        sc.close()
        keep.close()
        c_const = sem("c_const")
        wo_in = [sem(f"wo_in{i}") for i in range(2)]
        wo_hi, wo_lo = sem("wo_hi"), sem("wo_lo")
        res_in = [sem(f"res_in{i}") for i in range(2)]
        mx_hi, mx_lo, o_done = sem("mx_hi"), sem("mx_lo"), sem("o_done")
        r_ready, c_var, c_sd, h_ready = sem("r_ready"), sem("c_var"), sem("c_sd"), sem("h_ready")
        h_st = [sem(f"h_st{i}") for i in range(2)]
        acc_st = [sem(f"acc_st{i}") for i in range(2)]
        acc_ready, ht_done, ht_ready, l_done, l_ready = (sem("acc_ready"), sem("ht_done"), sem("ht_ready"),
                                                         sem("l_done"), sem("l_ready"))

        se = ExitStack()
        sb, pb = alloc(se), palloc(se)
        RING = 4
        CHUNK = KD * 2 * P
        w_raw = sb("w_raw", [P, RING, CHUNK])
        w_h = sb("w_h", [P, RING, CHUNK], f32r)
        w_l = sb("w_l", [P, RING, CHUNK], f32r)
        C2 = GROUPS * CAP
        hh = sb("hh", [P, KF, C2], f32r)
        hl = sb("hl", [P, KF, C2], f32r)
        x_h = sb("x_h", [P, KD, C2], f32r)
        x_l = sb("x_l", [P, KD, C2], f32r)
        xg = sb("xg", [P, GROUPS, D])
        ysb = sb("ysb", [P, GROUPS, D])
        sg = sb("sg", [P, 2, C2])
        hf = sb("hf", [P, 2, C2])
        lmax = sb("lmax", [P, TILES])
        lsum = sb("lsum", [P, TILES])
        GOFF = 32
        ROWS = GOFF + E
        aff = sb("aff", [ROWS, SEQ])
        top_v = sb("top_v", [ROWS, CAP])
        top_i = sb("top_i", [ROWS, CAP], u32)
        top_f = sb("top_f", [ROWS, CAP])
        gate_w8 = sb("gate_w8", [P, ROWS])
        idx_t = sb("idx_t", [P, ROWS], u32)
        idx_g = sb("idx_g", [P, GROUPS], u32)
        no_shift = sb("no_shift", [P, GROUPS], u32)
        idx_e = sb("idx_e", [P, GROUPS], u32)
        idx_s = sb("idx_s", [P, GROUPS], u32)
        ps_gu = [pb(f"ps_gu{i}", [P, 2, C2]) for i in range(3)]
        ps_y = [pb(f"ps_y{i}", [P, D]) for i in range(GROUPS)]
        ps_x = pb("ps_x", [P, 4, P])
        se.close()
        w_dma = [sem(f"w_dma{i}") for i in range(RING)]
        w_hi, w_lo = sem("w_hi"), sem("w_lo")
        d_step, d_exp, d_aff, d_vt = sem("d_step"), sem("d_exp"), sem("d_aff"), sem("d_vt")
        top_ready = sem("top_ready")
        x_in_g = [sem(f"x_in_g{g}") for g in range(GROUPS)]
        idx_ready = sem("idx_ready")
        xt_d, x_hi, x_lo = sem("xt_d"), sem("x_hi"), sem("x_lo")
        gu_done, silu_done, h_split = sem("gu_done"), sem("silu_done"), sem("h_split")
        dn_done, y_ready = sem("dn_done"), sem("y_ready")
        scat = [sem(f"scat{g}") for g in range(GROUPS)]

        sf = ExitStack()
        sb = alloc(sf)
        FR = 4
        y_raw = sb("y_raw", [P, FR, D])
        y_out = sb("y_out", [P, FR, D])
        fst = sb("fst", [P, FR, 2, 6])
        fmv = sb("fmv", [P, FR, 2])
        fsd = sb("fsd", [P, FR, 1])
        frs = sb("frs", [P, FR, 1])
        sf.close()
        f_const = sem("f_const")
        y_in = [sem(f"y_in{i}") for i in range(FR)]
        f_var, f_sd, f_ready = sem("f_var"), sem("f_sd"), sem("f_ready")
        y_st = [sem(f"y_st{i}") for i in range(FR)]

        NCHUNK = 2 * KF // 2 + KF // 2
        NUP = KF

        def used(e, c):
            if c < NUP:
                return gu_done, KF * e + 2 * (c // 2) + 2
            return dn_done, (KF // 2) * e + (c - NUP) + 1

        stage_over = sem("stage_over")
        ident_ready = sem("ident_ready")
        b_const, q_in, kv_in = sem("b_const"), sem("q_in"), sem("kv_in")
        k_hi, kv_split = sem("k_hi"), sem("kv_split")
        q_split = sem("q_split")
        s_done, max_ready, exp_ready, t_done = sem("s_done"), sem("max_ready"), sem("exp_ready"), sem("t_done")
        pt_hi, pt_lo, pv_done, o_ready = sem("pt_hi"), sem("pt_lo"), sem("pv_done"), sem("o_ready")
        m_full, m_free = sem("m_full"), sem("m_free")
        u_in, m_ready, pm_done, pl_ready = sem("u_in"), sem("m_ready"), sem("pm_done"), sem("pl_ready")
        pool_self = sem("pool_self")

        def stage_end(eng, n):
            eng.drain().then_inc(stage_over, 1)
            eng.wait_ge(stage_over, 5 * n)

        turns = [("K", 0, r) for r in range(GT // 4)] + [("K", 1, r) for r in range(GT // 4)]
        turns += [("Q", 0, r) for r in range(GT // 4)]
        NSTEP = QH * GT
        q_turn_at = {3: 0, 5: 1}

        def after_step(t):
            pv = t // 2 - 1 if t % 2 == 0 and 2 <= t <= NSTEP else None
            add = (t - 3) // 2 if t % 2 == 1 and 3 <= t <= NSTEP + 1 else None
            back = (t - 4) // 2 if t % 2 == 0 and 4 <= t <= NSTEP + 2 else None
            if back is not None and (back // (NQB // QH)) % 2 == 0:
                back = None
            return pv, add, back

        for t in range(NSTEP + 3):
            pv, add, back = after_step(t)
            if t < NSTEP and t % GT in q_turn_at and t // GT + 1 < QH:
                turns.append(("Q", t // GT + 1, q_turn_at[t % GT]))
            if add is not None:
                turns.append(("add", add))
            if back is not None:
                turns.append(("back", back))
        turn = {what: n for n, what in enumerate(turns)}
        TURNS = len(turns)

        const_in = sem("const_in")
        x_in = [sem(f"x_in{i}") for i in range(2)]
        win_in = [sem(f"win_in{i}") for i in range(RAW)]
        win_hi, win_lo = sem("win_hi"), sem("win_lo")
        var_ready, sd_ready, xln_ready = sem("var_ready"), sem("sd_ready"), sem("xln_ready")
        xln_st = [sem(f"xln_st{i}") for i in range(2)]
        xt_done, xt_hi, xt_lo = sem("xt_done"), sem("xt_hi"), sem("xt_lo")
        q_done, kv_done, u_done = sem("q_done"), sem("kv_done"), sem("u_done")
        ss_ready, rms_sd = sem("ss_ready"), sem("rms_sd")
        qn_ready, v_ready, roped = sem("qn_ready"), sem("v_ready"), sem("roped")
        u_ready = sem("u_ready")
        q_st = [sem(f"q_st{i}") for i in range(2)]
        kv_st = [sem(f"kv_st{i}") for i in range(2)]
        u_st = [sem(f"u_st{i}") for i in range(2)]
        eps_set = sem("eps_set")
        stage_a_read = sem("stage_a_read")

        block = ctx.enter_context(nc.Block())

        @block.sync
        def _(sp):
            sp.dma_start(xin[:, 0, :], x[0:P, :]).then_inc(x_in[0], 16)
            sp.dma_start(xin[:, 1, :], x[P:2 * P, :]).then_inc(x_in[1], 16)
            for dst, src in ((ident[:, :], eye), (gain_b[:, 0, :], ln_in_g), (gain_b[:, 1, :], ln_in_b),
                             (cos_t[:, :, :], rope_cos.rearrange("(t p) c -> p t c", p=P)),
                             (sin_t[:, :, :], rope_sin.rearrange("(t p) c -> p t c", p=P)),
                             (qkg[:, :], qk_gain)):
                sp.dma_start(dst, src).then_inc(const_in, 16)
            for k in range(KD):
                if k >= RAW:
                    sp.wait_ge(win_lo, k - RAW + 1)
                sp.dma_start(win_raw[:, k % RAW, :], w_in[k * P:(k + 1) * P, :]).then_inc(win_in[k % RAW], 16)

            q_t = q_d.rearrange("(v t) c -> v t c", v=KVH)
            kv_t = kv_d.rearrange("(v t) c -> v t c", v=KVH)

            def stage_a(b, first, last_b):
                for hf in range(2):
                    j = 2 * b + hf
                    rows = [bass.ds(at(sp, j * (2 * P) + k * P), P) for k in range(4)] if not (last_b and hf == 1) else \
                        [bass.ds(j * (2 * P) + k * P, P) for k in range(2)]
                    for tt in range(2):
                        sp.wait_ge(xln_ready, 2 * j + tt + 1)
                        sp.dma_start(xln_d[rows[tt], :], xln[:, tt, :]).then_inc(xln_st[tt], 16)
                        if not (last_b and hf == 1):
                            sp.dma_start(xin[:, tt, :], x[rows[2 + tt], :]).then_inc(x_in[tt], 16)
                    for tt in range(2):
                        sp.wait_ge(v_ready, 2 * j + tt + 1)
                        sp.wait_ge(roped, 2 * j + tt + 1)
                        sp.dma_start(q_t[:, rows[tt], :].rearrange("v p c -> p v c"),
                                     qkv[:, tt, :, 0:KVC - 2 * HD]).then_inc(q_st[tt], 16)
                        sp.dma_start(kv_t[:, rows[tt], :].rearrange("v p c -> p v c"),
                                     qkv[:, tt, :, KVC - 2 * HD:KVC]).then_inc(kv_st[tt], 16)

            steps(sp, PAIRS // 2, stage_a)
            for tt in range(2):
                sp.wait_ge(xln_st[tt], 16 * PAIRS)
                sp.wait_ge(q_st[tt], 16 * PAIRS)
                sp.wait_ge(kv_st[tt], 16 * PAIRS)
                sp.wait_ge(u_st[tt], 8 * PAIRS)

            stage_end(sp, 1)
            for dst, src in ((ident2[0:HD, :], eye[0:HD, 0:HD]), (ident2[HD:P, :], eye[0:HD, 0:HD]),
                             (edge_t[:, :, :, :], pool_edge.rearrange("p (w s n) -> p w s n", w=NW, s=2)),
                             (wp_sb[:, :, :], w_pool.rearrange("w c d -> c w d")),
                             (psc[:, :], pool_scale)):
                sp.dma_start(dst, src).then_inc(b_const, 16)

            def stage_b(s, first):
                rows = bass.ds(at(sp, s * SEQ), SEQ)
                if not first:
                    sp.wait_ge(kv_split, 4 * s)
                sp.dma_start(kv_raw[:, :, :], kv_d[rows, :].rearrange("(t p) c -> p t c", p=P)).then_inc(kv_in, 16)
                if not first:
                    sp.wait_ge(q_split, QH * s)
                sp.dma_start(q_raw[:, :, :], q_d[rows, :].rearrange("(t p) c -> p t c", p=P)).then_inc(q_in, 16)

            some_steps(sp, SLOTS, stage_b)
            stage_end(sp, 2)

            for dst, src in ((wr_sb[:, :, :], w_router.rearrange("(k p) e -> p k e", p=P)),
                             (gain_b[:, 0, :], ln1_g), (gain_b[:, 1, :], ln1_b)):
                sp.dma_start(dst, src).then_inc(c_const, 16)
            for k in range(KM):
                if k >= 2:
                    sp.wait_ge(wo_lo, k - 1)
                sp.dma_start(wo_raw[:, k % 2, :], w_out[k * P:(k + 1) * P, :]).then_inc(wo_in[k % 2], 16)
                if k < 2:
                    sp.dma_start(res[:, k, :], xln_d[k * P:(k + 1) * P, :]).then_inc(res_in[k], 16)

            def stage_c(b, first, last_b):
                rows = [bass.ds(at(sp, (2 * b + k) * P), P) for k in range(2 if last_b else 4)]
                for sl in range(2):
                    i = 2 * b + sl
                    if not last_b:
                        sp.wait_ge(r_ready, 2 * i + 2)
                        sp.dma_start(res[:, sl, :], xln_d[rows[2 + sl], :]).then_inc(res_in[sl], 16)
                    sp.wait_ge(h_ready, i + 1)
                    sp.dma_start(h_d[rows[sl], :], hid[:, sl, :]).then_inc(h_st[sl], 16)
                    sp.wait_ge(acc_ready, i + 1)
                    sp.dma_start(acc_d[rows[sl], :], acc[:, sl, :]).then_inc(acc_st[sl], 16)

            steps(sp, TILES // 2, stage_c)
            for sl in range(2):
                sp.wait_ge(h_st[sl], 8 * TILES)
                sp.wait_ge(acc_st[sl], 8 * TILES)
            stage_end(sp, 3)

            def stage_e(e, first, last_e):
                ex = bass.ds(e, 1)
                for c in range(NCHUNK):
                    if not (first and c < RING):
                        sp.wait_ge(w_lo, NCHUNK * e + c - RING + 1)
                    dst = w_raw[:, c % RING, :]
                    if c < NUP:
                        w = (w_gate, w_up)[c % 2]
                        src = w[ex, :, (c // 2) * 2 * P:(c // 2 + 1) * 2 * P].rearrange("o (k p) f -> p (o k) f", p=P)
                        dst = dst.rearrange("p (k f) -> p k f", k=KD)
                    else:
                        m = c - NUP
                        src = w_down[ex, m * 2 * P:(m + 1) * 2 * P, :].rearrange("o (k p) d -> p (o k) d", p=P)
                        dst = dst.rearrange("p (k d) -> p k d", k=2)
                    sp.dma_start(dst, src).then_inc(w_dma[c % RING], 16)

            steps(sp, E, stage_e)
            stage_end(sp, 4)

            for dst, src in ((gain_b[:, 0, :], ln2_g), (gain_b[:, 1, :], ln2_b)):
                sp.dma_start(dst, src).then_inc(f_const, 16)
            for i in range(FR):
                sp.dma_start(y_raw[:, i, :], acc_d[i * P:(i + 1) * P, :]).then_inc(y_in[i], 16)

            def stage_f(b, first, last_b):
                rows = [bass.ds(at(sp, (FR * b + k) * P), P) for k in range(FR if last_b else 2 * FR)]
                for k in range(FR):
                    sp.wait_ge(f_ready, FR * b + k + 1)
                    sp.dma_start(out[rows[k], :], y_out[:, k, :]).then_inc(y_st[k], 16)
                    if not last_b:
                        sp.dma_start(y_raw[:, k, :], acc_d[rows[FR + k], :]).then_inc(y_in[k], 16)

            steps(sp, TILES // FR, stage_f)
            for k in range(FR):
                sp.wait_ge(y_st[k], 16 * TILES // FR)

        @block.tensor
        def _(pe):
            def stage_a(b, first, last_b):
                for hf in range(2):
                    j = 2 * b + hf
                    start = first and hf == 0
                    for tt in range(2):
                        i = 2 * j + tt
                        pe.wait_ge(xln_ready, i + 1)
                        if start and tt == 0:
                            pe.wait_ge(const_in, 96)
                        if not start:
                            pe.wait_ge(xt_hi, i - 1)
                            pe.wait_ge(xt_lo, i - 1)
                        for k in range(KD):
                            last = nc.tensor.transpose(ps_xt[tt][:, k, :], xln[:, tt, k * P:(k + 1) * P], ident[:, :])
                        last.then_inc(xt_done, 1)
                    for tt in range(2):
                        i = 2 * j + tt
                        pe.wait_ge(xt_hi, i + 1)
                        pe.wait_ge(xt_lo, i + 1)
                        for ps, c0, c1, done in ((ps_q, 0, AW, q_done), (ps_kv, AW, QKVW, kv_done)):
                            if not (start and tt == 0):
                                pe.wait_ge(qn_ready, i)
                                pe.wait_ge(v_ready, i)
                            for k in range(KD):
                                if start and tt == 0 and c0 == 0:
                                    pe.wait_ge(win_hi, k + 1)
                                    pe.wait_ge(win_lo, k + 1)
                                t = slice(tt * P, (tt + 1) * P)
                                for n, (a, w) in enumerate(((xt_h, win_h), (xt_h, win_l), (xt_l, win_h))):
                                    last = nc.tensor.matmul(ps[:, 0:c1 - c0], a[:, hf, k, t], w[:, k, c0:c1],
                                                            start=k == 0 and n == 0, stop=k == KD - 1 and n == 2)
                            last.then_inc(done, 1)
                    for cp in range(2):
                        if not start:
                            pe.wait_ge(u_ready, 2 * j - 1 + cp)
                        for c in range(2):
                            c0 = QKVW + (2 * cp + c) * P
                            for k in range(KD):
                                for n, (w, a) in enumerate(((win_h, xt_h), (win_h, xt_l), (win_l, xt_h))):
                                    last = nc.tensor.matmul(ps_u[cp][:, c, :], w[:, k, c0:c0 + P], a[:, hf, k, :],
                                                            start=k == 0 and n == 0, stop=k == KD - 1 and n == 2)
                        last.then_inc(u_done, 1)

            steps(pe, PAIRS // 2, stage_a)

            stage_end(pe, 1)
            pe.wait_ge(b_const, 80)
            pe.wait_ge(ident_ready, 1)

            def stage_b(s, first):
                def m_turn(what):
                    n = turn[what]
                    if not (first and n == 0):
                        pe.wait_ge(m_free, TURNS * s + n)

                pe.wait_ge(kv_split, 4 * s + 2)
                for lo, kd in enumerate((kd_h, kd_l)):
                    for r in range(GT // 4):
                        m_turn(("K", lo, r))
                        for c in range(4):
                            last = nc.tensor.transpose(ps_m[:, c, :].bitcast(f32r), kd[:, 4 * r + c, :], ident_r[:, :])
                        last.then_inc(m_full, 1)

                def q_transposes(h, r):
                    pe.wait_ge(q_split, QH * s + h + 1)
                    m_turn(("Q", h, r))
                    for c in range(4):
                        last = nc.tensor.transpose(ps_m[:, c, :].bitcast(f32r), q_hl[:, h % 2, 4 * r + c, :], ident_r[:, :])
                    last.then_inc(m_full, 1)

                def scores(t):
                    h = t // GT
                    if t % GT == 0:
                        pe.wait_ge(m_free, TURNS * s + turn[("Q", h, 1)] + 1)
                    if not (first and t < 2):
                        pe.wait_ge(exp_ready, NSTEP * s + t - 1)
                    q = qt_hl[:, h % 2, (t % GT) * P:(t % GT + 1) * P]
                    for c in range(SEQ // 512):
                        cols = slice(c * 512, (c + 1) * 512)
                        nc.tensor.matmul(ps_s[t % 2][:, cols], q, kt_h[:, cols], start=True, stop=False)
                        last = nc.tensor.matmul(ps_s[t % 2][:, cols], q, kt_l[:, cols], start=False, stop=True)
                    last.then_inc(s_done, 1)

                def transposes(t):
                    pe.wait_ge(exp_ready, NSTEP * s + t + 1)
                    for r in range(2):
                        if not (first and t == 0):
                            pe.wait_ge(pt_lo, 2 * (NSTEP * s + t) + r - 1)
                        for c in range(4):
                            k = 4 * r + c
                            last = nc.tensor.transpose(ps_t[r][:, c, :], prob[:, t % 2, k * P:(k + 1) * P], ident[:, :])
                        last.then_inc(t_done, 1)

                def values(b):
                    pe.wait_ge(pt_lo, 2 * (NSTEP * s + 2 * b + 2))
                    if b == 0:
                        pe.wait_ge(kv_split, 4 * s + 4)
                    if not (first and b == 0):
                        pe.wait_ge(o_ready, NQB * s + b)
                    for k in range(GT):
                        for n, pt in enumerate((pt_h, pt_l)):
                            last = nc.tensor.matmul(ps_pv[:, 0:QB], v_hl[:, k, :], pt[:, b % 2, k, :],
                                                    start=k == 0 and n == 0, stop=k == GT - 1 and n == 1)
                    last.then_inc(pv_done, 1)

                def add_halves(b):
                    pe.wait_ge(o_ready, NQB * s + b + 1)
                    m_turn(("add", b))
                    for c in range(2):
                        last = nc.tensor.matmul(ps_m[:, c, 0:HD], o_hl[:, b % 2, c * P:(c + 1) * P], ident2[:, :],
                                                start=True, stop=True)
                    last.then_inc(m_full, 1)

                def back(b):
                    m_turn(("back", b))
                    for c in range(2):
                        i = (2 * b + c) % GT
                        last = nc.tensor.transpose(ps_m[:, c, :], at_tok[:, i, :], ident[:, :])
                    last.then_inc(m_full, 1)

                for r in range(2):
                    q_transposes(0, r)
                scores(0)
                scores(1)
                for t in range(NSTEP + 3):
                    if t < NSTEP:
                        transposes(t)
                        if t + 2 < NSTEP:
                            scores(t + 2)
                        if t % GT in q_turn_at and t // GT + 1 < QH:
                            q_transposes(t // GT + 1, q_turn_at[t % GT])
                    pv, add, bk = after_step(t)
                    if pv is not None:
                        values(pv)
                    if add is not None:
                        add_halves(add)
                    if bk is not None:
                        back(bk)

            some_steps(pe, SLOTS, stage_b)

            for n in range(GROUPS * NW):
                g, w = divmod(n, NW)
                pe.wait_ge(m_ready, n + 1)
                if n >= 2:
                    pe.wait_ge(pl_ready, n - 1)
                for c in range(SEQ // 512):
                    last = nc.tensor.matmul(ps_s[n % 2][:, c * 512:(c + 1) * 512], wp_sb[:, w, :],
                                            mix_pl[:, w, g * SEQ + c * 512:g * SEQ + (c + 1) * 512], start=True, stop=True)
                last.then_inc(pm_done, 1)
            stage_end(pe, 2)

            pe.wait_ge(c_const, 48)

            def out_proj(i, sl, c, start, first_tile):
                if c == 0:
                    pe.wait_ge(mx_lo, i + 1)
                if not start:
                    pe.wait_ge(r_ready, 2 * i - 3 + c)
                for k in range(KM):
                    if first_tile and c == 0:
                        pe.wait_ge(wo_lo, k + 1)
                    cols = slice(c * 512, (c + 1) * 512)
                    for n, (a, w) in enumerate(((mx_h, wo_h), (mx_h, wo_l), (mx_l, wo_h))):
                        last = nc.tensor.matmul(ps_o[sl][:, cols], a[:, sl, k, :], w[:, k, cols],
                                                start=k == 0 and n == 0, stop=k == KM - 1 and n == 2)
                last.then_inc(o_done, 1)

            def h_transposes(i, sl, start):
                pe.wait_ge(h_ready, i + 1)
                if not start:
                    pe.wait_ge(ht_ready, i)
                for k in range(KD):
                    last = nc.tensor.transpose(ps_ht[:, k, :], hid[:, sl, k * P:(k + 1) * P], ident[:, :])
                last.then_inc(ht_done, 1)

            def router(i, start):
                pe.wait_ge(ht_ready, i + 1)
                if not start:
                    pe.wait_ge(l_ready, i)
                for k in range(KD):
                    last = nc.tensor.matmul(ps_l[:, 0:E], ht[:, k, :], wr_sb[:, k, :], start=k == 0, stop=k == KD - 1)
                last.then_inc(l_done, 1)

            def stage_c(b, first):
                for sl in range(2):
                    i = 2 * b + sl
                    out_proj(i, sl, 0, first, first and sl == 0)
                    if not first:
                        router(i - 2, first)
                    out_proj(i, sl, 1, first, first and sl == 0)
                    if not (first and sl == 0):
                        h_transposes(i - 1, 1 - sl, first)

            stage_c(0, True)
            for sl in range(2):
                out_proj(2 + sl, sl, 0, False, False)
                router(sl, sl == 0)
                out_proj(2 + sl, sl, 1, False, False)
                h_transposes(1 + sl, 1 - sl, False)
            with pe.Fori(2, TILES // 2) as b:
                stage_c(b, False)
            router(TILES - 2, False)
            h_transposes(TILES - 1, 1, False)
            router(TILES - 1, False)
            stage_end(pe, 3)

            pe.wait_ge(d_aff, 1)
            for t in range(TILES):
                last = nc.tensor.transpose(ps_y[t // GT][0:E, (t % GT) * P:(t % GT + 1) * P], logits[:, t, :], ident[:, :])
            last.then_inc(d_step, 1)
            pe.wait_ge(top_ready, 1)
            nc.tensor.transpose(ps_x[:, 0, 0:ROWS], top_v[:, :], ident[0:ROWS, 0:ROWS])
            nc.tensor.transpose(ps_x[:, 1, 0:ROWS], top_f[:, :], ident[0:ROWS, 0:ROWS]).then_inc(d_step, 1)
            pe.wait_ge(top_ready, 2)

            XR = GROUPS * KD // 4

            def x_round(e, n, start):
                g, r = divmod(n, KD // 4)
                pe.wait_ge(x_in_g[g], 16 * (e + 1))
                if not start:
                    pe.wait_ge(x_lo, XR * e + n)
                for c in range(4):
                    k = 4 * r + c
                    last = nc.tensor.transpose(ps_x[:, c, :], xg[:, g, k * P:(k + 1) * P], ident[:, :])
                last.then_inc(xt_d, 1)

            for n in range(XR):
                x_round(0, n, n == 0)

            def stage_e(e, first, last_e):
                pe.wait_ge(x_lo, XR * (e + 1))
                for n in range(KF):
                    if n % 2 == 0:
                        pe.wait_ge(w_lo, NCHUNK * e + n + 2)
                    if not (first and n < 3):
                        pe.wait_ge(h_split, KF * e + n - 2)
                    for u in range(2):
                        c = (n // 2) * 2 + u
                        wh = w_h[:, c % RING, :].rearrange("p (k f) -> p k f", k=KD)
                        wl = w_l[:, c % RING, :].rearrange("p (k f) -> p k f", k=KD)
                        cols = slice((n % 2) * P, (n % 2 + 1) * P)
                        for k in range(KD):
                            for q, (w, a) in enumerate(((wh, x_h), (wh, x_l), (wl, x_h))):
                                last = nc.tensor.matmul(ps_gu[n % 3][:, u, :], w[:, k, cols], a[:, k, :],
                                                        start=k == 0 and q == 0, stop=k == KD - 1 and q == 2)
                    last.then_inc(gu_done, 1)
                for m in range(KF // 2):
                    c = NUP + m
                    pe.wait_ge(w_lo, NCHUNK * e + c + 1)
                    pe.wait_ge(h_split, KF * e + 2 * m + 2)
                    if m == 0 and not first:
                        pe.wait_ge(y_ready, GROUPS * e)
                    for kk in range(2):
                        k = 2 * m + kk
                        for g in range(GROUPS):
                            tok = slice(g * CAP, (g + 1) * CAP)
                            for q, (a, w) in enumerate(((hh, w_h), (hh, w_l), (hl, w_h))):
                                for c2 in range(D // 512):
                                    last = nc.tensor.matmul(
                                        ps_y[g][:, c2 * 512:(c2 + 1) * 512], a[:, k, tok],
                                        w[:, c % RING, kk * D + c2 * 512:kk * D + (c2 + 1) * 512],
                                        start=k == 0 and q == 0, stop=k == KF - 1 and q == 2)
                    last.then_inc(dn_done, 1)
                    if 2 <= m < 2 + XR and not last_e:
                        x_round(e + 1, m - 2, False)

            steps(pe, E, stage_e)
            stage_end(pe, 4)

        @block.scalar
        def _(act):
            act.wait_ge(eps_set, 1)

            def ln_in_sd(j):
                for tt in range(2):
                    act.wait_ge(var_ready, 2 * j + tt + 1)
                    nc.scalar.activation(sd[:, tt, :], mv[:, tt, 1:2], ACT.Sqrt, bias=eps[:, 0:1]).then_inc(sd_ready, 1)

            def stage_a(b, first, last_b):
                for hf in range(2):
                    j = 2 * b + hf
                    start = first and hf == 0
                    for tt in range(2):
                        i = 2 * j + tt
                        act.wait_ge(xt_done, i + 1)
                        if not first:
                            act.wait_ge(u_done, 2 * j - 2)
                        nc.scalar.activation(xt_h[:, hf, :, tt * P:(tt + 1) * P], ps_xt[tt][:, :, :], ACT.Copy).then_inc(xt_hi, 1)
                    for tt in range(2):
                        i = 2 * j + tt
                        act.wait_ge(q_done, i + 1)
                        if not (start and tt == 0):
                            act.wait_ge(ss_ready, i)
                        nc.scalar.activation(sq[:, 0:AW], ps_q[:, :], ACT.Square)
                        act.wait_ge(kv_done, i + 1)
                        nc.scalar.activation(sq[:, AW:QKW], ps_kv[:, 0:KVW], ACT.Square)
                        if not start:
                            act.wait_ge(kv_st[tt], 16 * j)
                        nc.scalar.activation(qkv[:, tt, :, KVC - HD:KVC],
                                             ps_kv[:, KVW:2 * KVW].rearrange("p (v c) -> p v c", c=HD), ACT.Copy).then_inc(v_ready, 1)
                        act.wait_ge(ss_ready, i + 1)
                        nc.scalar.activation(rn[:, tt, 0:HEADS + KVH], ss[:, tt, 0:HEADS + KVH], ACT.Sqrt,
                                             bias=eps[:, 1:2], scale=1.0 / HD).then_inc(rms_sd, 1)
                    if not (last_b and hf == 1):
                        ln_in_sd(j + 1)
                    row = at(act, j * (2 * P))
                    for cp in range(2):
                        act.wait_ge(u_done, 2 * j + cp + 1)
                        if not first:
                            act.wait_ge(u_st[hf], 16 * b)
                        nc.scalar.activation(ust[:, hf, 2 * cp:2 * cp + 2, :], ps_u[cp][:, :, :], ACT.Copy).then_inc(u_ready, 1)
                    act.wait_ge(u_ready, 2 * j + 2)
                    act.dma_start(ut_d[:, :, bass.ds(row, 2 * P)].rearrange("w p t -> p w t"),
                                  ust[:, hf, :, :]).then_inc(u_st[hf], 16)

            ln_in_sd(0)
            for k in range(KD):
                act.wait_ge(win_in[k % RAW], 16 * (k // RAW + 1))
                nc.scalar.activation(win_h[:, k, :], win_raw[:, k % RAW, :], ACT.Copy).then_inc(win_hi, 1)
            steps(act, PAIRS // 2, stage_a)

            stage_end(act, 1)
            nc.scalar.activation(ident_r[:, :], ident[:, :], ACT.Copy).then_inc(ident_ready, 1)

            def stage_b(s, first):
                act.wait_ge(kv_in, 16 * s + 16)
                if not first:
                    act.wait_ge(pv_done, NQB * s)
                for d in range(2):
                    last = nc.scalar.activation(kd_h[:, :, d * HD:(d + 1) * HD], kv_raw[:, :, 0:HD], ACT.Copy)
                last.then_inc(k_hi, 1)
                nc.scalar.activation(v_hl[:, :, 0:HD], kv_raw[:, :, HD:2 * HD], ACT.Copy).then_inc(k_hi, 1)

                def full(what):
                    act.wait_ge(m_full, TURNS * s + turn[what] + 1)

                for lo, kt in enumerate((kt_h, kt_l)):
                    for r in range(2):
                        full(("K", lo, r))
                        nc.scalar.activation(kt[:, r * 512:(r + 1) * 512], ps_m[:, :, :].bitcast(f32), ACT.Copy).then_inc(m_free, 1)

                def q_copy(h, r):
                    full(("Q", h, r))
                    nc.scalar.activation(qt_hl[:, h % 2, r * 512:(r + 1) * 512], ps_m[:, :, :].bitcast(f32), ACT.Copy).then_inc(m_free, 1)

                def exp(t):
                    act.wait_ge(max_ready, NSTEP * s + t + 1)
                    if not (first and t < 2):
                        act.wait_ge(t_done, 2 * (NSTEP * s + t - 1))
                    i = t % (2 * GT)
                    nc.scalar.activation(prob[:, t % 2, :], ps_s[t % 2][:, :], ACT.Exp, bias=nmax[:, t % 2:t % 2 + 1],
                                         scale=HD ** -0.5, accum_out=rsum[:, i:i + 1]).then_inc(exp_ready, 1)

                def hi(t):
                    b = t // 2
                    for r in range(2):
                        act.wait_ge(t_done, 2 * (NSTEP * s + t) + r + 1)
                        if t % 2 == 0 and r == 0 and not (first and b < 2):
                            act.wait_ge(pv_done, NQB * s + b - 1)
                        nc.scalar.activation(pt_h[:, b % 2, 4 * r:4 * r + 4, (t % 2) * P:(t % 2 + 1) * P],
                                             ps_t[r][:, :, :], ACT.Copy).then_inc(pt_hi, 1)

                for r in range(2):
                    q_copy(0, r)
                exp(0)
                if not first:
                    col = at(act, s * SEQ + (s // 2) * SEQ * (PAIR_H - 1) * GROUPS)
                else:
                    col = 0
                mix = mix_at.rearrange("p v j t -> p (v j t)")
                for t in range(NSTEP + 3):
                    if t < NSTEP:
                        if t + 1 < NSTEP:
                            exp(t + 1)
                        hi(t)
                        if t % GT in q_turn_at and t // GT + 1 < QH:
                            q_copy(t // GT + 1, q_turn_at[t % GT])
                    pv, add, bk = after_step(t)
                    if pv is not None:
                        act.wait_ge(pv_done, NQB * s + pv + 1)
                        if not (first and pv < 2):
                            act.wait_ge(m_full, TURNS * s + (turn[("add", pv - 2)] if pv >= 2 else
                                                             turn[("add", NQB - 2 + pv)] - TURNS) + 1)
                        nc.scalar.activation(o_hl[:, pv % 2, :], ps_pv[:, 0:QB], ACT.Copy).then_inc(o_ready, 1)
                    if bk is not None:
                        full(("back", bk))
                        pair, qb = divmod(bk, 2 * GT // 2)
                        off = pair * TOK + (qb % (GT // 2)) * QB
                        nc.scalar.activation(mix[:, bass.ds(col + off, QB)],
                                             ps_m[:, 0:2, :].rearrange("p c t -> p (c t)"), ACT.Copy).then_inc(m_free, 1)

            some_steps(act, SLOTS, stage_b)

            for n in range(GROUPS * NW):
                g, w = divmod(n, NW)
                act.wait_ge(pm_done, n + 1)
                act.wait_ge(b_const, 80)
                nc.scalar.activation(mix_pl[:, w, g * SEQ:(g + 1) * SEQ], ps_s[n % 2][:, :], ACT.Identity,
                                     scale=psc[:, w:w + 1]).then_inc(pl_ready, 1)
            stage_end(act, 2)

            def mix_hi(i, sl, start):
                if not start:
                    act.wait_ge(o_done, 2 * i - 2)
                cols = bass.ds(at(act, i * P), P)
                nc.scalar.activation(mx_h[:, sl, 0:NW, :], mix_at.rearrange("p v j t -> p (v j) t")[:, :, cols], ACT.Copy)
                nc.scalar.activation(mx_h[:, sl, NW:KM, :], mix_pl[:, :, cols], ACT.Copy).then_inc(mx_hi, 1)

            mix_hi(0, 0, True)
            for k in range(KM):
                act.wait_ge(wo_in[k % 2], 16 * (k // 2 + 1))
                nc.scalar.activation(wo_h[:, k, :], wo_raw[:, k % 2, :], ACT.Copy).then_inc(wo_hi, 1)

            def logit_copy(i):
                act.wait_ge(l_done, i + 1)
                nc.scalar.activation(logits[:, bass.ds(i, 1), :], ps_l[:, 0:E].unsqueeze(1), ACT.Copy).then_inc(l_ready, 1)

            def ht_copy(i, start):
                act.wait_ge(ht_done, i + 1)
                if not start:
                    act.wait_ge(l_done, i)
                nc.scalar.activation(ht[:, :, :], ps_ht[:, :, :], ACT.Copy).then_inc(ht_ready, 1)

            def stage_c(b, first, last_b):
                for sl in range(2):
                    i = 2 * b + sl
                    if not (last_b and sl == 1):
                        mix_hi(i + 1, 1 - sl, first and sl == 0)
                    if not first:
                        logit_copy(i - 2)
                    if not (first and sl == 0):
                        ht_copy(i - 1, first)
                    act.wait_ge(c_var, i + 1)
                    nc.scalar.activation(sd[:, sl, :], mv[:, sl, 1:2], ACT.Sqrt, bias=eps[:, 0:1]).then_inc(c_sd, 1)

            steps(act, TILES // 2, stage_c)
            logit_copy(TILES - 2)
            ht_copy(TILES - 1, False)
            logit_copy(TILES - 1)
            stage_end(act, 3)

            def w_hi_copy(e, c, start):
                act.wait_ge(w_dma[c % RING], 16 * ((NCHUNK // RING) * e + c // RING + 1))
                if not start:
                    act.wait_ge(*(used(e, c - RING) if c >= RING else used(e - 1, NCHUNK + c - RING)))
                nc.scalar.activation(w_h[:, c % RING, :], w_raw[:, c % RING, :], ACT.Copy).then_inc(w_hi, 1)

            act.wait_ge(d_exp, 1)
            nc.scalar.activation(logits[:, :, :], logits[:, :, :], ACT.Exp).then_inc(d_exp, 1)
            for c in range(RING):
                w_hi_copy(0, c, True)

            XR = GROUPS * KD // 4

            def x_hi_copy(e, n):
                g, r = divmod(n, KD // 4)
                act.wait_ge(xt_d, XR * e + n + 1)
                nc.scalar.activation(x_h[:, 4 * r:4 * r + 4, g * CAP:(g + 1) * CAP], ps_x[:, :, :], ACT.Copy).then_inc(x_hi, 1)

            for n in range(XR):
                x_hi_copy(0, n)

            def stage_e(e, first, last_e):
                for j in range(KF // 2):
                    for n in (2 * j, 2 * j + 1):
                        act.wait_ge(gu_done, KF * e + n + 1)
                        if not (first and n < 2):
                            act.wait_ge(h_split, KF * e + n - 1)
                        nc.scalar.activation(sg[:, n % 2, :], ps_gu[n % 3][:, 0, :], ACT.Silu).then_inc(silu_done, 1)
                    for c in (2 * j + RING, 2 * j + RING + 1):
                        w_hi_copy(e, c, False)
                for m in range(KF // 2):
                    if 2 <= m < 2 + XR and not last_e:
                        x_hi_copy(e + 1, m - 2)
                    c = NUP + m + RING
                    if c < NCHUNK:
                        w_hi_copy(e, c, False)
                    elif not last_e:
                        w_hi_copy(e + 1, c - NCHUNK, False)
                act.wait_ge(dn_done, (KF // 2) * (e + 1))
                for g in range(GROUPS):
                    if not first:
                        act.wait_ge(scat[g], 16 * e)
                    nc.scalar.activation(ysb[:, g, :], ps_y[g][:, :], ACT.Identity,
                                         scale=gate_w8[:, bass.ds(e + g * GOFF, 1)]).then_inc(y_ready, 1)

            steps(act, E, stage_e)
            stage_end(act, 4)

            def stage_f(b, first, last_b):
                for k in range(FR):
                    act.wait_ge(f_var, FR * b + k + 1)
                    nc.scalar.activation(fsd[:, k, :], fmv[:, k, 1:2], ACT.Sqrt, bias=eps[:, 0:1]).then_inc(f_sd, 1)

            steps(act, TILES // FR, stage_f)

        @block.vector
        def _(dve):
            nc.vector.memset(alpha[:, :], ALPHA)
            nc.vector.memset(eps[:, 0:1], LN_EPS)
            nc.vector.memset(eps[:, 1:2], RMS_EPS).then_inc(eps_set, 1)
            dve.wait_ge(const_in, 96)

            def split_w(k):
                dve.wait_ge(win_hi, k + 1)
                nc.vector.tensor_tensor(win_l[:, k, :], win_raw[:, k % RAW, :], win_h[:, k, :].bitcast(f32),
                                        ALU.subtract).then_inc(win_lo, 1)

            def ln_in_stats(j):
                for tt in range(2):
                    dve.wait_ge(x_in[tt], 16 * j + 16)
                    for c in range(2):
                        nc.vector.bn_stats(bst[:, tt, c, :], xin[:, tt, c * 512:(c + 1) * 512])
                    dve.drain()
                    nc.vector.bn_aggr(mv[:, tt, :], bst[:, tt, :, :]).then_inc(var_ready, 1)

            def ln_in_apply(j, start):
                for tt in range(2):
                    dve.wait_ge(sd_ready, 2 * j + tt + 1)
                    nc.vector.reciprocal(rs[:, tt, :], sd[:, tt, :])
                    if not start:
                        dve.wait_ge(xln_st[tt], 16 * j)
                        dve.wait_ge(xt_done, 2 * j + tt - 1)
                    nc.vector.scalar_tensor_tensor(xln[:, tt, :], xin[:, tt, :], mv[:, tt, 0:1], gain_b[:, 0, :],
                                                   ALU.subtract, ALU.mult)
                    dve.drain()
                    nc.vector.scalar_tensor_tensor(xln[:, tt, :], xln[:, tt, :], rs[:, tt, :], gain_b[:, 1, :],
                                                   ALU.mult, ALU.add).then_inc(xln_ready, 1)

            def stage_a(b, first, last_b):
                for hf in range(2):
                    j = 2 * b + hf
                    start = first and hf == 0
                    for tt in range(2):
                        i = 2 * j + tt
                        dve.wait_ge(xt_hi, i + 1)
                        nc.vector.tensor_tensor(xt_l[:, hf, :, tt * P:(tt + 1) * P], ps_xt[tt][:, :, :],
                                                xt_h[:, hf, :, tt * P:(tt + 1) * P].bitcast(f32), ALU.subtract).then_inc(xt_lo, 1)
                    for tt in range(2):
                        i = 2 * j + tt
                        H = HEADS + KVH
                        dve.wait_ge(v_ready, i + 1)
                        nc.vector.reduce_sum(ss[:, tt, 0:H], sq[:, :].rearrange("p (h c) -> p h c", c=HD), axis=AX.X).then_inc(ss_ready, 1)
                        dve.wait_ge(rms_sd, i + 1)
                        nc.vector.reciprocal(rn[:, tt, 0:H], rn[:, tt, 0:H])
                        dve.drain()
                        if not start:
                            dve.wait_ge(roped, i - 1)
                        nc.vector.tensor_tensor(qn[:, tt, 0:AW].rearrange("p (h c) -> p h c", c=HD),
                                                ps_q[:, :].rearrange("p (h c) -> p h c", c=HD),
                                                rn[:, tt, 0:HEADS].unsqueeze(2).to_broadcast([P, HEADS, HD]), ALU.mult)
                        nc.vector.tensor_tensor(qn[:, tt, AW:QKW].rearrange("p (h c) -> p h c", c=HD),
                                                ps_kv[:, 0:KVW].rearrange("p (h c) -> p h c", c=HD),
                                                rn[:, tt, HEADS:H].unsqueeze(2).to_broadcast([P, KVH, HD]),
                                                ALU.mult).then_inc(qn_ready, 1)
                    if not (last_b and hf == 1):
                        ln_in_stats(j + 1)
                        ln_in_apply(j + 1, False)

            ln_in_stats(0)
            ln_in_apply(0, True)
            for k in range(KD):
                split_w(k)
            steps(dve, PAIRS // 2, stage_a)

            stage_end(dve, 1)

            def stage_b(s, first):
                dve.wait_ge(k_hi, 2 * s + 1)
                for d in range(2):
                    nc.vector.tensor_tensor(kd_l[:, :, d * HD:(d + 1) * HD], kv_raw[:, :, 0:HD],
                                            kd_h[:, :, d * HD:(d + 1) * HD].bitcast(f32), ALU.subtract).then_inc(kv_split, 1)
                dve.wait_ge(k_hi, 2 * s + 2)
                nc.vector.tensor_tensor(v_hl[:, :, HD:2 * HD], kv_raw[:, :, HD:2 * HD],
                                        v_hl[:, :, 0:HD].bitcast(f32), ALU.subtract).then_inc(kv_split, 2)

                def row_max(t):
                    dve.wait_ge(s_done, NSTEP * s + t + 1)
                    nc.vector.reduce_max(smax[:, t % 2:t % 2 + 1], ps_s[t % 2][:, :], axis=AX.X)
                    dve.drain()
                    nc.vector.tensor_scalar(nmax[:, t % 2:t % 2 + 1], smax[:, t % 2:t % 2 + 1], -HD ** -0.5, None,
                                            ALU.mult).then_inc(max_ready, 1)

                def lo(t):
                    b = t // 2
                    for r in range(2):
                        dve.wait_ge(pt_hi, 2 * (NSTEP * s + t) + r + 1)
                        cols = slice((t % 2) * P, (t % 2 + 1) * P)
                        nc.vector.tensor_tensor(pt_l[:, b % 2, 4 * r:4 * r + 4, cols], ps_t[r][:, :, :],
                                                pt_h[:, b % 2, 4 * r:4 * r + 4, cols].bitcast(f32), ALU.subtract).then_inc(pt_lo, 1)

                row_max(0)
                row_max(1)
                for t in range(NSTEP + 3):
                    if t < NSTEP:
                        lo(t)
                        if t + 2 < NSTEP:
                            row_max(t + 2)
                    _, add, _ = after_step(t)
                    if add is not None:
                        h, i = add // (GT // 2), (2 * add) % GT
                        j = (2 * add) % (2 * GT)
                        nc.vector.reciprocal(rinv[:, j:j + 2], rsum[:, j:j + 2])
                        dve.drain()
                        dve.wait_ge(m_full, TURNS * s + turn[("add", add)] + 1)
                        nc.vector.tensor_tensor(at_tok[:, i:i + 2, (h % 2) * HD:(h % 2 + 1) * HD], ps_m[:, 0:2, 0:HD],
                                                rinv[:, j:j + 2].unsqueeze(2).to_broadcast([P, 2, HD]),
                                                ALU.mult).then_inc(m_free, 1)

            some_steps(dve, SLOTS, stage_b)
            stage_end(dve, 2)

            def mix_lo(i, sl):
                cols = bass.ds(at(dve, i * P), P)
                dve.wait_ge(mx_hi, i + 1)
                nc.vector.tensor_tensor(mx_l[:, sl, 0:NW, :], mix_at.rearrange("p v j t -> p (v j) t")[:, :, cols],
                                        mx_h[:, sl, 0:NW, :].bitcast(f32), ALU.subtract)
                nc.vector.tensor_tensor(mx_l[:, sl, NW:KM, :], mix_pl[:, :, cols],
                                        mx_h[:, sl, NW:KM, :].bitcast(f32), ALU.subtract).then_inc(mx_lo, 1)

            mix_lo(0, 0)
            for k in range(KM):
                dve.wait_ge(wo_hi, k + 1)
                nc.vector.tensor_tensor(wo_l[:, k, :], wo_raw[:, k % 2, :], wo_h[:, k, :].bitcast(f32),
                                        ALU.subtract).then_inc(wo_lo, 1)
            dve.wait_ge(c_const, 48)

            def stage_c(b, first, last_b):
                for sl in range(2):
                    i = 2 * b + sl
                    if not (last_b and sl == 1):
                        mix_lo(i + 1, 1 - sl)
                    dve.wait_ge(res_in[sl], 16 * b + 16)
                    if not first:
                        dve.wait_ge(h_st[sl], 16 * b)
                        dve.wait_ge(ht_done, i - 1)
                        dve.wait_ge(acc_ready, i - 1)
                    for c in range(2):
                        cols = slice(c * 512, (c + 1) * 512)
                        dve.wait_ge(o_done, 2 * i + c + 1)
                        nc.vector.scalar_tensor_tensor(hid[:, sl, cols], res[:, sl, cols], ALPHA, ps_o[sl][:, cols],
                                                       ALU.mult, ALU.add).then_inc(r_ready, 1)
                        dve.wait_ge(r_ready, 2 * i + c + 1)
                        nc.vector.bn_stats(bst[:, sl, c, :], hid[:, sl, cols])
                    dve.drain()
                    nc.vector.bn_aggr(mv[:, sl, :], bst[:, sl, :, :]).then_inc(c_var, 1)
                    dve.wait_ge(c_sd, i + 1)
                    nc.vector.reciprocal(rs[:, sl, :], sd[:, sl, :])
                    nc.vector.scalar_tensor_tensor(hid[:, sl, :], hid[:, sl, :], mv[:, sl, 0:1], gain_b[:, 0, :],
                                                   ALU.subtract, ALU.mult)
                    dve.drain()
                    nc.vector.scalar_tensor_tensor(hid[:, sl, :], hid[:, sl, :], rs[:, sl, :], gain_b[:, 1, :],
                                                   ALU.mult, ALU.add).then_inc(h_ready, 1)

            steps(dve, TILES // 2, stage_c)
            stage_end(dve, 3)

            nc.vector.memset(aff[:, :], 0.0)
            nc.vector.reduce_max(lmax[:, :], logits[:, :, :], axis=AX.X)
            dve.drain()
            nc.vector.tensor_tensor(logits[:, :, :], logits[:, :, :], lmax[:, :].unsqueeze(2).to_broadcast([P, TILES, E]),
                                    ALU.subtract).then_inc(d_exp, 1)
            dve.wait_ge(d_exp, 2)
            nc.vector.reduce_sum(lsum[:, :], logits[:, :, :], axis=AX.X)
            dve.drain()
            nc.vector.reciprocal(lsum[:, :], lsum[:, :])
            dve.drain()
            nc.vector.tensor_tensor(logits[:, :, :], logits[:, :, :], lsum[:, :].unsqueeze(2).to_broadcast([P, TILES, E]),
                                    ALU.mult).then_inc(d_aff, 1)
            dve.wait_ge(d_step, 1)
            for g in range(GROUPS):
                nc.vector.tensor_copy(aff[g * GOFF:g * GOFF + E, :], ps_y[g][0:E, :])

            def w_lo_sub(e, c):
                dve.wait_ge(w_hi, NCHUNK * e + c + 1)
                nc.vector.tensor_tensor(w_l[:, c % RING, :], w_raw[:, c % RING, :], w_h[:, c % RING, :].bitcast(f32),
                                        ALU.subtract).then_inc(w_lo, 1)

            for r in range(CAP // 8):
                cols = slice(8 * r, 8 * r + 8)
                dve.drain()
                nc.vector.max(top_v[:, cols], aff[:, :])
                dve.drain()
                nc.vector.max_index(top_i[:, cols], top_v[:, cols], aff[:, :])
                if r < CAP // 8 - 1:
                    nc.vector.match_replace(aff[:, :], top_v[:, cols], aff[:, :], -1.0)
            dve.drain()
            nc.vector.tensor_copy(top_f[:, :], top_i[:, :])
            dve.drain()
            nc.vector.tensor_scalar(top_f[GOFF:ROWS, :], top_f[GOFF:ROWS, :], float(SEQ), None, ALU.add).then_inc(top_ready, 1)
            dve.wait_ge(d_step, 2)
            nc.vector.tensor_copy(gate_w8[:, :], ps_x[:, 0, 0:ROWS])
            nc.vector.tensor_copy(idx_t[:, :], ps_x[:, 1, 0:ROWS]).then_inc(top_ready, 1)
            for c in range(RING):
                w_lo_sub(0, c)

            XR = GROUPS * KD // 4

            def x_lo_sub(e, n):
                g, r = divmod(n, KD // 4)
                dve.wait_ge(x_hi, XR * e + n + 1)
                dst = (slice(None), slice(4 * r, 4 * r + 4), slice(g * CAP, (g + 1) * CAP))
                nc.vector.tensor_tensor(x_l[dst], ps_x[:, :, :], x_h[dst].bitcast(f32), ALU.subtract).then_inc(x_lo, 1)

            for n in range(XR):
                x_lo_sub(0, n)

            def stage_e(e, first, last_e):
                for j in range(KF // 2):
                    for n in (2 * j, 2 * j + 1):
                        dve.wait_ge(silu_done, KF * e + n + 1)
                        if n == 0 and not first:
                            dve.wait_ge(dn_done, (KF // 2) * e)
                        nc.vector.tensor_tensor(hf[:, n % 2, :], sg[:, n % 2, :], ps_gu[n % 3][:, 1, :], ALU.mult)
                        dve.drain()
                        nc.vector.tensor_copy(hh[:, n, :], hf[:, n % 2, :])
                        dve.drain()
                        nc.vector.tensor_tensor(hl[:, n, :], hf[:, n % 2, :], hh[:, n, :].bitcast(f32),
                                                ALU.subtract).then_inc(h_split, 1)
                    for c in (2 * j + RING, 2 * j + RING + 1):
                        w_lo_sub(e, c)
                for m in range(KF // 2):
                    if 2 <= m < 2 + XR and not last_e:
                        x_lo_sub(e + 1, m - 2)
                    c = NUP + m + RING
                    if c < NCHUNK:
                        w_lo_sub(e, c)
                    elif not last_e:
                        w_lo_sub(e + 1, c - NCHUNK)

            steps(dve, E, stage_e)
            stage_end(dve, 4)

            dve.wait_ge(f_const, 32)

            def stage_f(b, first, last_b):
                for k in range(FR):
                    dve.wait_ge(y_in[k], 16 * b + 16)
                    for c in range(2):
                        nc.vector.bn_stats(fst[:, k, c, :], y_raw[:, k, c * 512:(c + 1) * 512])
                    dve.drain()
                    nc.vector.bn_aggr(fmv[:, k, :], fst[:, k, :, :]).then_inc(f_var, 1)
                for k in range(FR):
                    dve.wait_ge(f_sd, FR * b + k + 1)
                    nc.vector.reciprocal(frs[:, k, :], fsd[:, k, :])
                    if not first:
                        dve.wait_ge(y_st[k], 16 * b)
                    nc.vector.scalar_tensor_tensor(y_out[:, k, :], y_raw[:, k, :], fmv[:, k, 0:1], gain_b[:, 0, :],
                                                   ALU.subtract, ALU.mult)
                    dve.drain()
                    nc.vector.scalar_tensor_tensor(y_out[:, k, :], y_out[:, k, :], frs[:, k, :], gain_b[:, 1, :],
                                                   ALU.mult, ALU.add).then_inc(f_ready, 1)

            steps(dve, TILES // FR, stage_f)

        @block.gpsimd
        def _(pool):
            pool.wait_ge(const_in, 96)

            def stage_a(b, first, last_b):
                for hf in range(2):
                    j = 2 * b + hf
                    start = first and hf == 0
                    for tt in range(2):
                        i = 2 * j + tt
                        H = HEADS + KVH
                        qn3 = qn[:, tt, :].rearrange("p (h c) -> p h c", c=HD)
                        q4 = qn[:, tt, :].rearrange("p (h a s c) -> p h a s c", a=2, s=2, c=16)
                        r4 = rot[:, :].rearrange("p (h a s c) -> p h a s c", a=2, s=2, c=16)
                        pool.wait_ge(qn_ready, i + 1)
                        nc.gpsimd.tensor_tensor(qn[:, tt, :], qn[:, tt, :], qkg[:, :], ALU.mult)
                        pool.drain()
                        for s in range(2):
                            sn = sin_t[:, bass.ds(i, 1), :].rearrange("p t (a s c) -> p t a s c", s=2, c=16)[:, :, :, s, :]
                            nc.gpsimd.tensor_tensor(r4[:, :, :, s, :], q4[:, :, :, 1 - s, :],
                                                    sn.to_broadcast([P, H, 2, 16]), ALU.mult)
                        pool.drain()
                        cs = cos_t[:, bass.ds(i, 1), :]
                        nc.gpsimd.tensor_tensor(qn3, qn3, cs.to_broadcast([P, H, HD]), ALU.mult)
                        pool.drain()
                        if not start:
                            pool.wait_ge(q_st[tt], 16 * j)
                            pool.wait_ge(kv_st[tt], 16 * j)
                        for dst, c0, c1 in ((qkv[:, tt, :, 0:AW // KVH], 0, AW),
                                            (qkv[:, tt, :, AW // KVH:AW // KVH + HD], AW, QKW)):
                            last = nc.gpsimd.tensor_tensor(dst, qn[:, tt, c0:c1].rearrange("p (v c) -> p v c", v=KVH),
                                                           rot[:, c0:c1].rearrange("p (v c) -> p v c", v=KVH), ALU.add)
                        last.then_inc(roped, 1)

            steps(pool, PAIRS // 2, stage_a)

            stage_end(pool, 1)
            nc.gpsimd.memset(upad[:, 0:PAD], 0.0)
            nc.gpsimd.memset(upad[:, PAD + SEQ:], 0.0)

            def split_q(n):
                s, h = divmod(n, QH)
                pool.wait_ge(q_in, 16 * s + 16)
                if n >= 2:
                    s2, h2 = divmod(n - 2, QH)
                    pool.wait_ge(m_full, TURNS * s2 + turn[("Q", h2, 1)] + 1)
                q = q_raw[:, :, h * HD:(h + 1) * HD]
                nc.gpsimd.tensor_copy(q_hl[:, n % 2, :, 0:HD], q)
                pool.drain()
                nc.gpsimd.tensor_tensor(q_hl[:, n % 2, :, HD:P], q, q_hl[:, n % 2, :, 0:HD].bitcast(f32),
                                        ALU.subtract).then_inc(q_split, 1)

            def pool_window(n):
                g, w = divmod(n, NW)
                if n:
                    pool.wait_ge(m_ready, n)
                pool.dma_start(upad[:, PAD:PAD + SEQ], ut_d[w, :, g * SEQ:(g + 1) * SEQ]).then_inc(u_in, 16)
                pool.wait_ge(u_in, 16 * n + 16)
                src, n_in, width = upad, SEQ + 2 * PAD, 1
                for k in range(w + 1):
                    dst = (win_a, win_b)[k % 2]
                    n_in -= width
                    nc.gpsimd.tensor_tensor(dst[:, 0:n_in], src[:, 0:n_in], src[:, width:width + n_in], ALU.add)
                    pool.drain()
                    src, width = dst, 2 * width
                a = PAD - width // 2
                win = src[:, a:a + SEQ]
                for side, c in enumerate((slice(0, PAD), slice(SEQ - PAD, SEQ))):
                    nc.gpsimd.tensor_tensor(win[:, c], win[:, c], edge_t[:, w, side, :], ALU.mult)
                pool.drain()
                nc.gpsimd.tensor_scalar(win, win, 1.0 / width, None, ALU.mult)
                pool.drain()
                nc.gpsimd.tensor_tensor(mix_pl[:, w, g * SEQ:(g + 1) * SEQ], win, upad[:, PAD:PAD + SEQ],
                                        ALU.subtract).then_inc(m_ready, 1)

            pool.wait_ge(b_const, 80)
            split_q(0)
            split_q(1)
            for n in range(2, SLOTS * QH):
                split_q(n)
                if n % 2 == 1 and n // 2 <= GROUPS * NW:
                    pool_window(n // 2 - 1)
            pool_window(GROUPS * NW - 1)
            stage_end(pool, 2)

            def stage_c(b, first, last_b):
                for sl in range(2):
                    i = 2 * b + sl
                    pool.wait_ge(h_ready, i + 1)
                    if not first:
                        pool.wait_ge(acc_st[sl], 16 * b)
                    nc.gpsimd.tensor_tensor(acc[:, sl, :], hid[:, sl, :], alpha[:, 0:1].to_broadcast([P, D]),
                                            ALU.mult).then_inc(acc_ready, 1)

            steps(pool, TILES // 2, stage_c)
            stage_end(pool, 3)

            XR = GROUPS * KD // 4
            nc.gpsimd.memset(no_shift[:, :], 0)
            pool.wait_ge(top_ready, 2)

            def gather(e, start):
                if not start:
                    pool.wait_ge(xt_d, XR * e)
                for g in range(GROUPS):
                    nc.gpsimd.tensor_copy(idx_g[:, g:g + 1], idx_t[:, bass.ds(e + g * GOFF, 1)])
                pool.drain()
                for g in range(GROUPS):
                    pool.indirect_dma_start(out=xg[:, g, :], out_offset=None, in_=h_d[:, :],
                                            in_offset=bass.IndirectOffsetOnAxis(ap=idx_g[:, g:g + 1], axis=0)
                                            ).then_inc(x_in_g[g], 16)

            def scatter(e):
                for g in range(GROUPS):
                    nc.gpsimd.tensor_copy(idx_e[:, g:g + 1], idx_t[:, bass.ds(e + g * GOFF, 1)])
                pool.drain()
                pool.wait_ge(y_ready, GROUPS * (e + 1))
                nc.gpsimd.tensor_tensor(idx_s[:, :], idx_e[:, :], no_shift[:, :], ALU.add)
                pool.drain()
                for g in range(GROUPS):
                    pool.indirect_dma_start(out=acc_d[:, :], in_=ysb[:, g, :], in_offset=None,
                                            out_offset=bass.IndirectOffsetOnAxis(ap=idx_s[:, g:g + 1], axis=0),
                                            compute_op=ALU.add).then_inc(scat[g], 16)
                for g in range(GROUPS):
                    pool.wait_ge(scat[g], 16 * (e + 1))

            gather(0, True)

            def stage_e(e, first, last_e):
                if not last_e:
                    gather(e + 1, False)
                scatter(e)

            steps(pool, E, stage_e)
            stage_end(pool, 4)


_INS = ["x", "ln_in_g", "ln_in_b", "w_in", "qk_gain", "w_pool", "pool_scale", "w_out", "ln1_g", "ln1_b", "w_router",
        "w_gate", "w_up", "w_down", "ln2_g", "ln2_b", "rope_cos", "rope_sin", "pool_edge", "eye"]


def lay_out(x_prompt, x_sample, ln_in_g, ln_in_b, w_in, q_norm_g, k_norm_g, w_pool, pool_scale, w_out,
            ln1_g, ln1_b, w_router, w_gate, w_up, w_down, ln2_g, ln2_b):
    seq = x_prompt.shape[1]
    d = x_prompt.shape[2]
    rows = lambda v: np.ascontiguousarray(np.broadcast_to(v, (128, v.shape[-1])))
    grid_w, pairs, theta = 64, 16, 10000.0
    inv = theta ** (-np.arange(pairs, dtype=np.float32) / np.float32(pairs))
    row = np.repeat(np.arange(seq // grid_w), grid_w).astype(np.float32)[:, None] * inv.astype(np.float32)
    col = np.tile(np.arange(grid_w), seq // grid_w).astype(np.float32)[:, None] * inv.astype(np.float32)
    cos = np.concatenate([np.cos(row), np.cos(row), np.cos(col), np.cos(col)], axis=1)
    sin = np.concatenate([-np.sin(row), np.sin(row), -np.sin(col), np.sin(col)], axis=1)
    edge = np.ones((4, 2, 8), np.float32)
    for g, w in enumerate((2, 4, 8, 16)):
        for n in range(8):
            for side, t in ((0, n), (1, seq - 8 + n)):
                lo, hi = max(t - w // 2, 0), min(t - w // 2 + w, seq)
                edge[g, side, n] = w / (hi - lo)
    gains = np.concatenate([np.tile(q_norm_g[0], 8), np.tile(k_norm_g[0], 2)])
    return {
        "x": np.concatenate([x_prompt[0], x_sample[0]], axis=0),
        "ln_in_g": rows(ln_in_g), "ln_in_b": rows(ln_in_b), "w_in": w_in[0], "qk_gain": rows(gains),
        "w_pool": w_pool[0], "pool_scale": np.ascontiguousarray(pool_scale[0].reshape(4, 128).T), "w_out": w_out[0],
        "ln1_g": rows(ln1_g[0]), "ln1_b": rows(ln1_b[0]), "w_router": w_router[0],
        "w_gate": w_gate[0], "w_up": w_up[0], "w_down": w_down[0],
        "ln2_g": rows(ln2_g[0]), "ln2_b": rows(ln2_b[0]),
        "rope_cos": np.tile(cos, (2, 1)), "rope_sin": np.tile(sin, (2, 1)),
        "pool_edge": np.ascontiguousarray(np.broadcast_to(edge.reshape(-1), (128, 64))),
        "eye": np.eye(128, dtype=np.float32),
    }


def kernel(**inputs):
    import concourse.bacc as bacc
    from concourse.bass_utils import run_bass_kernel_spmd

    nc = bacc.Bacc("TRN2", target_bir_lowering=False, num_devices=1)
    arrays = {f"in_{n}": np.ascontiguousarray(a) for n, a in
              lay_out(**{k: np.asarray(v) for k, v in inputs.items()}).items()}
    args = [nc.dram_tensor(f"in_{n}", arrays[f"in_{n}"].shape, mybir.dt.float32, kind="ExternalInput").ap() for n in _INS]
    shape = arrays["in_x"].shape
    y = nc.dram_tensor("out_y", shape, mybir.dt.float32, kind="ExternalOutput").ap()
    encoder_layer(nc, *args, y)
    got = run_bass_kernel_spmd(nc, [arrays], core_ids=[0]).results[0]["out_y"]
    half = shape[0] // 2
    return got[:half].reshape(1, half, shape[1]), got[half:].reshape(1, half, shape[1])
```

```python
import numpy as np
from contextlib import ExitStack
import concourse.bass as bass
from concourse import mybir


def encoder_layer(nc, x, ln_in_g, ln_in_b, w_in, qk_gain, w_pool, pool_scale, w_out, ln1_g, ln1_b, w_router,
                  w_gate, w_up, w_down, ln2_g, ln2_b, rope_cos, rope_sin, pool_edge, eye, out):
    f32, f32r, u32 = mybir.dt.float32, mybir.dt.float32r, mybir.dt.uint32
    ALU, ACT, AX = mybir.AluOpType, mybir.ActivationFunctionType, mybir.AxisListType

    P = 128
    TOK, D = x.shape
    GROUPS = 2
    SEQ = TOK // GROUPS
    KD = D // P
    HD = 64
    HEADS, KVH = 8, 2
    AW, KVW = HEADS * HD, KVH * HD
    QKW = AW + KVW
    QKVW = AW + 2 * KVW
    PW = w_in.shape[1] - QKVW
    WINDOWS = (2, 4, 8, 16)
    PAD = max(WINDOWS) // 2
    NW = len(WINDOWS)
    E, _, F = w_gate.shape
    KF = F // P
    CAP = 2 * SEQ // E
    LN_EPS, RMS_EPS, ALPHA = 1e-5, 1e-6, 2.0 ** 0.25
    TILES = TOK // P
    GT = SEQ // P

    def dram(name, shape, dt=f32):
        return nc.dram_tensor(name, shape, dt, kind="Internal").ap()

    xln_d = dram("xln_d", (TOK, D))
    KVC = AW // KVH + 2 * HD
    q_d = dram("q_d", (KVH * TOK, AW // KVH))
    k_d = dram("k_d", (KVH * TOK, HD))
    v_d = dram("v_d", (KVH * TOK, HD))
    ut_d = dram("ut_d", (NW, P, TOK))
    h_d = dram("h_d", (TOK, D))
    acc_d = dram("acc_d", (TOK, D))

    ctx = ExitStack()
    with ctx:
        def sem(name):
            return ctx.enter_context(nc.semaphore(name))

        def alloc(stack):
            return lambda name, shape, dt=f32: stack.enter_context(nc.sbuf_tensor(name, shape, dt))

        def palloc(stack):
            return lambda name, shape, dt=f32: stack.enter_context(nc.psum_tensor(name, shape, dt))

        def at(eng, value):
            return value if isinstance(value, int) else eng.snap(value)

        def steps(eng, n, body):
            body(0, True, False)
            with eng.Fori(1, n - 1) as i:
                body(i, False, False)
            body(n - 1, False, True)

        sb = alloc(ctx)
        ident = sb("ident", [P, P])
        gain_b = sb("gain_b", [P, 2, D])
        eps = sb("eps", [P, 2])
        alpha = sb("alpha", [P, 1])
        logits = sb("logits", [P, TILES, E])
        mv = sb("mv", [P, 2, 2])
        bst = sb("bst", [P, 2, 2, 6])
        sd = sb("sd", [P, 2, 1])
        rs = sb("rs", [P, 2, 1])

        sa = ExitStack()
        sb, pb = alloc(sa), palloc(sa)
        PAIRS = TILES // 2
        win_h = sb("win_h", [P, KD, w_in.shape[1]], f32r)
        win_l = sb("win_l", [P, KD, w_in.shape[1]], f32r)
        RAW = 4
        win_raw = sb("win_raw", [P, RAW, w_in.shape[1]])
        xin = sb("xin", [P, 2, D])
        xln = sb("xln", [P, 2, D])
        xt_h = sb("xt_h", [P, 2, KD, 2 * P], f32r)
        xt_l = sb("xt_l", [P, 2, KD, 2 * P], f32r)
        cos_t = sb("cos_t", [P, TILES, HD])
        sin_t = sb("sin_t", [P, TILES, HD])
        qkg = sb("qkg", [P, QKW])
        sq = sb("sq", [P, QKW])
        qn = sb("qn", [P, 2, QKW])
        rot = sb("rot", [P, QKW])
        qkv = sb("qkv", [P, 2, KVH, KVC])
        ust = sb("ust", [P, 2, NW, 2 * P])
        ss = sb("ss", [P, 2, 16])
        rn = sb("rn", [P, 2, 16])
        ps_xt = [pb(f"ps_xt{i}", [P, KD, P]) for i in range(2)]
        ps_q = pb("ps_q", [P, AW])
        ps_kv = pb("ps_kv", [P, 512])
        ps_u = [pb(f"ps_u{i}", [P, 2, 2 * P]) for i in range(2)]
        sa.close()

        keep = ExitStack()
        sb = alloc(keep)
        SLOTS = KVH * GROUPS
        QH = HEADS // KVH
        QC = QH * HD
        PAIR_H = QH // 2
        mix_at = sb("mix_at", [P, KVH, PAIR_H, TOK])
        mix_pl = sb("mix_pl", [P, NW, TOK])
        sB = ExitStack()
        sb, pb = alloc(sB), palloc(sB)
        QB = 2 * P
        NQB = QH * SEQ // QB
        q_raw = sb("q_raw", [P, GT, QC])
        k_raw = sb("k_raw", [P, GT, HD])
        v_raw = sb("v_raw", [P, GT, HD])
        kd_h = sb("kd_h", [P, GT, P], f32r)
        kd_l = sb("kd_l", [P, GT, P], f32r)
        kt_h = sb("kt_h", [P, 2 * SEQ], f32r)
        kt_l = sb("kt_l", [P, 2 * SEQ], f32r)
        v_hl = sb("v_hl", [P, GT, P], f32r)
        q_hl = sb("q_hl", [P, 2, GT, P], f32r)
        qt_hl = sb("qt_hl", [P, 2, SEQ], f32r)
        prob = sb("prob", [P, 2, SEQ])
        pt_h = sb("pt_h", [P, 2, GT, QB], f32r)
        pt_l = sb("pt_l", [P, 2, GT, QB], f32r)
        o_hl = sb("o_hl", [P, 2, QB])
        at_tok = sb("at_tok", [P, GT, 2 * HD])
        nmax = sb("nmax", [P, 2])
        rsum = sb("rsum", [P, 2 * GT])
        rinv = sb("rinv", [P, 2 * GT])
        ident_r = sb("ident_r", [P, P], f32r)
        ident2 = sb("ident2", [P, HD])
        upad = sb("upad", [P, SEQ + 2 * PAD])
        win_a = sb("win_a", [P, SEQ + 2 * PAD])
        win_b = sb("win_b", [P, SEQ + 2 * PAD])
        edge_t = sb("edge_t", [P, NW, 2, PAD])
        wp_sb = sb("wp_sb", [P, NW, P])
        psc = sb("psc", [P, NW])
        ps_s = [pb(f"ps_s{i}", [P, SEQ]) for i in range(2)]
        ps_t = [pb(f"ps_t{i}", [P, 4, P]) for i in range(2)]
        ps_pv = pb("ps_pv", [P, 512])
        ps_m = pb("ps_m", [P, 4, P])
        sB.close()

        sc = ExitStack()
        sb, pb = alloc(sc), palloc(sc)
        KM = w_out.shape[0] // P
        wo_h = sb("wo_h", [P, KM, D], f32r)
        wo_l = sb("wo_l", [P, KM, D], f32r)
        wo_raw = sb("wo_raw", [P, 2, D])
        wr_sb = sb("wr_sb", [P, KD, E])
        mx_h = sb("mx_h", [P, 2, KM, P], f32r)
        mx_l = sb("mx_l", [P, 2, KM, P], f32r)
        res = sb("res", [P, 2, D])
        hid = sb("hid", [P, 2, D])
        acc = sb("acc", [P, 2, D])
        ht = sb("ht", [P, KD, P])
        ps_o = [pb(f"ps_o{i}", [P, D]) for i in range(2)]
        ps_ht = pb("ps_ht", [P, KD, P])
        ps_l = pb("ps_l", [P, 512])
        sc.close()
        keep.close()
        c_const = sem("c_const")
        wo_in = [sem(f"wo_in{i}") for i in range(2)]
        wo_hi, wo_lo = sem("wo_hi"), sem("wo_lo")
        res_in = [sem(f"res_in{i}") for i in range(2)]
        mx_hi, mx_lo, o_done = sem("mx_hi"), sem("mx_lo"), sem("o_done")
        r_ready, c_var, c_sd, h_ready = sem("r_ready"), sem("c_var"), sem("c_sd"), sem("h_ready")
        h_st = [sem(f"h_st{i}") for i in range(2)]
        acc_st = [sem(f"acc_st{i}") for i in range(2)]
        acc_ready, ht_done, ht_ready, l_done, l_ready = (sem("acc_ready"), sem("ht_done"), sem("ht_ready"),
                                                         sem("l_done"), sem("l_ready"))

        se = ExitStack()
        sb, pb = alloc(se), palloc(se)
        RING = 4
        CHUNK = KD * 2 * P
        w_raw = sb("w_raw", [P, RING, CHUNK])
        w_h = sb("w_h", [P, RING, CHUNK], f32r)
        w_l = sb("w_l", [P, RING, CHUNK], f32r)
        C2 = GROUPS * CAP
        hh = sb("hh", [P, KF, C2], f32r)
        hl = sb("hl", [P, KF, C2], f32r)
        x_h = sb("x_h", [P, KD, C2], f32r)
        x_l = sb("x_l", [P, KD, C2], f32r)
        xg = sb("xg", [P, GROUPS, D])
        ysb = sb("ysb", [P, GROUPS, D])
        sg = sb("sg", [P, 2, C2])
        hf = sb("hf", [P, 2, C2])
        lmax = sb("lmax", [P, TILES])
        lsum = sb("lsum", [P, TILES])
        GOFF = 32
        ROWS = GOFF + E
        aff = sb("aff", [ROWS, SEQ])
        top_v = sb("top_v", [ROWS, CAP])
        top_i = sb("top_i", [ROWS, CAP], u32)
        top_f = sb("top_f", [ROWS, CAP])
        gate_w8 = sb("gate_w8", [P, ROWS])
        idx_t = sb("idx_t", [P, ROWS], u32)
        idx_g = sb("idx_g", [P, GROUPS], u32)
        no_shift = sb("no_shift", [P, GROUPS], u32)
        idx_e = sb("idx_e", [P, GROUPS], u32)
        idx_s = sb("idx_s", [P, GROUPS], u32)
        ps_gu = [pb(f"ps_gu{i}", [P, 2, C2]) for i in range(3)]
        ps_y = [pb(f"ps_y{i}", [P, D]) for i in range(GROUPS)]
        ps_x = pb("ps_x", [P, 4, P])
        se.close()
        w_dma = [sem(f"w_dma{i}") for i in range(RING)]
        w_hi, w_lo = sem("w_hi"), sem("w_lo")
        d_step, d_exp, d_aff, d_vt = sem("d_step"), sem("d_exp"), sem("d_aff"), sem("d_vt")
        top_ready = sem("top_ready")
        x_in_g = [sem(f"x_in_g{g}") for g in range(GROUPS)]
        idx_ready = sem("idx_ready")
        xt_d, x_hi, x_lo = sem("xt_d"), sem("x_hi"), sem("x_lo")
        gu_done, silu_done, h_split = sem("gu_done"), sem("silu_done"), sem("h_split")
        dn_done, y_ready = sem("dn_done"), sem("y_ready")
        scat = [sem(f"scat{g}") for g in range(GROUPS)]

        sf = ExitStack()
        sb = alloc(sf)
        FR = 4
        y_raw = sb("y_raw", [P, FR, D])
        y_out = sb("y_out", [P, FR, D])
        fst = sb("fst", [P, FR, 2, 6])
        fmv = sb("fmv", [P, FR, 2])
        fsd = sb("fsd", [P, FR, 1])
        frs = sb("frs", [P, FR, 1])
        sf.close()
        f_const = sem("f_const")
        y_in = [sem(f"y_in{i}") for i in range(FR)]
        f_var, f_sd, f_ready = sem("f_var"), sem("f_sd"), sem("f_ready")
        y_st = [sem(f"y_st{i}") for i in range(FR)]

        NCHUNK = 2 * KF // 2 + KF // 2
        NUP = KF

        def used(e, c):
            if c < NUP:
                return gu_done, KF * e + 2 * (c // 2) + 2
            return dn_done, (KF // 2) * e + (c - NUP) + 1

        stage_over = sem("stage_over")
        ident_ready = sem("ident_ready")
        b_const, q_in, k_in, v_in = sem("b_const"), sem("q_in"), sem("k_in"), sem("v_in")
        k_hi, k_split, v_hi, v_split = sem("k_hi"), sem("k_split"), sem("v_hi"), sem("v_split")
        q_split = sem("q_split")
        s_done, max_ready, exp_ready, t_done = sem("s_done"), sem("max_ready"), sem("exp_ready"), sem("t_done")
        pt_hi, pt_lo, pv_done, o_ready = sem("pt_hi"), sem("pt_lo"), sem("pv_done"), sem("o_ready")
        m_full, m_free = sem("m_full"), sem("m_free")
        u_in, m_ready, pm_done, pl_ready = sem("u_in"), sem("m_ready"), sem("pm_done"), sem("pl_ready")
        pool_self = sem("pool_self")

        def stage_end(eng, n):
            eng.drain().then_inc(stage_over, 1)
            eng.wait_ge(stage_over, 5 * n)

        NSTEP = QH * GT
        k_turn_at = {6: (0, 0), 8: (0, 1), 22: (1, 0), 24: (1, 1)}
        q_turn_at = {3: 0, 5: 1}

        def before_step(t, last):
            found = []
            if t in k_turn_at and not last:
                found.append(("K", *k_turn_at[t]))
            if t < NSTEP and t % GT in q_turn_at and not (last and t // GT + 1 == QH):
                found.append(("Q", (t // GT + 1) % QH, q_turn_at[t % GT]))
            return found

        def after_step(t, start):
            pv = t // 2 - 1 if t % 2 == 0 else None
            add = (t - 3) // 2 if t % 2 == 1 else None
            back = (t - 4) // 2 if t % 2 == 0 else None
            if back is not None and (back // (NQB // QH)) % 2 == 0:
                back = None
            return tuple(None if b is not None and (b < 0 and start or b >= NQB) else b for b in (pv, add, back))

        def turns_of(last):
            found = []
            for t in range(NSTEP + (3 if last else 0)):
                found += before_step(t, last)
                _, add, back = after_step(t, False)
                found += [("add", add)] if add is not None else []
                found += [("back", back)] if back is not None else []
            return {what: n for n, what in enumerate(found)}

        turn_mid, turn_last = turns_of(False), turns_of(True)
        TURNS = len(turn_mid)
        first_turns = [("K", 0, 0), ("K", 0, 1), ("K", 1, 0), ("K", 1, 1), ("Q", 0, 0), ("Q", 0, 1)]
        TURN0 = len(first_turns) - 3

        def turn_no(s, last, what):
            return TURNS * s + TURN0 + (turn_last if last else turn_mid)[what]

        def q_turn(s, first, last, h):
            if h == 0:
                return len(first_turns) - 1 if first else turn_no(s - 1, False, ("Q", 0, 1))
            return turn_no(s, last, ("Q", h, 1))

        const_in = sem("const_in")
        x_in = [sem(f"x_in{i}") for i in range(2)]
        win_in = [sem(f"win_in{i}") for i in range(RAW)]
        win_hi, win_lo = sem("win_hi"), sem("win_lo")
        var_ready, sd_ready, xln_ready = sem("var_ready"), sem("sd_ready"), sem("xln_ready")
        xln_st = [sem(f"xln_st{i}") for i in range(2)]
        xt_done, xt_hi, xt_lo = sem("xt_done"), sem("xt_hi"), sem("xt_lo")
        q_done, kv_done, u_done = sem("q_done"), sem("kv_done"), sem("u_done")
        ss_ready, rms_sd = sem("ss_ready"), sem("rms_sd")
        qn_ready, v_ready, roped = sem("qn_ready"), sem("v_ready"), sem("roped")
        u_ready = sem("u_ready")
        q_st = [sem(f"q_st{i}") for i in range(2)]
        k_st = [sem(f"k_st{i}") for i in range(2)]
        v_st = [sem(f"v_st{i}") for i in range(2)]
        u_st = [sem(f"u_st{i}") for i in range(2)]
        eps_set = sem("eps_set")
        stage_a_read = sem("stage_a_read")

        block = ctx.enter_context(nc.Block())

        @block.sync
        def _(sp):
            sp.dma_start(xin[:, 0, :], x[0:P, :]).then_inc(x_in[0], 16)
            sp.dma_start(xin[:, 1, :], x[P:2 * P, :]).then_inc(x_in[1], 16)
            for dst, src in ((ident[:, :], eye), (gain_b[:, 0, :], ln_in_g), (gain_b[:, 1, :], ln_in_b),
                             (cos_t[:, :, :], rope_cos.rearrange("(t p) c -> p t c", p=P)),
                             (sin_t[:, :, :], rope_sin.rearrange("(t p) c -> p t c", p=P)),
                             (qkg[:, :], qk_gain)):
                sp.dma_start(dst, src).then_inc(const_in, 16)
            for k in range(KD):
                if k >= RAW:
                    sp.wait_ge(win_lo, k - RAW + 1)
                sp.dma_start(win_raw[:, k % RAW, :], w_in[k * P:(k + 1) * P, :]).then_inc(win_in[k % RAW], 16)

            q_t = q_d.rearrange("(v t) c -> v t c", v=KVH)
            k_t = k_d.rearrange("(v t) c -> v t c", v=KVH)
            v_t = v_d.rearrange("(v t) c -> v t c", v=KVH)

            def stage_a(b, first, last_b):
                for hf in range(2):
                    j = 2 * b + hf
                    rows = [bass.ds(at(sp, j * (2 * P) + k * P), P) for k in range(4)] if not (last_b and hf == 1) else \
                        [bass.ds(j * (2 * P) + k * P, P) for k in range(2)]
                    for tt in range(2):
                        sp.wait_ge(xln_ready, 2 * j + tt + 1)
                        sp.dma_start(xln_d[rows[tt], :], xln[:, tt, :]).then_inc(xln_st[tt], 16)
                        if not (last_b and hf == 1):
                            sp.dma_start(xin[:, tt, :], x[rows[2 + tt], :]).then_inc(x_in[tt], 16)
                    for tt in range(2):
                        sp.wait_ge(v_ready, 2 * j + tt + 1)
                        sp.wait_ge(roped, 2 * j + tt + 1)
                        sp.dma_start(q_t[:, rows[tt], :].rearrange("v p c -> p v c"),
                                     qkv[:, tt, :, 0:KVC - 2 * HD]).then_inc(q_st[tt], 16)
                        sp.dma_start(k_t[:, rows[tt], :].rearrange("v p c -> p v c"),
                                     qkv[:, tt, :, KVC - 2 * HD:KVC - HD]).then_inc(k_st[tt], 16)
                        sp.dma_start(v_t[:, rows[tt], :].rearrange("v p c -> p v c"),
                                     qkv[:, tt, :, KVC - HD:KVC]).then_inc(v_st[tt], 16)

            steps(sp, PAIRS // 2, stage_a)
            for tt in range(2):
                sp.wait_ge(xln_st[tt], 16 * PAIRS)
                sp.wait_ge(q_st[tt], 16 * PAIRS)
                sp.wait_ge(k_st[tt], 16 * PAIRS)
                sp.wait_ge(v_st[tt], 16 * PAIRS)
                sp.wait_ge(u_st[tt], 8 * PAIRS)

            stage_end(sp, 1)
            for dst, src in ((ident2[0:HD, :], eye[0:HD, 0:HD]), (ident2[HD:P, :], eye[0:HD, 0:HD]),
                             (edge_t[:, :, :, :], pool_edge.rearrange("p (w s n) -> p w s n", w=NW, s=2)),
                             (wp_sb[:, :, :], w_pool.rearrange("w c d -> c w d")),
                             (psc[:, :], pool_scale)):
                sp.dma_start(dst, src).then_inc(b_const, 16)

            def load_k(s, first):
                rows = bass.ds(at(sp, s * SEQ), SEQ)
                if not first:
                    sp.wait_ge(k_split, 2 * s)
                sp.dma_start(k_raw[:, :, :], k_d[rows, :].rearrange("(t p) c -> p t c", p=P)).then_inc(k_in, 16)

            def load_v(s, first):
                rows = bass.ds(at(sp, s * SEQ), SEQ)
                if not first:
                    sp.wait_ge(v_split, s)
                sp.dma_start(v_raw[:, :, :], v_d[rows, :].rearrange("(t p) c -> p t c", p=P)).then_inc(v_in, 16)

            def load_q(s, first):
                rows = bass.ds(at(sp, s * SEQ), SEQ)
                if not first:
                    sp.wait_ge(q_split, QH * s)
                sp.dma_start(q_raw[:, :, :], q_d[rows, :].rearrange("(t p) c -> p t c", p=P)).then_inc(q_in, 16)

            load_k(0, True)
            load_q(0, True)
            load_v(0, True)

            def stage_b(s, first, last_s):
                if not last_s:
                    load_k(s + 1, False)
                    load_v(s + 1, False)
                    load_q(s + 1, False)

            steps(sp, SLOTS, stage_b)
            stage_end(sp, 2)

            for dst, src in ((wr_sb[:, :, :], w_router.rearrange("(k p) e -> p k e", p=P)),
                             (gain_b[:, 0, :], ln1_g), (gain_b[:, 1, :], ln1_b)):
                sp.dma_start(dst, src).then_inc(c_const, 16)
            for k in range(KM):
                if k >= 2:
                    sp.wait_ge(wo_lo, k - 1)
                sp.dma_start(wo_raw[:, k % 2, :], w_out[k * P:(k + 1) * P, :]).then_inc(wo_in[k % 2], 16)
                if k < 2:
                    sp.dma_start(res[:, k, :], xln_d[k * P:(k + 1) * P, :]).then_inc(res_in[k], 16)

            def stage_c(b, first, last_b):
                rows = [bass.ds(at(sp, (2 * b + k) * P), P) for k in range(2 if last_b else 4)]
                for sl in range(2):
                    i = 2 * b + sl
                    if not last_b:
                        sp.wait_ge(r_ready, 2 * i + 2)
                        sp.dma_start(res[:, sl, :], xln_d[rows[2 + sl], :]).then_inc(res_in[sl], 16)
                    sp.wait_ge(h_ready, i + 1)
                    sp.dma_start(h_d[rows[sl], :], hid[:, sl, :]).then_inc(h_st[sl], 16)
                    sp.wait_ge(acc_ready, i + 1)
                    sp.dma_start(acc_d[rows[sl], :], acc[:, sl, :]).then_inc(acc_st[sl], 16)

            steps(sp, TILES // 2, stage_c)
            for sl in range(2):
                sp.wait_ge(h_st[sl], 8 * TILES)
                sp.wait_ge(acc_st[sl], 8 * TILES)
            stage_end(sp, 3)

            def stage_e(e, first, last_e):
                ex = bass.ds(e, 1)
                for c in range(NCHUNK):
                    if not (first and c < RING):
                        sp.wait_ge(w_lo, NCHUNK * e + c - RING + 1)
                    dst = w_raw[:, c % RING, :]
                    if c < NUP:
                        w = (w_gate, w_up)[c % 2]
                        src = w[ex, :, (c // 2) * 2 * P:(c // 2 + 1) * 2 * P].rearrange("o (k p) f -> p (o k) f", p=P)
                        dst = dst.rearrange("p (k f) -> p k f", k=KD)
                    else:
                        m = c - NUP
                        src = w_down[ex, m * 2 * P:(m + 1) * 2 * P, :].rearrange("o (k p) d -> p (o k) d", p=P)
                        dst = dst.rearrange("p (k d) -> p k d", k=2)
                    sp.dma_start(dst, src).then_inc(w_dma[c % RING], 16)

            steps(sp, E, stage_e)
            stage_end(sp, 4)

            for dst, src in ((gain_b[:, 0, :], ln2_g), (gain_b[:, 1, :], ln2_b)):
                sp.dma_start(dst, src).then_inc(f_const, 16)
            for i in range(FR):
                sp.dma_start(y_raw[:, i, :], acc_d[i * P:(i + 1) * P, :]).then_inc(y_in[i], 16)

            def stage_f(b, first, last_b):
                rows = [bass.ds(at(sp, (FR * b + k) * P), P) for k in range(FR if last_b else 2 * FR)]
                for k in range(FR):
                    sp.wait_ge(f_ready, FR * b + k + 1)
                    sp.dma_start(out[rows[k], :], y_out[:, k, :]).then_inc(y_st[k], 16)
                    if not last_b:
                        sp.dma_start(y_raw[:, k, :], acc_d[rows[FR + k], :]).then_inc(y_in[k], 16)

            steps(sp, TILES // FR, stage_f)
            for k in range(FR):
                sp.wait_ge(y_st[k], 16 * TILES // FR)

        @block.tensor
        def _(pe):
            def stage_a(b, first, last_b):
                for hf in range(2):
                    j = 2 * b + hf
                    start = first and hf == 0
                    for tt in range(2):
                        i = 2 * j + tt
                        pe.wait_ge(xln_ready, i + 1)
                        if start and tt == 0:
                            pe.wait_ge(const_in, 96)
                        if not start:
                            pe.wait_ge(xt_hi, i - 1)
                            pe.wait_ge(xt_lo, i - 1)
                        for k in range(KD):
                            last = nc.tensor.transpose(ps_xt[tt][:, k, :], xln[:, tt, k * P:(k + 1) * P], ident[:, :])
                        last.then_inc(xt_done, 1)
                    for tt in range(2):
                        i = 2 * j + tt
                        pe.wait_ge(xt_hi, i + 1)
                        pe.wait_ge(xt_lo, i + 1)
                        for ps, c0, c1, done in ((ps_q, 0, AW, q_done), (ps_kv, AW, QKVW, kv_done)):
                            if not (start and tt == 0):
                                pe.wait_ge(qn_ready, i)
                                pe.wait_ge(v_ready, i)
                            for k in range(KD):
                                if start and tt == 0 and c0 == 0:
                                    pe.wait_ge(win_hi, k + 1)
                                    pe.wait_ge(win_lo, k + 1)
                                t = slice(tt * P, (tt + 1) * P)
                                for n, (a, w) in enumerate(((xt_h, win_h), (xt_h, win_l), (xt_l, win_h))):
                                    last = nc.tensor.matmul(ps[:, 0:c1 - c0], a[:, hf, k, t], w[:, k, c0:c1],
                                                            start=k == 0 and n == 0, stop=k == KD - 1 and n == 2)
                            last.then_inc(done, 1)
                    for cp in range(2):
                        if not start:
                            pe.wait_ge(u_ready, 2 * j - 1 + cp)
                        for c in range(2):
                            c0 = QKVW + (2 * cp + c) * P
                            for k in range(KD):
                                for n, (w, a) in enumerate(((win_h, xt_h), (win_h, xt_l), (win_l, xt_h))):
                                    last = nc.tensor.matmul(ps_u[cp][:, c, :], w[:, k, c0:c0 + P], a[:, hf, k, :],
                                                            start=k == 0 and n == 0, stop=k == KD - 1 and n == 2)
                        last.then_inc(u_done, 1)

            steps(pe, PAIRS // 2, stage_a)

            stage_end(pe, 1)
            pe.wait_ge(b_const, 80)
            pe.wait_ge(ident_ready, 1)

            def through_m(number, what, s):
                if what[0] == "K":
                    _, lo, r = what
                    src = (kd_h, kd_l)[lo]
                    pe.wait_ge(k_split, 2 * s + 2)
                else:
                    _, h, r = what
                    src = q_hl[:, h % 2, :, :]
                    pe.wait_ge(q_split, QH * s + h + 1)
                if not isinstance(number, int) or number > 0:
                    pe.wait_ge(m_free, number)
                for c in range(4):
                    last = nc.tensor.transpose(ps_m[:, c, :].bitcast(f32r), src[:, 4 * r + c, :], ident_r[:, :])
                last.then_inc(m_full, 1)

            def scores(s, t, kt_at, early, q_number):
                h = t // GT
                keys = [bass.ds(at(pe, kt_at + c * 512), 512) for c in range(SEQ // 512)]
                if t % GT == 0:
                    pe.wait_ge(m_free, q_number + 1)
                if not early:
                    pe.wait_ge(exp_ready, NSTEP * s + t - 1)
                q = qt_hl[:, h % 2, (t % GT) * P:(t % GT + 1) * P]
                for c in range(SEQ // 512):
                    cols = slice(c * 512, (c + 1) * 512)
                    nc.tensor.matmul(ps_s[t % 2][:, cols], q, kt_h[:, keys[c]], start=True, stop=False)
                    last = nc.tensor.matmul(ps_s[t % 2][:, cols], q, kt_l[:, keys[c]], start=False, stop=True)
                last.then_inc(s_done, 1)

            for n, what in enumerate(first_turns):
                through_m(n, what, 0)
            scores(0, 0, 0, True, q_turn(0, True, False, 0))
            scores(0, 1, 0, True, None)

            def stage_b(s, first, last_s):
                here = at(pe, (s % 2) * SEQ)
                there = at(pe, ((s + 1) % 2) * SEQ)

                def m_turn(what):
                    pe.wait_ge(m_free, turn_no(s, last_s, what))

                def transposes(t):
                    pe.wait_ge(exp_ready, NSTEP * s + t + 1)
                    for r in range(2):
                        if not (first and t == 0):
                            pe.wait_ge(pt_lo, 2 * (NSTEP * s + t) + r - 1)
                        for c in range(4):
                            k = 4 * r + c
                            last = nc.tensor.transpose(ps_t[r][:, c, :], prob[:, t % 2, k * P:(k + 1) * P], ident[:, :])
                        last.then_inc(t_done, 1)

                def values(b):
                    pe.wait_ge(pt_lo, 2 * (NSTEP * s + 2 * b + 2))
                    if b == 0:
                        pe.wait_ge(v_split, s + 1)
                    if not (first and b == 0):
                        pe.wait_ge(o_ready, NQB * s + b)
                    for k in range(GT):
                        for n, pt in enumerate((pt_h, pt_l)):
                            last = nc.tensor.matmul(ps_pv[:, 0:QB], v_hl[:, k, :], pt[:, b % 2, k, :],
                                                    start=k == 0 and n == 0, stop=k == GT - 1 and n == 1)
                    last.then_inc(pv_done, 1)

                def add_halves(b):
                    pe.wait_ge(o_ready, NQB * s + b + 1)
                    m_turn(("add", b))
                    for c in range(2):
                        last = nc.tensor.matmul(ps_m[:, c, 0:HD], o_hl[:, b % 2, c * P:(c + 1) * P], ident2[:, :],
                                                start=True, stop=True)
                    last.then_inc(m_full, 1)

                def back(b):
                    m_turn(("back", b))
                    for c in range(2):
                        i = (2 * b + c) % GT
                        last = nc.tensor.transpose(ps_m[:, c, :], at_tok[:, i, :], ident[:, :])
                    last.then_inc(m_full, 1)

                for t in range(NSTEP + (3 if last_s else 0)):
                    if t < NSTEP:
                        if t + 2 < NSTEP:
                            scores(s, t + 2, here, False, q_turn(s, first, last_s, (t + 2) // GT))
                        elif not last_s:
                            scores(s + 1, t + 2 - NSTEP, there, False, q_turn(s + 1, False, None, 0))
                        for what in before_step(t, last_s):
                            ahead = what[0] == "K" or what[1] == 0
                            through_m(turn_no(s, last_s, what), what, s + 1 if ahead else s)
                        transposes(t)
                    pv, add, bk = after_step(t, first)
                    if pv is not None:
                        values(pv)
                    if add is not None:
                        add_halves(add)
                    if bk is not None:
                        back(bk)

            steps(pe, SLOTS, stage_b)

            for n in range(GROUPS * NW):
                g, w = divmod(n, NW)
                pe.wait_ge(m_ready, n + 1)
                if n >= 2:
                    pe.wait_ge(pl_ready, n - 1)
                for c in range(SEQ // 512):
                    last = nc.tensor.matmul(ps_s[n % 2][:, c * 512:(c + 1) * 512], wp_sb[:, w, :],
                                            mix_pl[:, w, g * SEQ + c * 512:g * SEQ + (c + 1) * 512], start=True, stop=True)
                last.then_inc(pm_done, 1)
            stage_end(pe, 2)

            pe.wait_ge(c_const, 48)

            def out_proj(i, sl, c, start, first_tile):
                if c == 0:
                    pe.wait_ge(mx_lo, i + 1)
                if not start:
                    pe.wait_ge(r_ready, 2 * i - 3 + c)
                for k in range(KM):
                    if first_tile and c == 0:
                        pe.wait_ge(wo_lo, k + 1)
                    cols = slice(c * 512, (c + 1) * 512)
                    for n, (a, w) in enumerate(((mx_h, wo_h), (mx_h, wo_l), (mx_l, wo_h))):
                        last = nc.tensor.matmul(ps_o[sl][:, cols], a[:, sl, k, :], w[:, k, cols],
                                                start=k == 0 and n == 0, stop=k == KM - 1 and n == 2)
                last.then_inc(o_done, 1)

            def h_transposes(i, sl, start):
                pe.wait_ge(h_ready, i + 1)
                if not start:
                    pe.wait_ge(ht_ready, i)
                for k in range(KD):
                    last = nc.tensor.transpose(ps_ht[:, k, :], hid[:, sl, k * P:(k + 1) * P], ident[:, :])
                last.then_inc(ht_done, 1)

            def router(i, start):
                pe.wait_ge(ht_ready, i + 1)
                if not start:
                    pe.wait_ge(l_ready, i)
                for k in range(KD):
                    last = nc.tensor.matmul(ps_l[:, 0:E], ht[:, k, :], wr_sb[:, k, :], start=k == 0, stop=k == KD - 1)
                last.then_inc(l_done, 1)

            def stage_c(b, first):
                for sl in range(2):
                    i = 2 * b + sl
                    out_proj(i, sl, 0, first, first and sl == 0)
                    if not first:
                        router(i - 2, first)
                    out_proj(i, sl, 1, first, first and sl == 0)
                    if not (first and sl == 0):
                        h_transposes(i - 1, 1 - sl, first)

            stage_c(0, True)
            for sl in range(2):
                out_proj(2 + sl, sl, 0, False, False)
                router(sl, sl == 0)
                out_proj(2 + sl, sl, 1, False, False)
                h_transposes(1 + sl, 1 - sl, False)
            with pe.Fori(2, TILES // 2) as b:
                stage_c(b, False)
            router(TILES - 2, False)
            h_transposes(TILES - 1, 1, False)
            router(TILES - 1, False)
            stage_end(pe, 3)

            pe.wait_ge(d_aff, 1)
            for t in range(TILES):
                last = nc.tensor.transpose(ps_y[t // GT][0:E, (t % GT) * P:(t % GT + 1) * P], logits[:, t, :], ident[:, :])
            last.then_inc(d_step, 1)
            pe.wait_ge(top_ready, 1)
            nc.tensor.transpose(ps_x[:, 0, 0:ROWS], top_v[:, :], ident[0:ROWS, 0:ROWS])
            nc.tensor.transpose(ps_x[:, 1, 0:ROWS], top_f[:, :], ident[0:ROWS, 0:ROWS]).then_inc(d_step, 1)
            pe.wait_ge(top_ready, 2)

            XR = GROUPS * KD // 4

            def x_round(e, n, start):
                g, r = divmod(n, KD // 4)
                pe.wait_ge(x_in_g[g], 16 * (e + 1))
                if not start:
                    pe.wait_ge(x_lo, XR * e + n)
                for c in range(4):
                    k = 4 * r + c
                    last = nc.tensor.transpose(ps_x[:, c, :], xg[:, g, k * P:(k + 1) * P], ident[:, :])
                last.then_inc(xt_d, 1)

            for n in range(XR):
                x_round(0, n, n == 0)

            def stage_e(e, first, last_e):
                pe.wait_ge(x_lo, XR * (e + 1))
                for n in range(KF):
                    if n % 2 == 0:
                        pe.wait_ge(w_lo, NCHUNK * e + n + 2)
                    if not (first and n < 3):
                        pe.wait_ge(h_split, KF * e + n - 2)
                    for u in range(2):
                        c = (n // 2) * 2 + u
                        wh = w_h[:, c % RING, :].rearrange("p (k f) -> p k f", k=KD)
                        wl = w_l[:, c % RING, :].rearrange("p (k f) -> p k f", k=KD)
                        cols = slice((n % 2) * P, (n % 2 + 1) * P)
                        for k in range(KD):
                            for q, (w, a) in enumerate(((wh, x_h), (wh, x_l), (wl, x_h))):
                                last = nc.tensor.matmul(ps_gu[n % 3][:, u, :], w[:, k, cols], a[:, k, :],
                                                        start=k == 0 and q == 0, stop=k == KD - 1 and q == 2)
                    last.then_inc(gu_done, 1)
                for m in range(KF // 2):
                    c = NUP + m
                    pe.wait_ge(w_lo, NCHUNK * e + c + 1)
                    pe.wait_ge(h_split, KF * e + 2 * m + 2)
                    if m == 0 and not first:
                        pe.wait_ge(y_ready, GROUPS * e)
                    for kk in range(2):
                        k = 2 * m + kk
                        for g in range(GROUPS):
                            tok = slice(g * CAP, (g + 1) * CAP)
                            for q, (a, w) in enumerate(((hh, w_h), (hh, w_l), (hl, w_h))):
                                for c2 in range(D // 512):
                                    last = nc.tensor.matmul(
                                        ps_y[g][:, c2 * 512:(c2 + 1) * 512], a[:, k, tok],
                                        w[:, c % RING, kk * D + c2 * 512:kk * D + (c2 + 1) * 512],
                                        start=k == 0 and q == 0, stop=k == KF - 1 and q == 2)
                    last.then_inc(dn_done, 1)
                    if 2 <= m < 2 + XR and not last_e:
                        x_round(e + 1, m - 2, False)

            steps(pe, E, stage_e)
            stage_end(pe, 4)

        @block.scalar
        def _(act):
            act.wait_ge(eps_set, 1)

            def ln_in_sd(j):
                for tt in range(2):
                    act.wait_ge(var_ready, 2 * j + tt + 1)
                    nc.scalar.activation(sd[:, tt, :], mv[:, tt, 1:2], ACT.Sqrt, bias=eps[:, 0:1]).then_inc(sd_ready, 1)

            def stage_a(b, first, last_b):
                for hf in range(2):
                    j = 2 * b + hf
                    start = first and hf == 0
                    for tt in range(2):
                        i = 2 * j + tt
                        act.wait_ge(xt_done, i + 1)
                        if not first:
                            act.wait_ge(u_done, 2 * j - 2)
                        nc.scalar.activation(xt_h[:, hf, :, tt * P:(tt + 1) * P], ps_xt[tt][:, :, :], ACT.Copy).then_inc(xt_hi, 1)
                    for tt in range(2):
                        i = 2 * j + tt
                        act.wait_ge(q_done, i + 1)
                        if not (start and tt == 0):
                            act.wait_ge(ss_ready, i)
                        nc.scalar.activation(sq[:, 0:AW], ps_q[:, :], ACT.Square)
                        act.wait_ge(kv_done, i + 1)
                        nc.scalar.activation(sq[:, AW:QKW], ps_kv[:, 0:KVW], ACT.Square)
                        if not start:
                            act.wait_ge(v_st[tt], 16 * j)
                        nc.scalar.activation(qkv[:, tt, :, KVC - HD:KVC],
                                             ps_kv[:, KVW:2 * KVW].rearrange("p (v c) -> p v c", c=HD), ACT.Copy).then_inc(v_ready, 1)
                        act.wait_ge(ss_ready, i + 1)
                        nc.scalar.activation(rn[:, tt, 0:HEADS + KVH], ss[:, tt, 0:HEADS + KVH], ACT.Sqrt,
                                             bias=eps[:, 1:2], scale=1.0 / HD).then_inc(rms_sd, 1)
                    if not (last_b and hf == 1):
                        ln_in_sd(j + 1)
                    row = at(act, j * (2 * P))
                    for cp in range(2):
                        act.wait_ge(u_done, 2 * j + cp + 1)
                        if not first:
                            act.wait_ge(u_st[hf], 16 * b)
                        nc.scalar.activation(ust[:, hf, 2 * cp:2 * cp + 2, :], ps_u[cp][:, :, :], ACT.Copy).then_inc(u_ready, 1)
                    act.wait_ge(u_ready, 2 * j + 2)
                    act.dma_start(ut_d[:, :, bass.ds(row, 2 * P)].rearrange("w p t -> p w t"),
                                  ust[:, hf, :, :]).then_inc(u_st[hf], 16)

            ln_in_sd(0)
            for k in range(KD):
                act.wait_ge(win_in[k % RAW], 16 * (k // RAW + 1))
                nc.scalar.activation(win_h[:, k, :], win_raw[:, k % RAW, :], ACT.Copy).then_inc(win_hi, 1)
            steps(act, PAIRS // 2, stage_a)

            stage_end(act, 1)
            nc.scalar.activation(ident_r[:, :], ident[:, :], ACT.Copy).then_inc(ident_ready, 1)

            def k_hi_copy(s):
                act.wait_ge(k_in, 16 * s + 16)
                for d in range(2):
                    last = nc.scalar.activation(kd_h[:, :, d * HD:(d + 1) * HD], k_raw[:, :, :], ACT.Copy)
                last.then_inc(k_hi, 1)

            def v_hi_copy(s, first):
                act.wait_ge(v_in, 16 * s + 16)
                if not first:
                    act.wait_ge(pv_done, NQB * s)
                nc.scalar.activation(v_hl[:, :, 0:HD], v_raw[:, :, :], ACT.Copy).then_inc(v_hi, 1)

            def from_m(number, what, kt_at):
                act.wait_ge(m_full, number + 1)
                src = ps_m[:, :, :].rearrange("p c t -> p (c t)")
                if what[0] == "K":
                    _, lo, r = what
                    nc.scalar.activation((kt_h, kt_l)[lo][:, bass.ds(kt_at + r * 512, 512)], src, ACT.Copy).then_inc(m_free, 1)
                else:
                    _, h, r = what
                    last = nc.scalar.activation(qt_hl[:, h % 2, r * 512:(r + 1) * 512], src, ACT.Copy, scale=HD ** -0.5)
                    last.then_inc(m_free, 1)

            def exp(s, t, early):
                act.wait_ge(max_ready, NSTEP * s + t + 1)
                if not early:
                    act.wait_ge(t_done, 2 * (NSTEP * s + t - 1))
                i = t % (2 * GT)
                nc.scalar.activation(prob[:, t % 2, :], ps_s[t % 2][:, :], ACT.Exp, bias=nmax[:, t % 2:t % 2 + 1],
                                     accum_out=rsum[:, i:i + 1]).then_inc(exp_ready, 1)

            k_hi_copy(0)
            for n, what in enumerate(first_turns):
                from_m(n, what, 0)
            v_hi_copy(0, True)
            exp(0, 0, True)
            exp(0, 1, True)

            def stage_b(s, first, last_s):
                def hi(t):
                    b = t // 2
                    for r in range(2):
                        act.wait_ge(t_done, 2 * (NSTEP * s + t) + r + 1)
                        if t % 2 == 0 and r == 0 and not (first and b < 2):
                            act.wait_ge(pv_done, NQB * s + b - 1)
                        nc.scalar.activation(pt_h[:, b % 2, 4 * r:4 * r + 4, (t % 2) * P:(t % 2 + 1) * P],
                                             ps_t[r][:, :, :], ACT.Copy).then_inc(pt_hi, 1)

                there = at(act, ((s + 1) % 2) * SEQ)
                col = at(act, s * SEQ + (s // 2) * (2 * SEQ))
                col_before = 0 if first else at(act, s * SEQ - SEQ + ((s - 1) // 2) * (2 * SEQ))
                mix = mix_at.rearrange("p v j t -> p (v j t)")
                for t in range(NSTEP + (3 if last_s else 0)):
                    if t < NSTEP:
                        for what in before_step(t, last_s):
                            from_m(turn_no(s, last_s, what), what, there)
                        hi(t)
                        if t + 2 < NSTEP:
                            exp(s, t + 2, False)
                        elif not last_s:
                            exp(s + 1, t + 2 - NSTEP, False)
                        if t == 3 and not last_s:
                            k_hi_copy(s + 1)
                    pv, add, bk = after_step(t, first)
                    if pv is not None:
                        act.wait_ge(pv_done, NQB * s + pv + 1)
                        nc.scalar.activation(o_hl[:, pv % 2, :], ps_pv[:, 0:QB], ACT.Copy).then_inc(o_ready, 1)
                        if pv == -1:
                            v_hi_copy(s, False)
                    if bk is not None:
                        act.wait_ge(m_full, turn_no(s, last_s, ("back", bk)) + 1)
                        pair, qb = divmod(bk % NQB, GT)
                        off = pair * TOK + (qb % (GT // 2)) * QB
                        nc.scalar.activation(mix[:, bass.ds((col if bk >= 0 else col_before) + off, QB)],
                                             ps_m[:, 0:2, :].rearrange("p c t -> p (c t)"), ACT.Copy).then_inc(m_free, 1)

            steps(act, SLOTS, stage_b)

            for n in range(GROUPS * NW):
                g, w = divmod(n, NW)
                act.wait_ge(pm_done, n + 1)
                act.wait_ge(b_const, 80)
                nc.scalar.activation(mix_pl[:, w, g * SEQ:(g + 1) * SEQ], ps_s[n % 2][:, :], ACT.Identity,
                                     scale=psc[:, w:w + 1]).then_inc(pl_ready, 1)
            stage_end(act, 2)

            def mix_hi(i, sl, start):
                if not start:
                    act.wait_ge(o_done, 2 * i - 2)
                cols = bass.ds(at(act, i * P), P)
                nc.scalar.activation(mx_h[:, sl, 0:NW, :], mix_at.rearrange("p v j t -> p (v j) t")[:, :, cols], ACT.Copy)
                nc.scalar.activation(mx_h[:, sl, NW:KM, :], mix_pl[:, :, cols], ACT.Copy).then_inc(mx_hi, 1)

            mix_hi(0, 0, True)
            for k in range(KM):
                act.wait_ge(wo_in[k % 2], 16 * (k // 2 + 1))
                nc.scalar.activation(wo_h[:, k, :], wo_raw[:, k % 2, :], ACT.Copy).then_inc(wo_hi, 1)

            def logit_copy(i):
                act.wait_ge(l_done, i + 1)
                nc.scalar.activation(logits[:, bass.ds(i, 1), :], ps_l[:, 0:E].unsqueeze(1), ACT.Copy).then_inc(l_ready, 1)

            def ht_copy(i, start):
                act.wait_ge(ht_done, i + 1)
                if not start:
                    act.wait_ge(l_done, i)
                nc.scalar.activation(ht[:, :, :], ps_ht[:, :, :], ACT.Copy).then_inc(ht_ready, 1)

            def stage_c(b, first, last_b):
                for sl in range(2):
                    i = 2 * b + sl
                    if not (last_b and sl == 1):
                        mix_hi(i + 1, 1 - sl, first and sl == 0)
                    if not first:
                        logit_copy(i - 2)
                    if not (first and sl == 0):
                        ht_copy(i - 1, first)
                    act.wait_ge(c_var, i + 1)
                    nc.scalar.activation(sd[:, sl, :], mv[:, sl, 1:2], ACT.Sqrt, bias=eps[:, 0:1]).then_inc(c_sd, 1)

            steps(act, TILES // 2, stage_c)
            logit_copy(TILES - 2)
            ht_copy(TILES - 1, False)
            logit_copy(TILES - 1)
            stage_end(act, 3)

            def w_hi_copy(e, c, start):
                act.wait_ge(w_dma[c % RING], 16 * ((NCHUNK // RING) * e + c // RING + 1))
                if not start:
                    act.wait_ge(*(used(e, c - RING) if c >= RING else used(e - 1, NCHUNK + c - RING)))
                nc.scalar.activation(w_h[:, c % RING, :], w_raw[:, c % RING, :], ACT.Copy).then_inc(w_hi, 1)

            act.wait_ge(d_exp, 1)
            nc.scalar.activation(logits[:, :, :], logits[:, :, :], ACT.Exp).then_inc(d_exp, 1)
            for c in range(RING):
                w_hi_copy(0, c, True)

            XR = GROUPS * KD // 4

            def x_hi_copy(e, n):
                g, r = divmod(n, KD // 4)
                act.wait_ge(xt_d, XR * e + n + 1)
                nc.scalar.activation(x_h[:, 4 * r:4 * r + 4, g * CAP:(g + 1) * CAP], ps_x[:, :, :], ACT.Copy).then_inc(x_hi, 1)

            for n in range(XR):
                x_hi_copy(0, n)

            def stage_e(e, first, last_e):
                for j in range(KF // 2):
                    for n in (2 * j, 2 * j + 1):
                        act.wait_ge(gu_done, KF * e + n + 1)
                        if not (first and n < 2):
                            act.wait_ge(h_split, KF * e + n - 1)
                        nc.scalar.activation(sg[:, n % 2, :], ps_gu[n % 3][:, 0, :], ACT.Silu).then_inc(silu_done, 1)
                    for c in (2 * j + RING, 2 * j + RING + 1):
                        w_hi_copy(e, c, False)
                for m in range(KF // 2):
                    if 2 <= m < 2 + XR and not last_e:
                        x_hi_copy(e + 1, m - 2)
                    c = NUP + m + RING
                    if c < NCHUNK:
                        w_hi_copy(e, c, False)
                    elif not last_e:
                        w_hi_copy(e + 1, c - NCHUNK, False)
                act.wait_ge(dn_done, (KF // 2) * (e + 1))
                for g in range(GROUPS):
                    if not first:
                        act.wait_ge(scat[g], 16 * e)
                    nc.scalar.activation(ysb[:, g, :], ps_y[g][:, :], ACT.Identity,
                                         scale=gate_w8[:, bass.ds(e + g * GOFF, 1)]).then_inc(y_ready, 1)

            steps(act, E, stage_e)
            stage_end(act, 4)

            def stage_f(b, first, last_b):
                for k in range(FR):
                    act.wait_ge(f_var, FR * b + k + 1)
                    nc.scalar.activation(fsd[:, k, :], fmv[:, k, 1:2], ACT.Sqrt, bias=eps[:, 0:1]).then_inc(f_sd, 1)

            steps(act, TILES // FR, stage_f)

        @block.vector
        def _(dve):
            nc.vector.memset(alpha[:, :], ALPHA)
            nc.vector.memset(eps[:, 0:1], LN_EPS)
            nc.vector.memset(eps[:, 1:2], RMS_EPS).then_inc(eps_set, 1)
            dve.wait_ge(const_in, 96)

            def split_w(k):
                dve.wait_ge(win_hi, k + 1)
                nc.vector.tensor_tensor(win_l[:, k, :], win_raw[:, k % RAW, :], win_h[:, k, :].bitcast(f32),
                                        ALU.subtract).then_inc(win_lo, 1)

            def ln_in_stats(j):
                for tt in range(2):
                    dve.wait_ge(x_in[tt], 16 * j + 16)
                    for c in range(2):
                        nc.vector.bn_stats(bst[:, tt, c, :], xin[:, tt, c * 512:(c + 1) * 512])
                    dve.drain()
                    nc.vector.bn_aggr(mv[:, tt, :], bst[:, tt, :, :]).then_inc(var_ready, 1)

            def ln_in_apply(j, start):
                for tt in range(2):
                    dve.wait_ge(sd_ready, 2 * j + tt + 1)
                    nc.vector.reciprocal(rs[:, tt, :], sd[:, tt, :])
                    if not start:
                        dve.wait_ge(xln_st[tt], 16 * j)
                        dve.wait_ge(xt_done, 2 * j + tt - 1)
                    nc.vector.scalar_tensor_tensor(xln[:, tt, :], xin[:, tt, :], mv[:, tt, 0:1], gain_b[:, 0, :],
                                                   ALU.subtract, ALU.mult)
                    dve.drain()
                    nc.vector.scalar_tensor_tensor(xln[:, tt, :], xln[:, tt, :], rs[:, tt, :], gain_b[:, 1, :],
                                                   ALU.mult, ALU.add).then_inc(xln_ready, 1)

            def stage_a(b, first, last_b):
                for hf in range(2):
                    j = 2 * b + hf
                    start = first and hf == 0
                    for tt in range(2):
                        i = 2 * j + tt
                        dve.wait_ge(xt_hi, i + 1)
                        nc.vector.tensor_tensor(xt_l[:, hf, :, tt * P:(tt + 1) * P], ps_xt[tt][:, :, :],
                                                xt_h[:, hf, :, tt * P:(tt + 1) * P].bitcast(f32), ALU.subtract).then_inc(xt_lo, 1)
                    for tt in range(2):
                        i = 2 * j + tt
                        H = HEADS + KVH
                        dve.wait_ge(v_ready, i + 1)
                        nc.vector.reduce_sum(ss[:, tt, 0:H], sq[:, :].rearrange("p (h c) -> p h c", c=HD), axis=AX.X).then_inc(ss_ready, 1)
                        dve.wait_ge(rms_sd, i + 1)
                        nc.vector.reciprocal(rn[:, tt, 0:H], rn[:, tt, 0:H])
                        dve.drain()
                        if not start:
                            dve.wait_ge(roped, i - 1)
                        nc.vector.tensor_tensor(qn[:, tt, 0:AW].rearrange("p (h c) -> p h c", c=HD),
                                                ps_q[:, :].rearrange("p (h c) -> p h c", c=HD),
                                                rn[:, tt, 0:HEADS].unsqueeze(2).to_broadcast([P, HEADS, HD]), ALU.mult)
                        nc.vector.tensor_tensor(qn[:, tt, AW:QKW].rearrange("p (h c) -> p h c", c=HD),
                                                ps_kv[:, 0:KVW].rearrange("p (h c) -> p h c", c=HD),
                                                rn[:, tt, HEADS:H].unsqueeze(2).to_broadcast([P, KVH, HD]),
                                                ALU.mult).then_inc(qn_ready, 1)
                    if not (last_b and hf == 1):
                        ln_in_stats(j + 1)
                        ln_in_apply(j + 1, False)

            ln_in_stats(0)
            ln_in_apply(0, True)
            for k in range(KD):
                split_w(k)
            steps(dve, PAIRS // 2, stage_a)

            stage_end(dve, 1)

            def k_lo_sub(s):
                dve.wait_ge(k_hi, s + 1)
                for d in range(2):
                    nc.vector.tensor_tensor(kd_l[:, :, d * HD:(d + 1) * HD], k_raw[:, :, :],
                                            kd_h[:, :, d * HD:(d + 1) * HD].bitcast(f32), ALU.subtract).then_inc(k_split, 1)

            def v_lo_sub(s):
                dve.wait_ge(v_hi, s + 1)
                nc.vector.tensor_tensor(v_hl[:, :, HD:2 * HD], v_raw[:, :, :], v_hl[:, :, 0:HD].bitcast(f32),
                                        ALU.subtract).then_inc(v_split, 1)

            def row_max(s, t):
                dve.wait_ge(s_done, NSTEP * s + t + 1)
                nc.vector.reduce_max(nmax[:, t % 2:t % 2 + 1], ps_s[t % 2][:, :], axis=AX.X,
                                     negate=True).then_inc(max_ready, 1)

            k_lo_sub(0)
            row_max(0, 0)
            row_max(0, 1)
            v_lo_sub(0)

            def stage_b(s, first, last_s):
                def lo(t):
                    b = t // 2
                    for r in range(2):
                        dve.wait_ge(pt_hi, 2 * (NSTEP * s + t) + r + 1)
                        cols = slice((t % 2) * P, (t % 2 + 1) * P)
                        nc.vector.tensor_tensor(pt_l[:, b % 2, 4 * r:4 * r + 4, cols], ps_t[r][:, :, :],
                                                pt_h[:, b % 2, 4 * r:4 * r + 4, cols].bitcast(f32), ALU.subtract).then_inc(pt_lo, 1)

                for t in range(NSTEP + (3 if last_s else 0)):
                    if t < NSTEP:
                        if t + 2 < NSTEP:
                            row_max(s, t + 2)
                        elif not last_s:
                            row_max(s + 1, t + 2 - NSTEP)
                        lo(t)
                        if t == 1 and not first:
                            v_lo_sub(s)
                        if t == 4 and not last_s:
                            k_lo_sub(s + 1)
                    _, add, _ = after_step(t, first)
                    if add is not None:
                        h, i = (add % NQB) // (GT // 2), (2 * add) % GT
                        j = (2 * add) % (2 * GT)
                        nc.vector.reciprocal(rinv[:, j:j + 2], rsum[:, j:j + 2])
                        dve.drain()
                        dve.wait_ge(m_full, turn_no(s, last_s, ("add", add)) + 1)
                        nc.vector.tensor_tensor(at_tok[:, i:i + 2, (h % 2) * HD:(h % 2 + 1) * HD], ps_m[:, 0:2, 0:HD],
                                                rinv[:, j:j + 2].unsqueeze(2).to_broadcast([P, 2, HD]),
                                                ALU.mult).then_inc(m_free, 1)

            steps(dve, SLOTS, stage_b)
            stage_end(dve, 2)

            def mix_lo(i, sl):
                cols = bass.ds(at(dve, i * P), P)
                dve.wait_ge(mx_hi, i + 1)
                nc.vector.tensor_tensor(mx_l[:, sl, 0:NW, :], mix_at.rearrange("p v j t -> p (v j) t")[:, :, cols],
                                        mx_h[:, sl, 0:NW, :].bitcast(f32), ALU.subtract)
                nc.vector.tensor_tensor(mx_l[:, sl, NW:KM, :], mix_pl[:, :, cols],
                                        mx_h[:, sl, NW:KM, :].bitcast(f32), ALU.subtract).then_inc(mx_lo, 1)

            mix_lo(0, 0)
            for k in range(KM):
                dve.wait_ge(wo_hi, k + 1)
                nc.vector.tensor_tensor(wo_l[:, k, :], wo_raw[:, k % 2, :], wo_h[:, k, :].bitcast(f32),
                                        ALU.subtract).then_inc(wo_lo, 1)
            dve.wait_ge(c_const, 48)

            def stage_c(b, first, last_b):
                for sl in range(2):
                    i = 2 * b + sl
                    if not (last_b and sl == 1):
                        mix_lo(i + 1, 1 - sl)
                    dve.wait_ge(res_in[sl], 16 * b + 16)
                    if not first:
                        dve.wait_ge(h_st[sl], 16 * b)
                        dve.wait_ge(ht_done, i - 1)
                        dve.wait_ge(acc_ready, i - 1)
                    for c in range(2):
                        cols = slice(c * 512, (c + 1) * 512)
                        dve.wait_ge(o_done, 2 * i + c + 1)
                        nc.vector.scalar_tensor_tensor(hid[:, sl, cols], res[:, sl, cols], ALPHA, ps_o[sl][:, cols],
                                                       ALU.mult, ALU.add).then_inc(r_ready, 1)
                        dve.wait_ge(r_ready, 2 * i + c + 1)
                        nc.vector.bn_stats(bst[:, sl, c, :], hid[:, sl, cols])
                    dve.drain()
                    nc.vector.bn_aggr(mv[:, sl, :], bst[:, sl, :, :]).then_inc(c_var, 1)
                    dve.wait_ge(c_sd, i + 1)
                    nc.vector.reciprocal(rs[:, sl, :], sd[:, sl, :])
                    nc.vector.scalar_tensor_tensor(hid[:, sl, :], hid[:, sl, :], mv[:, sl, 0:1], gain_b[:, 0, :],
                                                   ALU.subtract, ALU.mult)
                    dve.drain()
                    nc.vector.scalar_tensor_tensor(hid[:, sl, :], hid[:, sl, :], rs[:, sl, :], gain_b[:, 1, :],
                                                   ALU.mult, ALU.add).then_inc(h_ready, 1)

            steps(dve, TILES // 2, stage_c)
            stage_end(dve, 3)

            nc.vector.memset(aff[:, :], 0.0)
            nc.vector.reduce_max(lmax[:, :], logits[:, :, :], axis=AX.X)
            dve.drain()
            nc.vector.tensor_tensor(logits[:, :, :], logits[:, :, :], lmax[:, :].unsqueeze(2).to_broadcast([P, TILES, E]),
                                    ALU.subtract).then_inc(d_exp, 1)
            dve.wait_ge(d_exp, 2)
            nc.vector.reduce_sum(lsum[:, :], logits[:, :, :], axis=AX.X)
            dve.drain()
            nc.vector.reciprocal(lsum[:, :], lsum[:, :])
            dve.drain()
            nc.vector.tensor_tensor(logits[:, :, :], logits[:, :, :], lsum[:, :].unsqueeze(2).to_broadcast([P, TILES, E]),
                                    ALU.mult).then_inc(d_aff, 1)
            dve.wait_ge(d_step, 1)
            for g in range(GROUPS):
                nc.vector.tensor_copy(aff[g * GOFF:g * GOFF + E, :], ps_y[g][0:E, :])

            def w_lo_sub(e, c):
                dve.wait_ge(w_hi, NCHUNK * e + c + 1)
                nc.vector.tensor_tensor(w_l[:, c % RING, :], w_raw[:, c % RING, :], w_h[:, c % RING, :].bitcast(f32),
                                        ALU.subtract).then_inc(w_lo, 1)

            for r in range(CAP // 8):
                cols = slice(8 * r, 8 * r + 8)
                dve.drain()
                nc.vector.max(top_v[:, cols], aff[:, :])
                dve.drain()
                nc.vector.max_index(top_i[:, cols], top_v[:, cols], aff[:, :])
                if r < CAP // 8 - 1:
                    nc.vector.match_replace(aff[:, :], top_v[:, cols], aff[:, :], -1.0)
            dve.drain()
            nc.vector.tensor_copy(top_f[:, :], top_i[:, :])
            dve.drain()
            nc.vector.tensor_scalar(top_f[GOFF:ROWS, :], top_f[GOFF:ROWS, :], float(SEQ), None, ALU.add).then_inc(top_ready, 1)
            dve.wait_ge(d_step, 2)
            nc.vector.tensor_copy(gate_w8[:, :], ps_x[:, 0, 0:ROWS])
            nc.vector.tensor_copy(idx_t[:, :], ps_x[:, 1, 0:ROWS]).then_inc(top_ready, 1)
            for c in range(RING):
                w_lo_sub(0, c)

            XR = GROUPS * KD // 4

            def x_lo_sub(e, n):
                g, r = divmod(n, KD // 4)
                dve.wait_ge(x_hi, XR * e + n + 1)
                dst = (slice(None), slice(4 * r, 4 * r + 4), slice(g * CAP, (g + 1) * CAP))
                nc.vector.tensor_tensor(x_l[dst], ps_x[:, :, :], x_h[dst].bitcast(f32), ALU.subtract).then_inc(x_lo, 1)

            for n in range(XR):
                x_lo_sub(0, n)

            def stage_e(e, first, last_e):
                for j in range(KF // 2):
                    for n in (2 * j, 2 * j + 1):
                        dve.wait_ge(silu_done, KF * e + n + 1)
                        if n == 0 and not first:
                            dve.wait_ge(dn_done, (KF // 2) * e)
                        nc.vector.tensor_tensor(hf[:, n % 2, :], sg[:, n % 2, :], ps_gu[n % 3][:, 1, :], ALU.mult)
                        dve.drain()
                        nc.vector.tensor_copy(hh[:, n, :], hf[:, n % 2, :])
                        dve.drain()
                        nc.vector.tensor_tensor(hl[:, n, :], hf[:, n % 2, :], hh[:, n, :].bitcast(f32),
                                                ALU.subtract).then_inc(h_split, 1)
                    for c in (2 * j + RING, 2 * j + RING + 1):
                        w_lo_sub(e, c)
                for m in range(KF // 2):
                    if 2 <= m < 2 + XR and not last_e:
                        x_lo_sub(e + 1, m - 2)
                    c = NUP + m + RING
                    if c < NCHUNK:
                        w_lo_sub(e, c)
                    elif not last_e:
                        w_lo_sub(e + 1, c - NCHUNK)

            steps(dve, E, stage_e)
            stage_end(dve, 4)

            dve.wait_ge(f_const, 32)

            def stage_f(b, first, last_b):
                for k in range(FR):
                    dve.wait_ge(y_in[k], 16 * b + 16)
                    for c in range(2):
                        nc.vector.bn_stats(fst[:, k, c, :], y_raw[:, k, c * 512:(c + 1) * 512])
                    dve.drain()
                    nc.vector.bn_aggr(fmv[:, k, :], fst[:, k, :, :]).then_inc(f_var, 1)
                for k in range(FR):
                    dve.wait_ge(f_sd, FR * b + k + 1)
                    nc.vector.reciprocal(frs[:, k, :], fsd[:, k, :])
                    if not first:
                        dve.wait_ge(y_st[k], 16 * b)
                    nc.vector.scalar_tensor_tensor(y_out[:, k, :], y_raw[:, k, :], fmv[:, k, 0:1], gain_b[:, 0, :],
                                                   ALU.subtract, ALU.mult)
                    dve.drain()
                    nc.vector.scalar_tensor_tensor(y_out[:, k, :], y_out[:, k, :], frs[:, k, :], gain_b[:, 1, :],
                                                   ALU.mult, ALU.add).then_inc(f_ready, 1)

            steps(dve, TILES // FR, stage_f)

        @block.gpsimd
        def _(pool):
            pool.wait_ge(const_in, 96)

            def stage_a(b, first, last_b):
                for hf in range(2):
                    j = 2 * b + hf
                    start = first and hf == 0
                    for tt in range(2):
                        i = 2 * j + tt
                        H = HEADS + KVH
                        qn3 = qn[:, tt, :].rearrange("p (h c) -> p h c", c=HD)
                        q4 = qn[:, tt, :].rearrange("p (h a s c) -> p h a s c", a=2, s=2, c=16)
                        r4 = rot[:, :].rearrange("p (h a s c) -> p h a s c", a=2, s=2, c=16)
                        pool.wait_ge(qn_ready, i + 1)
                        nc.gpsimd.tensor_tensor(qn[:, tt, :], qn[:, tt, :], qkg[:, :], ALU.mult)
                        pool.drain()
                        for s in range(2):
                            sn = sin_t[:, bass.ds(i, 1), :].rearrange("p t (a s c) -> p t a s c", s=2, c=16)[:, :, :, s, :]
                            nc.gpsimd.tensor_tensor(r4[:, :, :, s, :], q4[:, :, :, 1 - s, :],
                                                    sn.to_broadcast([P, H, 2, 16]), ALU.mult)
                        pool.drain()
                        cs = cos_t[:, bass.ds(i, 1), :]
                        nc.gpsimd.tensor_tensor(qn3, qn3, cs.to_broadcast([P, H, HD]), ALU.mult)
                        pool.drain()
                        if not start:
                            pool.wait_ge(q_st[tt], 16 * j)
                            pool.wait_ge(k_st[tt], 16 * j)
                        for dst, c0, c1 in ((qkv[:, tt, :, 0:AW // KVH], 0, AW),
                                            (qkv[:, tt, :, AW // KVH:AW // KVH + HD], AW, QKW)):
                            last = nc.gpsimd.tensor_tensor(dst, qn[:, tt, c0:c1].rearrange("p (v c) -> p v c", v=KVH),
                                                           rot[:, c0:c1].rearrange("p (v c) -> p v c", v=KVH), ALU.add)
                        last.then_inc(roped, 1)

            steps(pool, PAIRS // 2, stage_a)

            stage_end(pool, 1)
            nc.gpsimd.memset(upad[:, 0:PAD], 0.0)
            nc.gpsimd.memset(upad[:, PAD + SEQ:], 0.0)

            def split_q(n):
                s, h = divmod(n, QH)
                pool.wait_ge(q_in, 16 * s + 16)
                if n >= 2:
                    s2, h2 = divmod(n - 2, QH)
                    pool.wait_ge(m_full, q_turn(s2, s2 == 0, s2 == SLOTS - 1, h2) + 1)
                q = q_raw[:, :, h * HD:(h + 1) * HD]
                nc.gpsimd.tensor_copy(q_hl[:, n % 2, :, 0:HD], q)
                pool.drain()
                nc.gpsimd.tensor_tensor(q_hl[:, n % 2, :, HD:P], q, q_hl[:, n % 2, :, 0:HD].bitcast(f32),
                                        ALU.subtract).then_inc(q_split, 1)

            def pool_window(n):
                g, w = divmod(n, NW)
                if n:
                    pool.wait_ge(m_ready, n)
                pool.dma_start(upad[:, PAD:PAD + SEQ], ut_d[w, :, g * SEQ:(g + 1) * SEQ]).then_inc(u_in, 16)
                pool.wait_ge(u_in, 16 * n + 16)
                src, n_in, width = upad, SEQ + 2 * PAD, 1
                for k in range(w + 1):
                    dst = (win_a, win_b)[k % 2]
                    n_in -= width
                    nc.gpsimd.tensor_tensor(dst[:, 0:n_in], src[:, 0:n_in], src[:, width:width + n_in], ALU.add)
                    pool.drain()
                    src, width = dst, 2 * width
                a = PAD - width // 2
                win = src[:, a:a + SEQ]
                for side, c in enumerate((slice(0, PAD), slice(SEQ - PAD, SEQ))):
                    nc.gpsimd.tensor_tensor(win[:, c], win[:, c], edge_t[:, w, side, :], ALU.mult)
                pool.drain()
                nc.gpsimd.tensor_scalar(win, win, 1.0 / width, None, ALU.mult)
                pool.drain()
                nc.gpsimd.tensor_tensor(mix_pl[:, w, g * SEQ:(g + 1) * SEQ], win, upad[:, PAD:PAD + SEQ],
                                        ALU.subtract).then_inc(m_ready, 1)

            pool.wait_ge(b_const, 80)
            split_q(0)
            split_q(1)
            for n in range(2, SLOTS * QH):
                split_q(n)
                if n % 2 == 1 and n // 2 <= GROUPS * NW:
                    pool_window(n // 2 - 1)
            pool_window(GROUPS * NW - 1)
            stage_end(pool, 2)

            def stage_c(b, first, last_b):
                for sl in range(2):
                    i = 2 * b + sl
                    pool.wait_ge(h_ready, i + 1)
                    if not first:
                        pool.wait_ge(acc_st[sl], 16 * b)
                    nc.gpsimd.tensor_tensor(acc[:, sl, :], hid[:, sl, :], alpha[:, 0:1].to_broadcast([P, D]),
                                            ALU.mult).then_inc(acc_ready, 1)

            steps(pool, TILES // 2, stage_c)
            stage_end(pool, 3)

            XR = GROUPS * KD // 4
            nc.gpsimd.memset(no_shift[:, :], 0)
            pool.wait_ge(top_ready, 2)

            def gather(e, start):
                if not start:
                    pool.wait_ge(xt_d, XR * e)
                for g in range(GROUPS):
                    nc.gpsimd.tensor_copy(idx_g[:, g:g + 1], idx_t[:, bass.ds(e + g * GOFF, 1)])
                pool.drain()
                for g in range(GROUPS):
                    pool.indirect_dma_start(out=xg[:, g, :], out_offset=None, in_=h_d[:, :],
                                            in_offset=bass.IndirectOffsetOnAxis(ap=idx_g[:, g:g + 1], axis=0)
                                            ).then_inc(x_in_g[g], 16)

            def scatter(e):
                for g in range(GROUPS):
                    nc.gpsimd.tensor_copy(idx_e[:, g:g + 1], idx_t[:, bass.ds(e + g * GOFF, 1)])
                pool.drain()
                pool.wait_ge(y_ready, GROUPS * (e + 1))
                nc.gpsimd.tensor_tensor(idx_s[:, :], idx_e[:, :], no_shift[:, :], ALU.add)
                pool.drain()
                for g in range(GROUPS):
                    pool.indirect_dma_start(out=acc_d[:, :], in_=ysb[:, g, :], in_offset=None,
                                            out_offset=bass.IndirectOffsetOnAxis(ap=idx_s[:, g:g + 1], axis=0),
                                            compute_op=ALU.add).then_inc(scat[g], 16)
                for g in range(GROUPS):
                    pool.wait_ge(scat[g], 16 * (e + 1))

            gather(0, True)

            def stage_e(e, first, last_e):
                if not last_e:
                    gather(e + 1, False)
                scatter(e)

            steps(pool, E, stage_e)
            stage_end(pool, 4)


_INS = ["x", "ln_in_g", "ln_in_b", "w_in", "qk_gain", "w_pool", "pool_scale", "w_out", "ln1_g", "ln1_b", "w_router",
        "w_gate", "w_up", "w_down", "ln2_g", "ln2_b", "rope_cos", "rope_sin", "pool_edge", "eye"]


def lay_out(x_prompt, x_sample, ln_in_g, ln_in_b, w_in, q_norm_g, k_norm_g, w_pool, pool_scale, w_out,
            ln1_g, ln1_b, w_router, w_gate, w_up, w_down, ln2_g, ln2_b):
    seq = x_prompt.shape[1]
    d = x_prompt.shape[2]
    rows = lambda v: np.ascontiguousarray(np.broadcast_to(v, (128, v.shape[-1])))
    grid_w, pairs, theta = 64, 16, 10000.0
    inv = theta ** (-np.arange(pairs, dtype=np.float32) / np.float32(pairs))
    row = np.repeat(np.arange(seq // grid_w), grid_w).astype(np.float32)[:, None] * inv.astype(np.float32)
    col = np.tile(np.arange(grid_w), seq // grid_w).astype(np.float32)[:, None] * inv.astype(np.float32)
    cos = np.concatenate([np.cos(row), np.cos(row), np.cos(col), np.cos(col)], axis=1)
    sin = np.concatenate([-np.sin(row), np.sin(row), -np.sin(col), np.sin(col)], axis=1)
    edge = np.ones((4, 2, 8), np.float32)
    for g, w in enumerate((2, 4, 8, 16)):
        for n in range(8):
            for side, t in ((0, n), (1, seq - 8 + n)):
                lo, hi = max(t - w // 2, 0), min(t - w // 2 + w, seq)
                edge[g, side, n] = w / (hi - lo)
    gains = np.concatenate([np.tile(q_norm_g[0], 8), np.tile(k_norm_g[0], 2)])
    return {
        "x": np.concatenate([x_prompt[0], x_sample[0]], axis=0),
        "ln_in_g": rows(ln_in_g), "ln_in_b": rows(ln_in_b), "w_in": w_in[0], "qk_gain": rows(gains),
        "w_pool": w_pool[0], "pool_scale": np.ascontiguousarray(pool_scale[0].reshape(4, 128).T), "w_out": w_out[0],
        "ln1_g": rows(ln1_g[0]), "ln1_b": rows(ln1_b[0]), "w_router": w_router[0],
        "w_gate": w_gate[0], "w_up": w_up[0], "w_down": w_down[0],
        "ln2_g": rows(ln2_g[0]), "ln2_b": rows(ln2_b[0]),
        "rope_cos": np.tile(cos, (2, 1)), "rope_sin": np.tile(sin, (2, 1)),
        "pool_edge": np.ascontiguousarray(np.broadcast_to(edge.reshape(-1), (128, 64))),
        "eye": np.eye(128, dtype=np.float32),
    }


def kernel(**inputs):
    import concourse.bacc as bacc
    from concourse.bass_utils import run_bass_kernel_spmd

    nc = bacc.Bacc("TRN2", target_bir_lowering=False, num_devices=1)
    arrays = {f"in_{n}": np.ascontiguousarray(a) for n, a in
              lay_out(**{k: np.asarray(v) for k, v in inputs.items()}).items()}
    args = [nc.dram_tensor(f"in_{n}", arrays[f"in_{n}"].shape, mybir.dt.float32, kind="ExternalInput").ap() for n in _INS]
    shape = arrays["in_x"].shape
    y = nc.dram_tensor("out_y", shape, mybir.dt.float32, kind="ExternalOutput").ap()
    encoder_layer(nc, *args, y)
    got = run_bass_kernel_spmd(nc, [arrays], core_ids=[0]).results[0]["out_y"]
    half = shape[0] // 2
    return got[:half].reshape(1, half, shape[1]), got[half:].reshape(1, half, shape[1])
```

```python
import numpy as np
from contextlib import ExitStack
import concourse.bass as bass
from concourse import mybir


def encoder_layer(nc, x, ln_in_g, ln_in_b, w_in, qk_gain, w_pool, pool_scale, w_out, ln1_g, ln1_b, w_router,
                  w_gate, w_up, w_down, ln2_g, ln2_b, rope_cos, rope_sin, pool_edge, eye, flip, out):
    f32, f32r, u32 = mybir.dt.float32, mybir.dt.float32r, mybir.dt.uint32
    ALU, ACT, AX = mybir.AluOpType, mybir.ActivationFunctionType, mybir.AxisListType

    P = 128
    TOK, D = x.shape
    GROUPS = 2
    SEQ = TOK // GROUPS
    KD = D // P
    HD = 64
    HEADS, KVH = 8, 2
    AW, KVW = HEADS * HD, KVH * HD
    QKW = AW + KVW
    QKVW = AW + 2 * KVW
    WINDOWS = (2, 4, 8, 16)
    PAD = max(WINDOWS) // 2
    NW = len(WINDOWS)
    E, _, F = w_gate.shape
    KF = F // P
    CAP = 2 * SEQ // E
    LN_EPS, RMS_EPS, ALPHA = 1e-5, 1e-6, 2.0 ** 0.25
    TILES = TOK // P
    GT = SEQ // P

    def dram(name, shape, dt=f32):
        return nc.dram_tensor(name, shape, dt, kind="Internal").ap()

    xln_d = dram("xln_d", (TOK, D))
    KVC = AW // KVH + 2 * HD
    q_d = dram("q_d", (KVH * TOK, AW // KVH))
    k_d = dram("k_d", (KVH * TOK, HD))
    v_d = dram("v_d", (KVH * TOK, HD))
    ut_d = dram("ut_d", (NW, P, TOK))
    h_d = dram("h_d", (TOK, D))
    acc_d = dram("acc_d", (TOK, D))

    ctx = ExitStack()
    with ctx:
        def sem(name):
            return ctx.enter_context(nc.semaphore(name))

        def alloc(stack):
            return lambda name, shape, dt=f32: stack.enter_context(nc.sbuf_tensor(name, shape, dt))

        def palloc(stack):
            return lambda name, shape, dt=f32: stack.enter_context(nc.psum_tensor(name, shape, dt))

        def at(eng, value):
            return value if isinstance(value, int) else eng.snap(value)

        def steps(eng, n, body):
            body(0, True, False)
            with eng.Fori(1, n - 1) as i:
                body(i, False, False)
            body(n - 1, False, True)

        sb = alloc(ctx)
        ident = sb("ident", [P, P])
        gain_b = sb("gain_b", [P, 2, D])
        eps = sb("eps", [P, 2])
        alpha = sb("alpha", [P, 1])
        logits = sb("logits", [P, TILES, E])
        mv = sb("mv", [P, 2, 2])
        bst = sb("bst", [P, 2, 2, 6])
        sd = sb("sd", [P, 2, 1])
        rs = sb("rs", [P, 2, 1])

        QC = AW // KVH
        W_RING = 3
        early = sb("early", [P, max(GT * (QC + 2 * HD), W_RING * D)])
        q_raw = early[:, 0:GT * QC].rearrange("p (t c) -> p t c", c=QC)
        k_raw = early[:, GT * QC:GT * (QC + HD)].rearrange("p (t c) -> p t c", c=HD)
        v_raw = early[:, GT * (QC + HD):GT * (QC + 2 * HD)].rearrange("p (t c) -> p t c", c=HD)
        wo_raw = early[:, 0:W_RING * D].rearrange("p (k c) -> p k c", c=D)
        ident_r = sb("ident_r", [P, P], f32r)

        sa = ExitStack()
        sb, pb = alloc(sa), palloc(sa)
        PAIRS = TILES // 2
        win_h = sb("win_h", [P, KD, w_in.shape[1]], f32r)
        win_l = sb("win_l", [P, KD, w_in.shape[1]], f32r)
        RAW = 6
        W_EARLY = 2
        W_COLS = w_in.shape[1]
        win_rest = sb("win_rest", [P, RAW - 2, W_COLS])
        win_raw = [early[:, i * W_COLS:(i + 1) * W_COLS] for i in range(2)] + [win_rest[:, i, :] for i in range(RAW - 2)]
        xin = sb("xin", [P, 2, D])
        xt_h = sb("xt_h", [P, 2, KD, 2 * P], f32r)
        xt_l = sb("xt_l", [P, 2, KD, 2 * P], f32r)
        cos_t = sb("cos_t", [P, TILES, HD])
        sin_t = sb("sin_t", [P, TILES, HD])
        qkg = sb("qkg", [P, QKW])
        sq = sb("sq", [P, QKW])
        qn = sb("qn", [P, 2, QKW])
        rot = sb("rot", [P, QKW])
        xln = sb("xln", [P, 2, D])
        qkv = sb("qkv", [P, 2, KVH, KVC])
        ust = sb("ust", [P, 2, NW, 2 * P])
        ss = sb("ss", [P, 2, 16])
        rn = sb("rn", [P, 2, 16])
        ps_xt = [pb(f"ps_xt{i}", [P, KD, P]) for i in range(2)]
        ps_q = pb("ps_q", [P, AW])
        ps_kv = pb("ps_kv", [P, 512])
        ps_u = [pb(f"ps_u{i}", [P, 2, 2 * P]) for i in range(2)]
        sa.close()

        keep = ExitStack()
        sb = alloc(keep)
        SLOTS = KVH * GROUPS
        QH = HEADS // KVH
        PAIR_H = QH // 2
        mix_at = sb("mix_at", [P, KVH, PAIR_H, TOK])
        mix_pl = sb("mix_pl", [P, NW, TOK])
        sB = ExitStack()
        sb, pb = alloc(sB), palloc(sB)
        QB = 2 * P
        NQB = QH * SEQ // QB
        kd_h = sb("kd_h", [P, GT, P], f32r)
        kd_l = sb("kd_l", [P, GT, P], f32r)
        kt_h = sb("kt_h", [P, 2 * SEQ], f32r)
        kt_l = sb("kt_l", [P, 2 * SEQ], f32r)
        v_hl = sb("v_hl", [P, GT, P], f32r)
        q_hl = sb("q_hl", [P, 2, GT, P], f32r)
        qt_hl = sb("qt_hl", [P, 2, SEQ], f32r)
        prob = sb("prob", [P, 2, SEQ])
        pt_h = sb("pt_h", [P, 2, GT, QB], f32r)
        pt_l = sb("pt_l", [P, 2, GT, QB], f32r)
        o_hl = sb("o_hl", [P, 2, QB])
        at_tok = sb("at_tok", [P, GT, 2 * HD])
        nmax = sb("nmax", [P, 2])
        rsum = sb("rsum", [P, 2 * GT])
        rinv = sb("rinv", [P, 2 * GT])
        ident2 = sb("ident2", [P, HD])
        upad = sb("upad", [P, SEQ + 2 * PAD])
        win_a = sb("win_a", [P, SEQ + 2 * PAD])
        win_b = sb("win_b", [P, SEQ + 2 * PAD])
        edge_t = sb("edge_t", [P, NW, 2, PAD])
        wp_sb = sb("wp_sb", [P, NW, P])
        psc = sb("psc", [P, NW])
        ps_s = [pb(f"ps_s{i}", [P, SEQ]) for i in range(2)]
        ps_t = [pb(f"ps_t{i}", [P, 4, P]) for i in range(2)]
        ps_pv = pb("ps_pv", [P, 512])
        ps_m = pb("ps_m", [P, 4, P])
        sB.close()

        sc = ExitStack()
        sb, pb = alloc(sc), palloc(sc)
        KM = w_out.shape[0] // P
        wo_h = sb("wo_h", [P, KM, D], f32r)
        wo_l = sb("wo_l", [P, KM, D], f32r)
        wr_sb = sb("wr_sb", [P, KD, E])
        mx_h = sb("mx_h", [P, 2, KM, P], f32r)
        mx_l = sb("mx_l", [P, 2, KM, P], f32r)
        res = sb("res", [P, 2, D])
        hid = sb("hid", [P, 2, D])
        acc = sb("acc", [P, 2, D])
        ht = sb("ht", [P, KD, P])
        ps_o = [pb(f"ps_o{i}", [P, D]) for i in range(2)]
        ps_ht = pb("ps_ht", [P, KD, P])
        ps_l = pb("ps_l", [P, 512])
        sc.close()
        keep.close()
        c_const = sem("c_const")
        wo_in = [sem(f"wo_in{i}") for i in range(W_RING)]
        wo_hi, wo_lo = sem("wo_hi"), sem("wo_lo")
        res_in = [sem(f"res_in{i}") for i in range(2)]
        mx_hi, mx_lo, o_done = sem("mx_hi"), sem("mx_lo"), sem("o_done")
        r_ready, c_var, c_sd, h_ready = sem("r_ready"), sem("c_var"), sem("c_sd"), sem("h_ready")
        h_st = [sem(f"h_st{i}") for i in range(2)]
        acc_st = [sem(f"acc_st{i}") for i in range(2)]
        acc_ready, ht_done, ht_ready, l_done, l_ready = (sem("acc_ready"), sem("ht_done"), sem("ht_ready"),
                                                         sem("l_done"), sem("l_ready"))

        se = ExitStack()
        sb, pb = alloc(se), palloc(se)
        RING = 4
        CHUNK = KD * 2 * P
        w_raw = sb("w_raw", [P, RING, CHUNK])
        w_h = sb("w_h", [P, RING, CHUNK], f32r)
        w_l = sb("w_l", [P, RING, CHUNK], f32r)
        C2 = GROUPS * CAP
        hh = sb("hh", [P, KF, C2], f32r)
        hl = sb("hl", [P, KF, C2], f32r)
        x_h = sb("x_h", [P, KD, C2], f32r)
        x_l = sb("x_l", [P, KD, C2], f32r)
        xg = sb("xg", [P, GROUPS, D])
        ysb = sb("ysb", [P, GROUPS, D])
        sg = sb("sg", [P, 2, C2])
        hf = sb("hf", [P, 2, C2])
        lmax = sb("lmax", [P, TILES])
        lsum = sb("lsum", [P, TILES])
        HALF = SEQ // 2
        GOFF = E
        HT = HALF // P
        ROWS = GROUPS * 2 * E
        soft = sb("soft", [P, HT, ROWS])
        aff = sb("aff", [ROWS, HALF])
        top_v = sb("top_v", [ROWS, CAP])
        top_i = sb("top_i", [ROWS, CAP], u32)
        top_f = sb("top_f", [ROWS, CAP])
        flip_sb = sb("flip_sb", [P, P])
        cols_vf = sb("cols_vf", [P, 2, ROWS])
        first_wins = sb("first_wins", [P, GROUPS, E])
        idx_diff = sb("idx_diff", [P, GROUPS, E])
        gate_w8 = sb("gate_w8", [P, GROUPS * E])
        idx_t = sb("idx_t", [P, GROUPS * E], u32)
        idx_g = sb("idx_g", [P, GROUPS], u32)
        no_shift = sb("no_shift", [P, GROUPS], u32)
        idx_e = sb("idx_e", [P, GROUPS], u32)
        idx_s = sb("idx_s", [P, GROUPS], u32)
        ps_gu = [pb(f"ps_gu{i}", [P, 2, C2]) for i in range(3)]
        ps_y = [pb(f"ps_y{i}", [P, D]) for i in range(GROUPS)]
        ps_x = pb("ps_x", [P, 4, P])
        se.close()
        w_dma = [sem(f"w_dma{i}") for i in range(RING)]
        w_hi, w_lo = sem("w_hi"), sem("w_lo")
        cols_ready = sem("cols_ready")
        d_step, d_exp, d_aff = sem("d_step"), sem("d_exp"), sem("d_aff")
        top_ready, flip_in = sem("top_ready"), sem("flip_in")
        x_in_g = [sem(f"x_in_g{g}") for g in range(GROUPS)]
        xt_d, x_hi, x_lo = sem("xt_d"), sem("x_hi"), sem("x_lo")
        gu_done, silu_done, h_split = sem("gu_done"), sem("silu_done"), sem("h_split")
        dn_done, y_ready = sem("dn_done"), sem("y_ready")
        scat = [sem(f"scat{g}") for g in range(GROUPS)]

        sf = ExitStack()
        sb = alloc(sf)
        FR = 4
        y_raw = sb("y_raw", [P, TILES, D])
        y_out = sb("y_out", [P, FR, D])
        fst = sb("fst", [P, FR, 2, 6])
        fmv = sb("fmv", [P, FR, 2])
        fsd = sb("fsd", [P, FR, 1])
        frs = sb("frs", [P, FR, 1])
        fminus = sb("fminus", [P, FR, 1])
        sf.close()
        f_const = sem("f_const")
        y_in = [sem(f"y_in{i}") for i in range(FR)]
        f_var, f_sd, f_centred = sem("f_var"), sem("f_sd"), sem("f_centred")
        f_gained, f_ready = sem("f_gained"), sem("f_ready")
        y_st = [sem(f"y_st{i}") for i in range(FR)]

        NCHUNK = 2 * KF // 2 + KF // 2
        NUP = KF

        def x_bank(n, start):
            if not start:
                return ps_x[:, :, :]
            return ps_y[n // 2][:, (n % 2) * 512:(n % 2 + 1) * 512].rearrange("p (k t) -> p k t", t=P)

        def used(e, c):
            if c < NUP:
                return gu_done, KF * e + 2 * (c // 2) + 2
            return dn_done, (KF // 2) * e + (c - NUP) + 1

        stage_over = sem("stage_over")
        ident_ready = sem("ident_ready")
        b_const, q_in, k_in, v_in = sem("b_const"), sem("q_in"), sem("k_in"), sem("v_in")
        k_hi, k_split, v_hi, v_split = sem("k_hi"), sem("k_split"), sem("v_hi"), sem("v_split")
        q_split = sem("q_split")
        s_done, max_ready, exp_ready, t_done = sem("s_done"), sem("max_ready"), sem("exp_ready"), sem("t_done")
        pt_hi, pt_lo, pv_done, o_ready = sem("pt_hi"), sem("pt_lo"), sem("pv_done"), sem("o_ready")
        m_full, m_free = sem("m_full"), sem("m_free")
        kt_full, kt_free = sem("kt_full"), sem("kt_free")
        u_in, m_ready, pm_done, pl_ready = sem("u_in"), sem("m_ready"), sem("pm_done"), sem("pl_ready")

        def stage_end(eng, n):
            eng.drain().then_inc(stage_over, 1)
            eng.wait_ge(stage_over, 5 * n)

        NSTEP = QH * GT
        k_turn_at = {6: (0, 0), 8: (0, 1), 22: (1, 0), 24: (1, 1)}
        q_turn_at = {3: 0, 5: 1}

        def before_step(t, last):
            found = []
            if t in k_turn_at and not last:
                found.append(("K", *k_turn_at[t]))
            if t < NSTEP and t % GT in q_turn_at and not (last and t // GT + 1 == QH):
                found.append(("Q", (t // GT + 1) % QH, q_turn_at[t % GT]))
            return found

        def after_step(t, start):
            pv = t // 2 - 1 if t % 2 == 0 else None
            add = (t - 3) // 2 if t % 2 == 1 else None
            back = (t - 4) // 2 if t % 2 == 0 else None
            if back is not None and (back // (NQB // QH)) % 2 == 0:
                back = None
            return tuple(None if b is not None and (b < 0 and start or b >= NQB) else b for b in (pv, add, back))

        def turns_of(last):
            found = []
            for t in range(NSTEP + (3 if last else 0)):
                found += before_step(t, last)
                _, add, back = after_step(t, False)
                found += [("add", add)] if add is not None else []
                found += [("back", back)] if back is not None else []
            return {what: n for n, what in enumerate(found)}

        turn_mid, turn_last = turns_of(False), turns_of(True)
        TURNS = len(turn_mid)
        first_turns = [("Q", 0, 0), ("Q", 0, 1)]
        TURN0 = len(first_turns) - 3

        def turn_no(s, last, what):
            return TURNS * s + TURN0 + (turn_last if last else turn_mid)[what]

        def q_turn(s, first, last, h):
            if h == 0:
                return len(first_turns) - 1 if first else turn_no(s - 1, False, ("Q", 0, 1))
            return turn_no(s, last, ("Q", h, 1))

        gain_in, eye_in, rope_in = sem("gain_in"), sem("eye_in"), sem("rope_in")
        x_in = [sem(f"x_in{i}") for i in range(2)]
        win_in = [sem(f"win_in{i}") for i in range(RAW)]
        win_hi, win_lo = sem("win_hi"), sem("win_lo")
        var_ready, sd_ready, xln_ready = sem("var_ready"), sem("sd_ready"), sem("xln_ready")
        xln_st = [sem(f"xln_st{i}") for i in range(2)]
        xt_done, xt_hi, xt_lo = sem("xt_done"), sem("xt_hi"), sem("xt_lo")
        q_done, kv_done, u_done = sem("q_done"), sem("kv_done"), sem("u_done")
        ss_ready, rms_sd = sem("ss_ready"), sem("rms_sd")
        qn_ready, v_ready, roped = sem("qn_ready"), sem("v_ready"), sem("roped")
        u_ready = sem("u_ready")
        q_st = [sem(f"q_st{i}") for i in range(2)]
        k_st = [sem(f"k_st{i}") for i in range(2)]
        v_st = [sem(f"v_st{i}") for i in range(2)]
        u_st = [sem(f"u_st{i}") for i in range(2)]
        eps_set = sem("eps_set")

        block = ctx.enter_context(nc.Block())

        @block.sync
        def _(sp):
            sp.dma_start(xin[:, 0, :], x[0:P, :]).then_inc(x_in[0], 16)
            sp.dma_start(gain_b[:, 0, :], ln_in_g).then_inc(gain_in, 16)
            sp.dma_start(gain_b[:, 1, :], ln_in_b).then_inc(gain_in, 16)
            sp.dma_start(xin[:, 1, :], x[P:2 * P, :]).then_inc(x_in[1], 16)
            sp.dma_start(ident[:, :], eye).then_inc(eye_in, 16)
            for k in range(KD):
                if k >= RAW:
                    sp.wait_ge(win_lo, k - RAW + 1)
                sp.dma_start(win_raw[k % RAW], w_in[k * P:(k + 1) * P, :]).then_inc(win_in[k % RAW], 16)
            for tt in range(2):
                sp.wait_ge(xln_ready, tt + 1)
                sp.dma_start(xln_d[tt * P:(tt + 1) * P, :], xln[:, tt, :]).then_inc(xln_st[tt], 16)
                sp.dma_start(xin[:, tt, :], x[(2 + tt) * P:(3 + tt) * P, :]).then_inc(x_in[tt], 16)
            for dst, src in ((qkg[:, :], qk_gain),
                             (sin_t[:, :, :], rope_sin.rearrange("(t p) c -> p t c", p=P)),
                             (cos_t[:, :, :], rope_cos.rearrange("(t p) c -> p t c", p=P))):
                sp.dma_start(dst, src).then_inc(rope_in, 16)

            q_t = q_d.rearrange("(v t) c -> v t c", v=KVH)
            k_t = k_d.rearrange("(v t) c -> v t c", v=KVH)
            v_t = v_d.rearrange("(v t) c -> v t c", v=KVH)

            def load_k(s, first):
                rows = bass.ds(at(sp, s * SEQ), SEQ)
                if not first:
                    sp.wait_ge(k_split, 2 * s)
                sp.dma_start(k_raw[:, :, :], k_d[rows, :].rearrange("(t p) c -> p t c", p=P)).then_inc(k_in, 16)

            def load_v(s, first):
                rows = bass.ds(at(sp, s * SEQ), SEQ)
                if not first:
                    sp.wait_ge(v_split, s)
                sp.dma_start(v_raw[:, :, :], v_d[rows, :].rearrange("(t p) c -> p t c", p=P)).then_inc(v_in, 16)

            def load_q(s, first):
                rows = bass.ds(at(sp, s * SEQ), SEQ)
                if not first:
                    sp.wait_ge(q_split, QH * s)
                sp.dma_start(q_raw[:, :, :], q_d[rows, :].rearrange("(t p) c -> p t c", p=P)).then_inc(q_in, 16)

            def stage_a(b, first, last_b):
                if last_b:
                    for tt in range(2):
                        sp.wait_ge(k_st[tt], 16 * 2 * b)
                        sp.wait_ge(q_st[tt], 16 * 2 * b)
                        sp.wait_ge(v_st[tt], 16 * 2 * b)
                    load_k(0, True)
                    load_q(0, True)
                    load_v(0, True)
                for hf in range(2):
                    j = 2 * b + hf
                    rows = [bass.ds(at(sp, j * (2 * P) + k * P), P)
                            for k in range(6 if not last_b else 4 - 2 * hf)]
                    for tt in range(2):
                        if not (last_b and hf == 1):
                            sp.wait_ge(xln_ready, 2 * j + 3 + tt)
                            sp.dma_start(xln_d[rows[2 + tt], :], xln[:, tt, :]).then_inc(xln_st[tt], 16)
                        if not last_b:
                            sp.dma_start(xin[:, tt, :], x[rows[4 + tt], :]).then_inc(x_in[tt], 16)
                    for tt in range(2):
                        sp.wait_ge(v_ready, 2 * j + tt + 1)
                        sp.wait_ge(roped, 2 * j + tt + 1)
                        sp.dma_start(q_t[:, rows[tt], :].rearrange("v p c -> p v c"),
                                     qkv[:, tt, :, 0:KVC - 2 * HD]).then_inc(q_st[tt], 16)
                        sp.dma_start(k_t[:, rows[tt], :].rearrange("v p c -> p v c"),
                                     qkv[:, tt, :, KVC - 2 * HD:KVC - HD]).then_inc(k_st[tt], 16)
                        sp.dma_start(v_t[:, rows[tt], :].rearrange("v p c -> p v c"),
                                     qkv[:, tt, :, KVC - HD:KVC]).then_inc(v_st[tt], 16)

            steps(sp, PAIRS // 2, stage_a)
            stage_end(sp, 1)
            for tt in range(2):
                sp.wait_ge(xln_st[tt], 16 * PAIRS)
                sp.wait_ge(q_st[tt], 16 * PAIRS)
                sp.wait_ge(k_st[tt], 16 * PAIRS)
                sp.wait_ge(v_st[tt], 16 * PAIRS)
                sp.wait_ge(u_st[tt], 8 * PAIRS)

            for dst, src in ((ident2[0:HD, :], eye[0:HD, 0:HD]), (ident2[HD:P, :], eye[0:HD, 0:HD]),
                             (edge_t[:, :, :, :], pool_edge.rearrange("p (w s n) -> p w s n", w=NW, s=2)),
                             (wp_sb[:, :, :], w_pool.rearrange("w c d -> c w d")),
                             (psc[:, :], pool_scale)):
                sp.dma_start(dst, src).then_inc(b_const, 16)

            def stage_b(s, first, last_s):
                if not last_s:
                    load_k(s + 1, False)
                    load_v(s + 1, False)
                    load_q(s + 1, False)

            steps(sp, SLOTS, stage_b)
            sp.wait_ge(k_split, 2 * SLOTS)
            sp.wait_ge(v_split, SLOTS)
            sp.wait_ge(q_split, QH * SLOTS)
            for k in range(KM):
                if k >= W_RING:
                    sp.wait_ge(wo_lo, k - W_RING + 1)
                sp.dma_start(wo_raw[:, k % W_RING, :], w_out[k * P:(k + 1) * P, :]).then_inc(wo_in[k % W_RING], 16)
            for dst, src in ((wr_sb[:, :, :], w_router.rearrange("(k p) e -> p k e", p=P)),
                             (gain_b[:, 0, :], ln1_g), (gain_b[:, 1, :], ln1_b)):
                sp.dma_start(dst, src).then_inc(c_const, 16)
            stage_end(sp, 2)

            for k in range(2):
                sp.dma_start(res[:, k, :], xln_d[k * P:(k + 1) * P, :]).then_inc(res_in[k], 16)

            def stage_c(b, first, last_b):
                rows = [bass.ds(at(sp, (2 * b + k) * P), P) for k in range(2 if last_b else 4)]
                for sl in range(2):
                    i = 2 * b + sl
                    if not last_b:
                        sp.wait_ge(r_ready, 2 * i + 2)
                        sp.dma_start(res[:, sl, :], xln_d[rows[2 + sl], :]).then_inc(res_in[sl], 16)
                    sp.wait_ge(h_ready, i + 1)
                    sp.dma_start(h_d[rows[sl], :], hid[:, sl, :]).then_inc(h_st[sl], 16)
                    sp.wait_ge(acc_ready, i + 1)
                    sp.dma_start(acc_d[rows[sl], :], acc[:, sl, :]).then_inc(acc_st[sl], 16)

            steps(sp, TILES // 2, stage_c)
            for sl in range(2):
                sp.wait_ge(h_st[sl], 8 * TILES)
                sp.wait_ge(acc_st[sl], 8 * TILES)
            stage_end(sp, 3)

            sp.dma_start(flip_sb[:, :], flip).then_inc(flip_in, 16)
            for dst, src in ((gain_b[:, 0, :], ln2_g), (gain_b[:, 1, :], ln2_b)):
                sp.dma_start(dst, src).then_inc(f_const, 16)

            def stage_e(e, first, last_e):
                ex = bass.ds(e, 1)
                for c in range(NCHUNK):
                    if not (first and c < RING):
                        sp.wait_ge(w_lo, NCHUNK * e + c - RING + 1)
                    dst = w_raw[:, c % RING, :]
                    if c < NUP:
                        w = (w_gate, w_up)[c % 2]
                        src = w[ex, :, (c // 2) * 2 * P:(c // 2 + 1) * 2 * P].rearrange("o (k p) f -> p (o k) f", p=P)
                        dst = dst.rearrange("p (k f) -> p k f", k=KD)
                    else:
                        m = c - NUP
                        src = w_down[ex, m * 2 * P:(m + 1) * 2 * P, :].rearrange("o (k p) d -> p (o k) d", p=P)
                        dst = dst.rearrange("p (k d) -> p k d", k=2)
                    sp.dma_start(dst, src).then_inc(w_dma[c % RING], 16)

            steps(sp, E, stage_e)
            stage_end(sp, 4)

            for i in range(TILES):
                if i >= FR:
                    sp.wait_ge(y_in[i % FR], 16 * (i // FR))
                sp.dma_start(y_raw[:, i, :], acc_d[i * P:(i + 1) * P, :]).then_inc(y_in[i % FR], 16)

            def stage_f(b, first, last_b):
                rows = [bass.ds(at(sp, (FR * b + k) * P), P) for k in range(FR)]
                for k in range(FR):
                    sp.wait_ge(f_ready, FR * b + k + 1)
                    sp.dma_start(out[rows[k], :], y_out[:, k, :]).then_inc(y_st[k], 16)

            steps(sp, TILES // FR, stage_f)
            for k in range(FR):
                sp.wait_ge(y_st[k], 16 * TILES // FR)

        @block.tensor
        def _(pe):
            def x_transposes(j, start):
                for tt in range(2):
                    i = 2 * j + tt
                    pe.wait_ge(xln_ready, i + 1)
                    if not start:
                        pe.wait_ge(xt_hi, i - 1)
                        pe.wait_ge(xt_lo, i - 1)
                    for k in range(KD):
                        last = nc.tensor.transpose(ps_xt[tt][:, k, :], xln[:, tt, k * P:(k + 1) * P], ident[:, :])
                    last.then_inc(xt_done, 1)

            def qkv_product(j, hf, tt, start):
                i = 2 * j + tt
                pe.wait_ge(xt_hi, i + 1)
                pe.wait_ge(xt_lo, i + 1)
                for ps, c0, c1, done in ((ps_q, 0, AW, q_done), (ps_kv, AW, QKVW, kv_done)):
                    if not start:
                        pe.wait_ge(qn_ready, i)
                        pe.wait_ge(v_ready, i)
                    for k in range(KD):
                        if start and c0 == 0:
                            pe.wait_ge(win_hi, k + 1)
                            pe.wait_ge(win_lo, k + 1)
                        t = slice(tt * P, (tt + 1) * P)
                        for n, (a, w) in enumerate(((xt_h, win_h), (xt_h, win_l), (xt_l, win_h))):
                            last = nc.tensor.matmul(ps[:, 0:c1 - c0], a[:, hf, k, t], w[:, k, c0:c1],
                                                    start=k == 0 and n == 0, stop=k == KD - 1 and n == 2)
                    last.then_inc(done, 1)

            def u_product(j, hf, cp, start):
                pe.wait_ge(xt_hi, 2 * j + 2)
                pe.wait_ge(xt_lo, 2 * j + 2)
                if not start:
                    pe.wait_ge(u_ready, 2 * j - 1 + cp)
                for c in range(2):
                    c0 = QKVW + (2 * cp + c) * P
                    for k in range(KD):
                        for n, (w, a) in enumerate(((win_h, xt_h), (win_h, xt_l), (win_l, xt_h))):
                            last = nc.tensor.matmul(ps_u[cp][:, c, :], w[:, k, c0:c0 + P], a[:, hf, k, :],
                                                    start=k == 0 and n == 0, stop=k == KD - 1 and n == 2)
                last.then_inc(u_done, 1)

            def stage_a(b, first, last_b):
                for hf in range(2):
                    j = 2 * b + hf
                    start = first and hf == 0
                    qkv_product(j, hf, 0, start)
                    u_product(j, hf, 0, start)
                    if not (last_b and hf == 1):
                        x_transposes(j + 1, False)
                    qkv_product(j, hf, 1, False)
                    u_product(j, hf, 1, start)

            pe.wait_ge(eye_in, 16)
            x_transposes(0, True)
            steps(pe, PAIRS // 2, stage_a)

            stage_end(pe, 1)
            pe.wait_ge(ident_ready, 1)

            def through_m(number, what, s):
                if what[0] == "K":
                    _, lo, r = what
                    src = (kd_h, kd_l)[lo]
                    pe.wait_ge(k_split, 2 * s + 2)
                else:
                    _, h, r = what
                    src = q_hl[:, h % 2, :, :]
                    pe.wait_ge(q_split, QH * s + h + 1)
                if not isinstance(number, int) or number > 0:
                    pe.wait_ge(m_free, number)
                for c in range(4):
                    last = nc.tensor.transpose(ps_m[:, c, :].bitcast(f32r), src[:, 4 * r + c, :], ident_r[:, :])
                last.then_inc(m_full, 1)

            def scores(s, t, kt_at, early, q_number):
                h = t // GT
                keys = [bass.ds(at(pe, kt_at + c * 512), 512) for c in range(SEQ // 512)]
                if t % GT == 0:
                    pe.wait_ge(m_free, q_number + 1)
                if not early:
                    pe.wait_ge(exp_ready, NSTEP * s + t - 1)
                q = qt_hl[:, h % 2, (t % GT) * P:(t % GT + 1) * P]
                for c in range(SEQ // 512):
                    cols = slice(c * 512, (c + 1) * 512)
                    nc.tensor.matmul(ps_s[t % 2][:, cols], q, kt_h[:, keys[c]], start=True, stop=False)
                    last = nc.tensor.matmul(ps_s[t % 2][:, cols], q, kt_l[:, keys[c]], start=False, stop=True)
                last.then_inc(s_done, 1)

            for lo in range(2):
                if lo:
                    pe.wait_ge(k_split, 2)
                else:
                    pe.wait_ge(k_hi, 1)
                for c in range(GT):
                    last = nc.tensor.transpose(ps_s[lo][:, c * P:(c + 1) * P].bitcast(f32r), (kd_h, kd_l)[lo][:, c, :],
                                               ident_r[:, :])
                last.then_inc(kt_full, 1)
            for n, what in enumerate(first_turns):
                through_m(n, what, 0)
            pe.wait_ge(kt_free, 2)
            scores(0, 0, 0, True, q_turn(0, True, False, 0))
            scores(0, 1, 0, True, None)
            pe.wait_ge(b_const, 80)

            def stage_b(s, first, last_s):
                here = at(pe, (s % 2) * SEQ)
                there = at(pe, ((s + 1) % 2) * SEQ)

                def m_turn(what):
                    pe.wait_ge(m_free, turn_no(s, last_s, what))

                def transposes(t):
                    pe.wait_ge(exp_ready, NSTEP * s + t + 1)
                    for r in range(2):
                        if not (first and t == 0):
                            pe.wait_ge(pt_lo, 2 * (NSTEP * s + t) + r - 1)
                        for c in range(4):
                            k = 4 * r + c
                            last = nc.tensor.transpose(ps_t[r][:, c, :], prob[:, t % 2, k * P:(k + 1) * P], ident[:, :])
                        last.then_inc(t_done, 1)

                def values(b):
                    pe.wait_ge(pt_lo, 2 * (NSTEP * s + 2 * b + 2))
                    if b == 0:
                        pe.wait_ge(v_split, s + 1)
                    if not (first and b == 0):
                        pe.wait_ge(o_ready, NQB * s + b)
                    for k in range(GT):
                        for n, pt in enumerate((pt_h, pt_l)):
                            last = nc.tensor.matmul(ps_pv[:, 0:QB], v_hl[:, k, :], pt[:, b % 2, k, :],
                                                    start=k == 0 and n == 0, stop=k == GT - 1 and n == 1)
                    last.then_inc(pv_done, 1)

                def add_halves(b):
                    pe.wait_ge(o_ready, NQB * s + b + 1)
                    m_turn(("add", b))
                    for c in range(2):
                        last = nc.tensor.matmul(ps_m[:, c, 0:HD], o_hl[:, b % 2, c * P:(c + 1) * P], ident2[:, :],
                                                start=True, stop=True)
                    last.then_inc(m_full, 1)

                def back(b):
                    m_turn(("back", b))
                    for c in range(2):
                        i = (2 * b + c) % GT
                        last = nc.tensor.transpose(ps_m[:, c, :], at_tok[:, i, :], ident[:, :])
                    last.then_inc(m_full, 1)

                for t in range(NSTEP + (3 if last_s else 0)):
                    if t < NSTEP:
                        if t + 2 < NSTEP:
                            scores(s, t + 2, here, False, q_turn(s, first, last_s, (t + 2) // GT))
                        elif not last_s:
                            scores(s + 1, t + 2 - NSTEP, there, False, q_turn(s + 1, False, None, 0))
                        for what in before_step(t, last_s):
                            ahead = what[0] == "K" or what[1] == 0
                            through_m(turn_no(s, last_s, what), what, s + 1 if ahead else s)
                        transposes(t)
                    pv, add, bk = after_step(t, first)
                    if pv is not None:
                        values(pv)
                    if add is not None:
                        add_halves(add)
                    if bk is not None:
                        back(bk)

            steps(pe, SLOTS, stage_b)

            for n in range(GROUPS * NW):
                g, w = divmod(n, NW)
                pe.wait_ge(m_ready, n + 1)
                if n >= 2:
                    pe.wait_ge(pl_ready, n - 1)
                for c in range(SEQ // 512):
                    last = nc.tensor.matmul(ps_s[n % 2][:, c * 512:(c + 1) * 512], wp_sb[:, w, :],
                                            mix_pl[:, w, g * SEQ + c * 512:g * SEQ + (c + 1) * 512], start=True, stop=True)
                last.then_inc(pm_done, 1)
            stage_end(pe, 2)

            def out_proj(i, sl, c, start, first_tile):
                if c == 0:
                    pe.wait_ge(mx_lo, i + 1)
                if not start:
                    pe.wait_ge(r_ready, 2 * i - 3 + c)
                for k in range(KM):
                    if first_tile and c == 0:
                        pe.wait_ge(wo_lo, k + 1)
                    cols = slice(c * 512, (c + 1) * 512)
                    for n, (a, w) in enumerate(((mx_h, wo_h), (mx_h, wo_l), (mx_l, wo_h))):
                        last = nc.tensor.matmul(ps_o[sl][:, cols], a[:, sl, k, :], w[:, k, cols],
                                                start=k == 0 and n == 0, stop=k == KM - 1 and n == 2)
                last.then_inc(o_done, 1)

            def h_transposes(i, sl, start):
                pe.wait_ge(h_ready, i + 1)
                if not start:
                    pe.wait_ge(ht_ready, i)
                for k in range(KD):
                    last = nc.tensor.transpose(ps_ht[:, k, :], hid[:, sl, k * P:(k + 1) * P], ident[:, :])
                last.then_inc(ht_done, 1)

            def router(i, start):
                pe.wait_ge(ht_ready, i + 1)
                if not start:
                    pe.wait_ge(l_ready, i)
                for k in range(KD):
                    last = nc.tensor.matmul(ps_l[:, 0:E], ht[:, k, :], wr_sb[:, k, :], start=k == 0, stop=k == KD - 1)
                last.then_inc(l_done, 1)

            def stage_c(b, first):
                for sl in range(2):
                    i = 2 * b + sl
                    out_proj(i, sl, 0, first, first and sl == 0)
                    if not first:
                        router(i - 2, first)
                    out_proj(i, sl, 1, first, first and sl == 0)
                    if not (first and sl == 0):
                        h_transposes(i - 1, 1 - sl, first)

            stage_c(0, True)
            pe.wait_ge(c_const, 48)
            for sl in range(2):
                out_proj(2 + sl, sl, 0, False, False)
                router(sl, sl == 0)
                out_proj(2 + sl, sl, 1, False, False)
                h_transposes(1 + sl, 1 - sl, False)
            with pe.Fori(2, TILES // 2) as b:
                stage_c(b, False)
            router(TILES - 2, False)
            h_transposes(TILES - 1, 1, False)
            router(TILES - 1, False)
            stage_end(pe, 3)

            pe.wait_ge(d_aff, 1)
            for t in range(HT):
                last = nc.tensor.transpose(ps_y[0][0:ROWS, t * P:(t + 1) * P], soft[:, t, :], ident[:, :])
            last.then_inc(d_step, 1)
            pe.wait_ge(top_ready, 1)
            nc.tensor.transpose(ps_x[:, 0, 0:ROWS], top_v[:, :], ident[0:ROWS, 0:ROWS])
            nc.tensor.transpose(ps_x[:, 0, ROWS:2 * ROWS], top_f[:, :], ident[0:ROWS, 0:ROWS]).then_inc(d_step, 1)
            pe.wait_ge(flip_in, 16)
            pe.wait_ge(cols_ready, 1)
            nc.tensor.matmul(ps_x[:, 1, 0:2 * ROWS], flip_sb[:, :], cols_vf[:, :, :].rearrange("p c r -> p (c r)"),
                             start=True, stop=True).then_inc(d_step, 1)
            pe.wait_ge(top_ready, 2)

            XR = GROUPS * KD // 4

            def x_round(e, n, start):
                g, r = divmod(n, KD // 4)
                pe.wait_ge(x_in_g[g], 16 * (e + 1))
                if not start:
                    pe.wait_ge(x_lo, XR * e + n)
                dst = x_bank(n, start)
                for c in range(4):
                    k = 4 * r + c
                    last = nc.tensor.transpose(dst[:, c, :], xg[:, g, k * P:(k + 1) * P], ident[:, :])
                last.then_inc(xt_d, 1)

            for n in range(XR):
                x_round(0, n, True)

            def stage_e(e, first, last_e):
                pe.wait_ge(x_lo, XR * (e + 1))
                for n in range(KF):
                    if n % 2 == 0:
                        pe.wait_ge(w_lo, NCHUNK * e + n + 2)
                    if not (first and n < 3):
                        pe.wait_ge(h_split, KF * e + n - 2)
                    for u in range(2):
                        c = (n // 2) * 2 + u
                        wh = w_h[:, c % RING, :].rearrange("p (k f) -> p k f", k=KD)
                        wl = w_l[:, c % RING, :].rearrange("p (k f) -> p k f", k=KD)
                        cols = slice((n % 2) * P, (n % 2 + 1) * P)
                        for k in range(KD):
                            for q, (w, a) in enumerate(((wh, x_h), (wh, x_l), (wl, x_h))):
                                last = nc.tensor.matmul(ps_gu[n % 3][:, u, :], w[:, k, cols], a[:, k, :],
                                                        start=k == 0 and q == 0, stop=k == KD - 1 and q == 2)
                    last.then_inc(gu_done, 1)
                for m in range(KF // 2):
                    c = NUP + m
                    pe.wait_ge(w_lo, NCHUNK * e + c + 1)
                    pe.wait_ge(h_split, KF * e + 2 * m + 2)
                    if m == 0 and not first:
                        pe.wait_ge(y_ready, GROUPS * e)
                    for kk in range(2):
                        k = 2 * m + kk
                        for g in range(GROUPS):
                            tok = slice(g * CAP, (g + 1) * CAP)
                            for q, (a, w) in enumerate(((hh, w_h), (hh, w_l), (hl, w_h))):
                                for c2 in range(D // 512):
                                    last = nc.tensor.matmul(
                                        ps_y[g][:, c2 * 512:(c2 + 1) * 512], a[:, k, tok],
                                        w[:, c % RING, kk * D + c2 * 512:kk * D + (c2 + 1) * 512],
                                        start=k == 0 and q == 0, stop=k == KF - 1 and q == 2)
                    last.then_inc(dn_done, 1)
                    if 2 <= m < 2 + XR and not last_e:
                        x_round(e + 1, m - 2, False)

            steps(pe, E, stage_e)
            stage_end(pe, 4)

        @block.scalar
        def _(act):
            act.wait_ge(eps_set, 1)

            def ln_in_sd(j):
                for tt in range(2):
                    act.wait_ge(var_ready, 2 * j + tt + 1)
                    nc.scalar.activation(sd[:, tt, :], mv[:, tt, 1:2], ACT.Sqrt, bias=eps[:, 0:1]).then_inc(sd_ready, 1)

            def xt_hi_copy(j, hf, free):
                for tt in range(2):
                    act.wait_ge(xt_done, 2 * j + tt + 1)
                    if not free:
                        act.wait_ge(u_done, 2 * j - 2)
                    nc.scalar.activation(xt_h[:, hf, :, tt * P:(tt + 1) * P], ps_xt[tt][:, :, :], ACT.Copy).then_inc(xt_hi, 1)

            def squares(j, tt, start):
                i = 2 * j + tt
                act.wait_ge(q_done, i + 1)
                if not (start and tt == 0):
                    act.wait_ge(ss_ready, i)
                nc.scalar.activation(sq[:, 0:AW], ps_q[:, :], ACT.Square)
                act.wait_ge(kv_done, i + 1)
                nc.scalar.activation(sq[:, AW:QKW], ps_kv[:, 0:KVW], ACT.Square)
                if not start:
                    act.wait_ge(v_st[tt], 16 * j)
                nc.scalar.activation(qkv[:, tt, :, KVC - HD:KVC],
                                     ps_kv[:, KVW:2 * KVW].rearrange("p (v c) -> p v c", c=HD), ACT.Copy).then_inc(v_ready, 1)
                act.wait_ge(ss_ready, i + 1)
                nc.scalar.activation(rn[:, tt, 0:HEADS + KVH], ss[:, tt, 0:HEADS + KVH], ACT.Sqrt,
                                     bias=eps[:, 1:2], scale=1.0 / HD).then_inc(rms_sd, 1)

            def u_copy(j, hf, cp, free, b):
                act.wait_ge(u_done, 2 * j + cp + 1)
                if not free:
                    act.wait_ge(u_st[hf], 16 * b)
                nc.scalar.activation(ust[:, hf, 2 * cp:2 * cp + 2, :], ps_u[cp][:, :, :], ACT.Copy).then_inc(u_ready, 1)

            def stage_a(b, first, last_b):
                for hf in range(2):
                    j = 2 * b + hf
                    start = first and hf == 0
                    row = at(act, j * (2 * P))
                    if not (last_b and hf == 1):
                        ln_in_sd(j + 1)
                    squares(j, 0, start)
                    u_copy(j, hf, 0, first, b)
                    if not (last_b and hf == 1):
                        xt_hi_copy(j + 1, 1 - hf, start)
                    squares(j, 1, start)
                    u_copy(j, hf, 1, first, b)
                    act.wait_ge(u_ready, 2 * j + 2)
                    act.dma_start(ut_d[:, :, bass.ds(row, 2 * P)].rearrange("w p t -> p w t"),
                                  ust[:, hf, :, :]).then_inc(u_st[hf], 16)

            def win_hi_copy(k):
                act.wait_ge(win_in[k % RAW], 16 * (k // RAW + 1))
                nc.scalar.activation(win_h[:, k, :], win_raw[k % RAW], ACT.Copy).then_inc(win_hi, 1)

            ln_in_sd(0)
            for k in range(W_EARLY):
                win_hi_copy(k)
            xt_hi_copy(0, 0, True)
            for k in range(W_EARLY, KD):
                win_hi_copy(k)
            act.wait_ge(eye_in, 16)
            nc.scalar.activation(ident_r[:, :], ident[:, :], ACT.Copy).then_inc(ident_ready, 1)
            steps(act, PAIRS // 2, stage_a)

            stage_end(act, 1)

            def k_hi_copy():
                act.wait_ge(k_in, 16)
                for d in range(2):
                    last = nc.scalar.activation(kd_h[:, :, d * HD:(d + 1) * HD], k_raw[:, :, :], ACT.Copy)
                last.then_inc(k_hi, 1)

            def v_hi_copy(s, first):
                act.wait_ge(v_in, 16 * s + 16)
                if not first:
                    act.wait_ge(pv_done, NQB * s)
                nc.scalar.activation(v_hl[:, :, 0:HD], v_raw[:, :, :], ACT.Copy).then_inc(v_hi, 1)

            def from_m(number, what, kt_at):
                act.wait_ge(m_full, number + 1)
                src = ps_m[:, :, :].rearrange("p c t -> p (c t)")
                if what[0] == "K":
                    _, lo, r = what
                    nc.scalar.activation((kt_h, kt_l)[lo][:, bass.ds(kt_at + r * 512, 512)], src, ACT.Copy).then_inc(m_free, 1)
                else:
                    _, h, r = what
                    last = nc.scalar.activation(qt_hl[:, h % 2, r * 512:(r + 1) * 512], src, ACT.Copy, scale=HD ** -0.5)
                    last.then_inc(m_free, 1)

            def exp(s, t, early):
                act.wait_ge(max_ready, NSTEP * s + t + 1)
                if not early:
                    act.wait_ge(t_done, 2 * (NSTEP * s + t - 1))
                i = t % (2 * GT)
                nc.scalar.activation(prob[:, t % 2, :], ps_s[t % 2][:, :], ACT.Exp, bias=nmax[:, t % 2:t % 2 + 1],
                                     accum_out=rsum[:, i:i + 1]).then_inc(exp_ready, 1)

            k_hi_copy()
            for lo in range(2):
                act.wait_ge(kt_full, lo + 1)
                nc.scalar.activation((kt_h, kt_l)[lo][:, 0:SEQ], ps_s[lo][:, :], ACT.Copy).then_inc(kt_free, 1)
            for n, what in enumerate(first_turns):
                from_m(n, what, 0)
            v_hi_copy(0, True)
            exp(0, 0, True)
            exp(0, 1, True)

            def stage_b(s, first, last_s):
                def hi(t):
                    b = t // 2
                    for r in range(2):
                        act.wait_ge(t_done, 2 * (NSTEP * s + t) + r + 1)
                        if t % 2 == 0 and r == 0 and not (first and b < 2):
                            act.wait_ge(pv_done, NQB * s + b - 1)
                        nc.scalar.activation(pt_h[:, b % 2, 4 * r:4 * r + 4, (t % 2) * P:(t % 2 + 1) * P],
                                             ps_t[r][:, :, :], ACT.Copy).then_inc(pt_hi, 1)

                there = at(act, ((s + 1) % 2) * SEQ)
                col = at(act, s * SEQ + (s // 2) * (2 * SEQ))
                col_before = 0 if first else at(act, s * SEQ - SEQ + ((s - 1) // 2) * (2 * SEQ))
                mix = mix_at.rearrange("p v j t -> p (v j t)")
                for t in range(NSTEP + (3 if last_s else 0)):
                    if t < NSTEP:
                        for what in before_step(t, last_s):
                            from_m(turn_no(s, last_s, what), what, there)
                        hi(t)
                        if t + 2 < NSTEP:
                            exp(s, t + 2, False)
                        elif not last_s:
                            exp(s + 1, t + 2 - NSTEP, False)
                    pv, add, bk = after_step(t, first)
                    if pv is not None:
                        act.wait_ge(pv_done, NQB * s + pv + 1)
                        nc.scalar.activation(o_hl[:, pv % 2, :], ps_pv[:, 0:QB], ACT.Copy).then_inc(o_ready, 1)
                        if pv == -1:
                            v_hi_copy(s, False)
                    if bk is not None:
                        act.wait_ge(m_full, turn_no(s, last_s, ("back", bk)) + 1)
                        pair, qb = divmod(bk % NQB, GT)
                        off = pair * TOK + (qb % (GT // 2)) * QB
                        nc.scalar.activation(mix[:, bass.ds((col if bk >= 0 else col_before) + off, QB)],
                                             ps_m[:, 0:2, :].rearrange("p c t -> p (c t)"), ACT.Copy).then_inc(m_free, 1)

            steps(act, SLOTS, stage_b)

            def mix_hi(i, sl, start):
                if not start:
                    act.wait_ge(o_done, 2 * i - 2)
                cols = bass.ds(at(act, i * P), P)
                nc.scalar.activation(mx_h[:, sl, 0:NW, :], mix_at.rearrange("p v j t -> p (v j) t")[:, :, cols], ACT.Copy)
                nc.scalar.activation(mx_h[:, sl, NW:KM, :], mix_pl[:, :, cols], ACT.Copy).then_inc(mx_hi, 1)

            def wo_hi_copy(k):
                act.wait_ge(wo_in[k % W_RING], 16 * (k // W_RING + 1))
                nc.scalar.activation(wo_h[:, k, :], wo_raw[:, k % W_RING, :], ACT.Copy).then_inc(wo_hi, 1)

            for n in range(GROUPS * NW):
                g, w = divmod(n, NW)
                act.wait_ge(pm_done, n + 1)
                act.wait_ge(b_const, 80)
                nc.scalar.activation(mix_pl[:, w, g * SEQ:(g + 1) * SEQ], ps_s[n % 2][:, :], ACT.Identity,
                                     scale=psc[:, w:w + 1]).then_inc(pl_ready, 1)
                if n < KM:
                    wo_hi_copy(n)
            for k in range(GROUPS * NW, KM):
                wo_hi_copy(k)
            act.drain()
            mix_hi(0, 0, True)
            stage_end(act, 2)

            def logit_copy(i):
                act.wait_ge(l_done, i + 1)
                nc.scalar.activation(logits[:, bass.ds(i, 1), :], ps_l[:, 0:E].unsqueeze(1), ACT.Copy).then_inc(l_ready, 1)

            def ht_copy(i, start):
                act.wait_ge(ht_done, i + 1)
                if not start:
                    act.wait_ge(l_done, i)
                nc.scalar.activation(ht[:, :, :], ps_ht[:, :, :], ACT.Copy).then_inc(ht_ready, 1)

            def stage_c(b, first, last_b):
                for sl in range(2):
                    i = 2 * b + sl
                    if not (last_b and sl == 1):
                        mix_hi(i + 1, 1 - sl, first and sl == 0)
                    if not first:
                        logit_copy(i - 2)
                    if not (first and sl == 0):
                        ht_copy(i - 1, first)
                    act.wait_ge(c_var, i + 1)
                    nc.scalar.activation(sd[:, sl, :], mv[:, sl, 1:2], ACT.Sqrt, bias=eps[:, 0:1]).then_inc(c_sd, 1)

            steps(act, TILES // 2, stage_c)
            logit_copy(TILES - 2)
            ht_copy(TILES - 1, False)
            logit_copy(TILES - 1)
            stage_end(act, 3)

            def w_hi_copy(e, c, start):
                act.wait_ge(w_dma[c % RING], 16 * ((NCHUNK // RING) * e + c // RING + 1))
                if not start:
                    act.wait_ge(*(used(e, c - RING) if c >= RING else used(e - 1, NCHUNK + c - RING)))
                nc.scalar.activation(w_h[:, c % RING, :], w_raw[:, c % RING, :], ACT.Copy).then_inc(w_hi, 1)

            act.wait_ge(d_exp, 1)
            nc.scalar.activation(logits[:, :, :], logits[:, :, :], ACT.Exp).then_inc(d_exp, 1)
            for c in range(RING):
                w_hi_copy(0, c, True)

            XR = GROUPS * KD // 4

            def x_hi_copy(e, n, start):
                g, r = divmod(n, KD // 4)
                act.wait_ge(xt_d, XR * e + n + 1)
                nc.scalar.activation(x_h[:, 4 * r:4 * r + 4, g * CAP:(g + 1) * CAP], x_bank(n, start), ACT.Copy).then_inc(x_hi, 1)

            for n in range(XR):
                x_hi_copy(0, n, True)

            def stage_e(e, first, last_e):
                for j in range(KF // 2):
                    for n in (2 * j, 2 * j + 1):
                        act.wait_ge(gu_done, KF * e + n + 1)
                        if not (first and n < 2):
                            act.wait_ge(h_split, KF * e + n - 1)
                        nc.scalar.activation(sg[:, n % 2, :], ps_gu[n % 3][:, 0, :], ACT.Silu).then_inc(silu_done, 1)
                    for c in (2 * j + RING, 2 * j + RING + 1):
                        w_hi_copy(e, c, False)
                for m in range(KF // 2):
                    if 2 <= m < 2 + XR and not last_e:
                        x_hi_copy(e + 1, m - 2, False)
                    c = NUP + m + RING
                    if c < NCHUNK:
                        w_hi_copy(e, c, False)
                    elif not last_e:
                        w_hi_copy(e + 1, c - NCHUNK, False)
                act.wait_ge(dn_done, (KF // 2) * (e + 1))
                for g in range(GROUPS):
                    if not first:
                        act.wait_ge(scat[g], 16 * e)
                    nc.scalar.activation(ysb[:, g, :], ps_y[g][:, :], ACT.Identity,
                                         scale=gate_w8[:, bass.ds(e + g * GOFF, 1)]).then_inc(y_ready, 1)

            steps(act, E, stage_e)
            stage_end(act, 4)

            def stage_f(b, first, last_b):
                for k in range(FR):
                    tile = y_raw[:, bass.ds(at(act, FR * b + k), 1), :].rearrange("p o d -> p (o d)")
                    act.wait_ge(f_var, FR * b + k + 1)
                    nc.scalar.activation(fminus[:, k, :], fmv[:, k, 0:1], ACT.Copy, scale=-1.0)
                    if not first:
                        act.wait_ge(f_ready, FR * (b - 1) + k + 1)
                    nc.scalar.activation(fsd[:, k, :], fmv[:, k, 1:2], ACT.Sqrt, bias=eps[:, 0:1]).then_inc(f_sd, 1)
                    act.drain()
                    if not first:
                        act.wait_ge(y_st[k], 16 * b)
                    nc.scalar.activation(y_out[:, k, :], tile, ACT.Identity, bias=fminus[:, k, :]).then_inc(f_centred, 1)

            steps(act, TILES // FR, stage_f)

        @block.vector
        def _(dve):
            nc.vector.memset(alpha[:, :], ALPHA)
            nc.vector.memset(eps[:, 0:1], LN_EPS)
            nc.vector.memset(eps[:, 1:2], RMS_EPS).then_inc(eps_set, 1)

            def split_w(k):
                dve.wait_ge(win_hi, k + 1)
                nc.vector.tensor_tensor(win_l[:, k, :], win_raw[k % RAW], win_h[:, k, :].bitcast(f32),
                                        ALU.subtract).then_inc(win_lo, 1)

            def ln_in_stats(j):
                for tt in range(2):
                    dve.wait_ge(x_in[tt], 16 * j + 16)
                    for c in range(2):
                        nc.vector.bn_stats(bst[:, tt, c, :], xin[:, tt, c * 512:(c + 1) * 512])
                    dve.drain()
                    nc.vector.bn_aggr(mv[:, tt, :], bst[:, tt, :, :]).then_inc(var_ready, 1)

            def ln_in_apply(j, start):
                for tt in range(2):
                    dve.wait_ge(sd_ready, 2 * j + tt + 1)
                    nc.vector.reciprocal(rs[:, tt, :], sd[:, tt, :])
                    if not start:
                        dve.wait_ge(xln_st[tt], 16 * j)
                        dve.wait_ge(xt_done, 2 * j + tt - 1)
                    nc.vector.scalar_tensor_tensor(xln[:, tt, :], xin[:, tt, :], mv[:, tt, 0:1], gain_b[:, 0, :],
                                                   ALU.subtract, ALU.mult)
                    dve.drain()
                    nc.vector.scalar_tensor_tensor(xln[:, tt, :], xln[:, tt, :], rs[:, tt, :], gain_b[:, 1, :],
                                                   ALU.mult, ALU.add).then_inc(xln_ready, 1)

            def xt_lo_sub(j, hf):
                for tt in range(2):
                    dve.wait_ge(xt_hi, 2 * j + tt + 1)
                    nc.vector.tensor_tensor(xt_l[:, hf, :, tt * P:(tt + 1) * P], ps_xt[tt][:, :, :],
                                            xt_h[:, hf, :, tt * P:(tt + 1) * P].bitcast(f32), ALU.subtract).then_inc(xt_lo, 1)

            def rms_norm(j, tt, start):
                i = 2 * j + tt
                H = HEADS + KVH
                dve.wait_ge(v_ready, i + 1)
                nc.vector.reduce_sum(ss[:, tt, 0:H], sq[:, :].rearrange("p (h c) -> p h c", c=HD), axis=AX.X).then_inc(ss_ready, 1)
                dve.wait_ge(rms_sd, i + 1)
                nc.vector.reciprocal(rn[:, tt, 0:H], rn[:, tt, 0:H])
                dve.drain()
                if not start:
                    dve.wait_ge(roped, i - 1)
                nc.vector.tensor_tensor(qn[:, tt, 0:AW].rearrange("p (h c) -> p h c", c=HD),
                                        ps_q[:, :].rearrange("p (h c) -> p h c", c=HD),
                                        rn[:, tt, 0:HEADS].unsqueeze(2).to_broadcast([P, HEADS, HD]), ALU.mult)
                nc.vector.tensor_tensor(qn[:, tt, AW:QKW].rearrange("p (h c) -> p h c", c=HD),
                                        ps_kv[:, 0:KVW].rearrange("p (h c) -> p h c", c=HD),
                                        rn[:, tt, HEADS:H].unsqueeze(2).to_broadcast([P, KVH, HD]),
                                        ALU.mult).then_inc(qn_ready, 1)

            def stage_a(b, first, last_b):
                for hf in range(2):
                    j = 2 * b + hf
                    start = first and hf == 0
                    if not (last_b and hf == 1):
                        ln_in_stats(j + 1)
                        ln_in_apply(j + 1, False)
                    rms_norm(j, 0, start)
                    if not (last_b and hf == 1):
                        xt_lo_sub(j + 1, 1 - hf)
                    rms_norm(j, 1, start)

            ln_in_stats(0)
            dve.wait_ge(gain_in, 32)
            ln_in_apply(0, True)
            for k in range(W_EARLY):
                split_w(k)
            xt_lo_sub(0, 0)
            for k in range(W_EARLY, KD):
                split_w(k)
            steps(dve, PAIRS // 2, stage_a)

            stage_end(dve, 1)

            def k_lo_sub():
                dve.wait_ge(k_hi, 1)
                for d in range(2):
                    nc.vector.tensor_tensor(kd_l[:, :, d * HD:(d + 1) * HD], k_raw[:, :, :],
                                            kd_h[:, :, d * HD:(d + 1) * HD].bitcast(f32), ALU.subtract).then_inc(k_split, 1)

            def v_lo_sub(s):
                dve.wait_ge(v_hi, s + 1)
                nc.vector.tensor_tensor(v_hl[:, :, HD:2 * HD], v_raw[:, :, :], v_hl[:, :, 0:HD].bitcast(f32),
                                        ALU.subtract).then_inc(v_split, 1)

            def row_max(s, t):
                dve.wait_ge(s_done, NSTEP * s + t + 1)
                nc.vector.reduce_max(nmax[:, t % 2:t % 2 + 1], ps_s[t % 2][:, :], axis=AX.X,
                                     negate=True).then_inc(max_ready, 1)

            k_lo_sub()
            row_max(0, 0)
            row_max(0, 1)
            v_lo_sub(0)

            def stage_b(s, first, last_s):
                def lo(t):
                    b = t // 2
                    for r in range(2):
                        dve.wait_ge(pt_hi, 2 * (NSTEP * s + t) + r + 1)
                        cols = slice((t % 2) * P, (t % 2 + 1) * P)
                        nc.vector.tensor_tensor(pt_l[:, b % 2, 4 * r:4 * r + 4, cols], ps_t[r][:, :, :],
                                                pt_h[:, b % 2, 4 * r:4 * r + 4, cols].bitcast(f32), ALU.subtract).then_inc(pt_lo, 1)

                for t in range(NSTEP + (3 if last_s else 0)):
                    if t < NSTEP:
                        if t + 2 < NSTEP:
                            row_max(s, t + 2)
                        elif not last_s:
                            row_max(s + 1, t + 2 - NSTEP)
                        lo(t)
                        if t == 1 and not first:
                            v_lo_sub(s)
                    _, add, _ = after_step(t, first)
                    if add is not None:
                        h, i = (add % NQB) // (GT // 2), (2 * add) % GT
                        j = (2 * add) % (2 * GT)
                        nc.vector.reciprocal(rinv[:, j:j + 2], rsum[:, j:j + 2])
                        dve.drain()
                        dve.wait_ge(m_full, turn_no(s, last_s, ("add", add)) + 1)
                        nc.vector.tensor_tensor(at_tok[:, i:i + 2, (h % 2) * HD:(h % 2 + 1) * HD], ps_m[:, 0:2, 0:HD],
                                                rinv[:, j:j + 2].unsqueeze(2).to_broadcast([P, 2, HD]),
                                                ALU.mult).then_inc(m_free, 1)

            steps(dve, SLOTS, stage_b)
            def mix_lo(i, sl):
                cols = bass.ds(at(dve, i * P), P)
                dve.wait_ge(mx_hi, i + 1)
                nc.vector.tensor_tensor(mx_l[:, sl, 0:NW, :], mix_at.rearrange("p v j t -> p (v j) t")[:, :, cols],
                                        mx_h[:, sl, 0:NW, :].bitcast(f32), ALU.subtract)
                nc.vector.tensor_tensor(mx_l[:, sl, NW:KM, :], mix_pl[:, :, cols],
                                        mx_h[:, sl, NW:KM, :].bitcast(f32), ALU.subtract).then_inc(mx_lo, 1)

            for k in range(KM):
                dve.wait_ge(wo_hi, k + 1)
                nc.vector.tensor_tensor(wo_l[:, k, :], wo_raw[:, k % W_RING, :], wo_h[:, k, :].bitcast(f32),
                                        ALU.subtract).then_inc(wo_lo, 1)
            mix_lo(0, 0)
            stage_end(dve, 2)

            dve.wait_ge(c_const, 48)

            def stage_c(b, first, last_b):
                for sl in range(2):
                    i = 2 * b + sl
                    if not (last_b and sl == 1):
                        mix_lo(i + 1, 1 - sl)
                    dve.wait_ge(res_in[sl], 16 * b + 16)
                    if not first:
                        dve.wait_ge(h_st[sl], 16 * b)
                        dve.wait_ge(ht_done, i - 1)
                        dve.wait_ge(acc_ready, i - 1)
                    for c in range(2):
                        cols = slice(c * 512, (c + 1) * 512)
                        dve.wait_ge(o_done, 2 * i + c + 1)
                        nc.vector.scalar_tensor_tensor(hid[:, sl, cols], res[:, sl, cols], ALPHA, ps_o[sl][:, cols],
                                                       ALU.mult, ALU.add).then_inc(r_ready, 1)
                        dve.wait_ge(r_ready, 2 * i + c + 1)
                        nc.vector.bn_stats(bst[:, sl, c, :], hid[:, sl, cols])
                    dve.drain()
                    nc.vector.bn_aggr(mv[:, sl, :], bst[:, sl, :, :]).then_inc(c_var, 1)
                    dve.wait_ge(c_sd, i + 1)
                    nc.vector.reciprocal(rs[:, sl, :], sd[:, sl, :])
                    nc.vector.scalar_tensor_tensor(hid[:, sl, :], hid[:, sl, :], mv[:, sl, 0:1], gain_b[:, 0, :],
                                                   ALU.subtract, ALU.mult)
                    dve.drain()
                    nc.vector.scalar_tensor_tensor(hid[:, sl, :], hid[:, sl, :], rs[:, sl, :], gain_b[:, 1, :],
                                                   ALU.mult, ALU.add).then_inc(h_ready, 1)

            steps(dve, TILES // 2, stage_c)
            stage_end(dve, 3)

            nc.vector.reduce_max(lmax[:, :], logits[:, :, :], axis=AX.X)
            dve.drain()
            nc.vector.tensor_tensor(logits[:, :, :], logits[:, :, :], lmax[:, :].unsqueeze(2).to_broadcast([P, TILES, E]),
                                    ALU.subtract).then_inc(d_exp, 1)
            dve.wait_ge(d_exp, 2)
            nc.vector.reduce_sum(lsum[:, :], logits[:, :, :], axis=AX.X)
            dve.drain()
            nc.vector.reciprocal(lsum[:, :], lsum[:, :])
            dve.drain()
            by_half = lambda a: a.rearrange("p (q t) e -> p q t e", t=HT)
            nc.vector.tensor_tensor(soft.rearrange("p t (q e) -> p q t e", e=E), by_half(logits[:, :, :]),
                                    by_half(lsum[:, :].unsqueeze(2).to_broadcast([P, TILES, E])),
                                    ALU.mult).then_inc(d_aff, 1)
            dve.wait_ge(d_step, 1)
            nc.vector.tensor_copy(aff[:, :], ps_y[0][0:ROWS, 0:HALF])

            def w_lo_sub(e, c):
                dve.wait_ge(w_hi, NCHUNK * e + c + 1)
                nc.vector.tensor_tensor(w_l[:, c % RING, :], w_raw[:, c % RING, :], w_h[:, c % RING, :].bitcast(f32),
                                        ALU.subtract).then_inc(w_lo, 1)

            for r in range(CAP // 8):
                cols = slice(8 * r, 8 * r + 8)
                dve.drain()
                nc.vector.max(top_v[:, cols], aff[:, :])
                dve.drain()
                nc.vector.max_index(top_i[:, cols], top_v[:, cols], aff[:, :])
                if r < CAP // 8 - 1:
                    nc.vector.match_replace(aff[:, :], top_v[:, cols], aff[:, :], -1.0)
            dve.drain()
            nc.vector.tensor_copy(top_f[:, :], top_i[:, :]).then_inc(top_ready, 1)
            dve.wait_ge(d_step, 2)
            nc.vector.tensor_copy(cols_vf[:, :, :], ps_x[:, 0, 0:2 * ROWS].rearrange("p (c r) -> p c r", c=2)).then_inc(cols_ready, 1)
            dve.wait_ge(d_step, 3)
            a_val, a_at = (cols_vf[:, c, :].rearrange("p (g h e) -> p g h e", g=GROUPS, h=2)[:, :, 0, :] for c in range(2))
            b_val, b_at = (ps_x[:, 1, c * ROWS:(c + 1) * ROWS].rearrange("p (g h e) -> p g h e", g=GROUPS, h=2)[:, :, 1, :]
                           for c in range(2))
            nc.vector.tensor_tensor(first_wins[:, :, :], a_val, b_val, ALU.is_ge)
            nc.vector.tensor_tensor(gate_w8.rearrange("p (g e) -> p g e", g=GROUPS), a_val, b_val, ALU.max)
            nc.vector.scalar_tensor_tensor(idx_diff[:, :, :], a_at, float(HALF), b_at, ALU.subtract, ALU.subtract)
            dve.drain()
            nc.vector.tensor_tensor(idx_diff[:, :, :], idx_diff[:, :, :], first_wins[:, :, :], ALU.mult)
            dve.drain()
            for g in range(GROUPS):
                last = nc.vector.scalar_tensor_tensor(idx_t[:, g * E:(g + 1) * E], b_at[:, g, :], float(g * SEQ + HALF),
                                                      idx_diff[:, g, :], ALU.add, ALU.add)
            last.then_inc(top_ready, 1)

            XR = GROUPS * KD // 4

            def x_lo_sub(e, n, start):
                g, r = divmod(n, KD // 4)
                dve.wait_ge(x_hi, XR * e + n + 1)
                dst = (slice(None), slice(4 * r, 4 * r + 4), slice(g * CAP, (g + 1) * CAP))
                nc.vector.tensor_tensor(x_l[dst], x_bank(n, start), x_h[dst].bitcast(f32), ALU.subtract).then_inc(x_lo, 1)

            for n in range(XR):
                x_lo_sub(0, n, True)

            def stage_e(e, first, last_e):
                for j in range(KF // 2):
                    for n in (2 * j, 2 * j + 1):
                        dve.wait_ge(silu_done, KF * e + n + 1)
                        if n == 0 and not first:
                            dve.wait_ge(dn_done, (KF // 2) * e)
                        nc.vector.tensor_tensor(hf[:, n % 2, :], sg[:, n % 2, :], ps_gu[n % 3][:, 1, :], ALU.mult)
                        dve.drain()
                        nc.vector.tensor_copy(hh[:, n, :], hf[:, n % 2, :])
                        dve.drain()
                        nc.vector.tensor_tensor(hl[:, n, :], hf[:, n % 2, :], hh[:, n, :].bitcast(f32),
                                                ALU.subtract).then_inc(h_split, 1)
                    for c in (2 * j + RING, 2 * j + RING + 1):
                        w_lo_sub(e, c)
                for m in range(KF // 2):
                    if 2 <= m < 2 + XR and not last_e:
                        x_lo_sub(e + 1, m - 2, False)
                    c = NUP + m + RING
                    if c < NCHUNK:
                        w_lo_sub(e, c)
                    elif not last_e:
                        w_lo_sub(e + 1, c - NCHUNK)

            steps(dve, E, stage_e)
            stage_end(dve, 4)

            dve.wait_ge(f_const, 32)

            def stage_f(b, first, last_b):
                def stats(k):
                    tile = y_raw[:, bass.ds(at(dve, FR * b + k), 1), :].rearrange("p o d -> p (o d)")
                    if not first:
                        dve.wait_ge(f_centred, FR * (b - 1) + k + 1)
                    dve.wait_ge(y_in[k], 16 * b + 16)
                    for c in range(2):
                        nc.vector.bn_stats(fst[:, k, c, :], tile[:, c * 512:(c + 1) * 512])
                    dve.drain()
                    nc.vector.bn_aggr(fmv[:, k, :], fst[:, k, :, :]).then_inc(f_var, 1)

                def inverse(k):
                    dve.wait_ge(f_sd, FR * b + k + 1)
                    nc.vector.reciprocal(frs[:, k % FR, :], fsd[:, k % FR, :])

                def finish(k):
                    dve.wait_ge(f_gained, FR * b + k + 1)
                    nc.vector.scalar_tensor_tensor(y_out[:, k % FR, :], y_out[:, k % FR, :], frs[:, k % FR, :],
                                                   gain_b[:, 1, :], ALU.mult, ALU.add).then_inc(f_ready, 1)

                for k in range(FR + (2 if last_b else 0)):
                    if k < FR:
                        stats(k)
                    if not (first and k == 0) and k <= FR:
                        inverse(k - 1)
                        if k == FR:
                            dve.drain()
                    if not (first and k < 2):
                        finish(k - 2)

            steps(dve, TILES // FR, stage_f)

        @block.gpsimd
        def _(pool):
            pool.wait_ge(rope_in, 48)

            def stage_a(b, first, last_b):
                for hf in range(2):
                    j = 2 * b + hf
                    start = first and hf == 0
                    for tt in range(2):
                        i = 2 * j + tt
                        H = HEADS + KVH
                        qn3 = qn[:, tt, :].rearrange("p (h c) -> p h c", c=HD)
                        q4 = qn[:, tt, :].rearrange("p (h a s c) -> p h a s c", a=2, s=2, c=16)
                        r4 = rot[:, :].rearrange("p (h a s c) -> p h a s c", a=2, s=2, c=16)
                        pool.wait_ge(qn_ready, i + 1)
                        nc.gpsimd.tensor_tensor(qn[:, tt, :], qn[:, tt, :], qkg[:, :], ALU.mult)
                        pool.drain()
                        for s in range(2):
                            sn = sin_t[:, bass.ds(i, 1), :].rearrange("p t (a s c) -> p t a s c", s=2, c=16)[:, :, :, s, :]
                            nc.gpsimd.tensor_tensor(r4[:, :, :, s, :], q4[:, :, :, 1 - s, :],
                                                    sn.to_broadcast([P, H, 2, 16]), ALU.mult)
                        pool.drain()
                        cs = cos_t[:, bass.ds(i, 1), :]
                        nc.gpsimd.tensor_tensor(qn3, qn3, cs.to_broadcast([P, H, HD]), ALU.mult)
                        pool.drain()
                        if not start:
                            pool.wait_ge(q_st[tt], 16 * j)
                            pool.wait_ge(k_st[tt], 16 * j)
                        for dst, c0, c1 in ((qkv[:, tt, :, 0:AW // KVH], 0, AW),
                                            (qkv[:, tt, :, AW // KVH:AW // KVH + HD], AW, QKW)):
                            last = nc.gpsimd.tensor_tensor(dst, qn[:, tt, c0:c1].rearrange("p (v c) -> p v c", v=KVH),
                                                           rot[:, c0:c1].rearrange("p (v c) -> p v c", v=KVH), ALU.add)
                        last.then_inc(roped, 1)

            steps(pool, PAIRS // 2, stage_a)

            stage_end(pool, 1)

            def split_q(n):
                s, h = divmod(n, QH)
                pool.wait_ge(q_in, 16 * s + 16)
                if n >= 2:
                    s2, h2 = divmod(n - 2, QH)
                    pool.wait_ge(m_full, q_turn(s2, s2 == 0, s2 == SLOTS - 1, h2) + 1)
                q = q_raw[:, :, h * HD:(h + 1) * HD]
                nc.gpsimd.tensor_copy(q_hl[:, n % 2, :, 0:HD], q)
                pool.drain()
                nc.gpsimd.tensor_tensor(q_hl[:, n % 2, :, HD:P], q, q_hl[:, n % 2, :, 0:HD].bitcast(f32),
                                        ALU.subtract).then_inc(q_split, 1)

            def split_k(s):
                pool.wait_ge(k_in, 16 * s + 16)
                if s == 1:
                    pool.wait_ge(kt_full, 2)
                else:
                    pool.wait_ge(m_full, turn_no(s - 2, False, ("K", 1, 1)) + 1)
                for d in range(2):
                    nc.gpsimd.tensor_copy(kd_h[:, :, d * HD:(d + 1) * HD], k_raw[:, :, :])
                pool.drain()
                for d in range(2):
                    nc.gpsimd.tensor_tensor(kd_l[:, :, d * HD:(d + 1) * HD], k_raw[:, :, :],
                                            kd_h[:, :, d * HD:(d + 1) * HD].bitcast(f32), ALU.subtract).then_inc(k_split, 1)

            def pool_window(n):
                g, w = divmod(n, NW)
                if n:
                    pool.wait_ge(m_ready, n)
                pool.dma_start(upad[:, PAD:PAD + SEQ], ut_d[w, :, g * SEQ:(g + 1) * SEQ]).then_inc(u_in, 16)
                pool.wait_ge(u_in, 16 * n + 16)
                src, n_in, width = upad, SEQ + 2 * PAD, 1
                for k in range(w + 1):
                    dst = (win_a, win_b)[k % 2]
                    n_in -= width
                    nc.gpsimd.tensor_tensor(dst[:, 0:n_in], src[:, 0:n_in], src[:, width:width + n_in], ALU.add)
                    pool.drain()
                    src, width = dst, 2 * width
                a = PAD - width // 2
                win = src[:, a:a + SEQ]
                for side, c in enumerate((slice(0, PAD), slice(SEQ - PAD, SEQ))):
                    nc.gpsimd.tensor_tensor(win[:, c], win[:, c], edge_t[:, w, side, :], ALU.mult)
                pool.drain()
                nc.gpsimd.tensor_scalar(win, win, 1.0 / width, None, ALU.mult)
                pool.drain()
                nc.gpsimd.tensor_tensor(mix_pl[:, w, g * SEQ:(g + 1) * SEQ], win, upad[:, PAD:PAD + SEQ],
                                        ALU.subtract).then_inc(m_ready, 1)

            split_q(0)
            split_q(1)
            pool.wait_ge(b_const, 80)
            nc.gpsimd.memset(upad[:, 0:PAD], 0.0)
            nc.gpsimd.memset(upad[:, PAD + SEQ:], 0.0)
            for n in range(2, SLOTS * QH):
                if n % QH == 2 and n // QH + 1 < SLOTS:
                    split_k(n // QH + 1)
                split_q(n)
                if n % 2 == 1 and n // 2 <= GROUPS * NW:
                    pool_window(n // 2 - 1)
            pool_window(GROUPS * NW - 1)
            stage_end(pool, 2)

            def stage_c(b, first, last_b):
                for sl in range(2):
                    i = 2 * b + sl
                    pool.wait_ge(h_ready, i + 1)
                    if not first:
                        pool.wait_ge(acc_st[sl], 16 * b)
                    nc.gpsimd.tensor_tensor(acc[:, sl, :], hid[:, sl, :], alpha[:, 0:1].to_broadcast([P, D]),
                                            ALU.mult).then_inc(acc_ready, 1)

            steps(pool, TILES // 2, stage_c)
            stage_end(pool, 3)

            XR = GROUPS * KD // 4
            nc.gpsimd.memset(no_shift[:, :], 0)
            for c in range(RING):
                pool.wait_ge(w_hi, c + 1)
                nc.gpsimd.tensor_tensor(w_l[:, c, :], w_raw[:, c, :], w_h[:, c, :].bitcast(f32), ALU.subtract).then_inc(w_lo, 1)
            pool.wait_ge(top_ready, 2)

            def gather(e, start):
                if not start:
                    pool.wait_ge(xt_d, XR * e)
                for g in range(GROUPS):
                    nc.gpsimd.tensor_copy(idx_g[:, g:g + 1], idx_t[:, bass.ds(e + g * GOFF, 1)])
                pool.drain()
                for g in range(GROUPS):
                    pool.indirect_dma_start(out=xg[:, g, :], out_offset=None, in_=h_d[:, :],
                                            in_offset=bass.IndirectOffsetOnAxis(ap=idx_g[:, g:g + 1], axis=0)
                                            ).then_inc(x_in_g[g], 16)

            def scatter(e):
                for g in range(GROUPS):
                    nc.gpsimd.tensor_copy(idx_e[:, g:g + 1], idx_t[:, bass.ds(e + g * GOFF, 1)])
                pool.drain()
                pool.wait_ge(y_ready, GROUPS * (e + 1))
                nc.gpsimd.tensor_tensor(idx_s[:, :], idx_e[:, :], no_shift[:, :], ALU.add)
                pool.drain()
                for g in range(GROUPS):
                    pool.indirect_dma_start(out=acc_d[:, :], in_=ysb[:, g, :], in_offset=None,
                                            out_offset=bass.IndirectOffsetOnAxis(ap=idx_s[:, g:g + 1], axis=0),
                                            compute_op=ALU.add).then_inc(scat[g], 16)
                for g in range(GROUPS):
                    pool.wait_ge(scat[g], 16 * (e + 1))

            gather(0, True)

            def stage_e(e, first, last_e):
                if not last_e:
                    gather(e + 1, False)
                scatter(e)

            steps(pool, E, stage_e)
            stage_end(pool, 4)

            pool.wait_ge(f_const, 32)

            def stage_f(b, first, last_b):
                for k in range(FR):
                    pool.wait_ge(f_centred, FR * b + k + 1)
                    nc.gpsimd.tensor_tensor(y_out[:, k, :], y_out[:, k, :], gain_b[:, 0, :], ALU.mult).then_inc(f_gained, 1)

            steps(pool, TILES // FR, stage_f)


_INS = ["x", "ln_in_g", "ln_in_b", "w_in", "qk_gain", "w_pool", "pool_scale", "w_out", "ln1_g", "ln1_b", "w_router",
        "w_gate", "w_up", "w_down", "ln2_g", "ln2_b", "rope_cos", "rope_sin", "pool_edge", "eye", "flip"]


def lay_out(x_prompt, x_sample, ln_in_g, ln_in_b, w_in, q_norm_g, k_norm_g, w_pool, pool_scale, w_out,
            ln1_g, ln1_b, w_router, w_gate, w_up, w_down, ln2_g, ln2_b):
    seq = x_prompt.shape[1]
    d = x_prompt.shape[2]
    rows = lambda v: np.ascontiguousarray(np.broadcast_to(v, (128, v.shape[-1])))
    grid_w, pairs, theta = 64, 16, 10000.0
    inv = theta ** (-np.arange(pairs, dtype=np.float32) / np.float32(pairs))
    row = np.repeat(np.arange(seq // grid_w), grid_w).astype(np.float32)[:, None] * inv.astype(np.float32)
    col = np.tile(np.arange(grid_w), seq // grid_w).astype(np.float32)[:, None] * inv.astype(np.float32)
    cos = np.concatenate([np.cos(row), np.cos(row), np.cos(col), np.cos(col)], axis=1)
    sin = np.concatenate([-np.sin(row), np.sin(row), -np.sin(col), np.sin(col)], axis=1)
    edge = np.ones((4, 2, 8), np.float32)
    for g, w in enumerate((2, 4, 8, 16)):
        for n in range(8):
            for side, t in ((0, n), (1, seq - 8 + n)):
                lo, hi = max(t - w // 2, 0), min(t - w // 2 + w, seq)
                edge[g, side, n] = w / (hi - lo)
    gains = np.concatenate([np.tile(q_norm_g[0], 8), np.tile(k_norm_g[0], 2)])
    return {
        "x": np.concatenate([x_prompt[0], x_sample[0]], axis=0),
        "ln_in_g": rows(ln_in_g), "ln_in_b": rows(ln_in_b), "w_in": w_in[0], "qk_gain": rows(gains),
        "w_pool": w_pool[0], "pool_scale": np.ascontiguousarray(pool_scale[0].reshape(4, 128).T), "w_out": w_out[0],
        "ln1_g": rows(ln1_g[0]), "ln1_b": rows(ln1_b[0]), "w_router": w_router[0],
        "w_gate": w_gate[0], "w_up": w_up[0], "w_down": w_down[0],
        "ln2_g": rows(ln2_g[0]), "ln2_b": rows(ln2_b[0]),
        "rope_cos": np.tile(cos, (2, 1)), "rope_sin": np.tile(sin, (2, 1)),
        "pool_edge": np.ascontiguousarray(np.broadcast_to(edge.reshape(-1), (128, 64))),
        "eye": np.eye(128, dtype=np.float32),
        "flip": np.ascontiguousarray(np.eye(128, dtype=np.float32)[::-1]),
    }


def kernel(**inputs):
    import concourse.bacc as bacc
    from concourse.bass_utils import run_bass_kernel_spmd

    nc = bacc.Bacc("TRN2", target_bir_lowering=False, num_devices=1)
    arrays = {f"in_{n}": np.ascontiguousarray(a) for n, a in
              lay_out(**{k: np.asarray(v) for k, v in inputs.items()}).items()}
    args = [nc.dram_tensor(f"in_{n}", arrays[f"in_{n}"].shape, mybir.dt.float32, kind="ExternalInput").ap() for n in _INS]
    shape = arrays["in_x"].shape
    y = nc.dram_tensor("out_y", shape, mybir.dt.float32, kind="ExternalOutput").ap()
    encoder_layer(nc, *args, y)
    got = run_bass_kernel_spmd(nc, [arrays], core_ids=[0]).results[0]["out_y"]
    half = shape[0] // 2
    return got[:half].reshape(1, half, shape[1]), got[half:].reshape(1, half, shape[1])
```
